# Optimizing a Trainium2 kernel written in Bass

```python
import math
import jax, jax.numpy as jnp
from jax import lax
import numpy as np

D_MODEL = 1024
BATCH = 1
SEQ = 256
DEPTH = 2

D_MIX = D_MODEL
HEAD_DIM = 64
RET_HEADS = 4
RET_WIDTH = RET_HEADS * HEAD_DIM
RET_CHUNK = 128
ROPE_BASE = 10000.0
NSA_HEADS = 8
NSA_KV_HEADS = 2
NSA_GROUP = NSA_HEADS // NSA_KV_HEADS
NSA_WIDTH = NSA_HEADS * HEAD_DIM
NSA_KV_WIDTH = NSA_KV_HEADS * HEAD_DIM
CMP_LEN = 32
CMP_STRIDE = 16
SEL_LEN = 64
N_SELECT = 16
WINDOW = 512
NSA_QBLOCK = 64
N_BRANCH = 3
FORCE_SCORE = 1.0e4
LRU_WIDTH = D_MIX - RET_WIDTH - NSA_WIDTH
LRU_BLOCKS = 4
LRU_BLOCK_DIM = LRU_WIDTH // LRU_BLOCKS
CONV_WIDTH = 4
LRU_C = 8.0
DEEPNORM_ALPHA = (2.0 * DEPTH) ** 0.25
DEEPNORM_BETA = (8.0 * DEPTH) ** -0.25
LN_EPS = 1e-5

IN_SIZES = (RET_WIDTH,) * 4 + (NSA_WIDTH,) + (NSA_KV_WIDTH,) * 6 + (NSA_WIDTH, NSA_HEADS * N_BRANCH, LRU_WIDTH, LRU_WIDTH)
D_IN = sum(IN_SIZES)
IN_SPLIT_POINTS = tuple(int(v) for v in np.cumsum(IN_SIZES)[:-1])


def _normalize(x):
    xf = x.astype(jnp.float32)
    mu = jnp.mean(xf, axis=-1, keepdims=True)
    var = jnp.mean(jnp.square(xf - mu), axis=-1, keepdims=True)
    return (xf - mu) * lax.rsqrt(var + LN_EPS)

def layer_norm(x, g, b):
    return (_normalize(x) * g.astype(jnp.float32) + b.astype(jnp.float32)).astype(x.dtype)

def rotary(x, pos):
    half = x.shape[-1] // 2
    inv = 1.0 / (ROPE_BASE ** (jnp.arange(half, dtype=jnp.float32) / half))
    ang = pos.astype(jnp.float32)[:, None] * inv[None, :]
    cos, sin = jnp.cos(ang), jnp.sin(ang)
    x1, x2 = x[..., :half], x[..., half:]
    return jnp.concatenate([x1 * cos - x2 * sin, x1 * sin + x2 * cos], axis=-1).astype(x.dtype)

def masked_softmax(s, mask):
    logits = jnp.where(mask, s.astype(jnp.float32), -1e30)
    return jax.nn.softmax(logits, axis=-1)

def retention(q, k, v):
    B, S, _ = q.shape
    dt = q.dtype
    H, d, C = RET_HEADS, HEAD_DIM, RET_CHUNK
    nc = S // C

    def heads(t):
        return t.reshape(B, S, H, d).transpose(0, 2, 1, 3)

    pos = jnp.arange(S)
    qh = rotary(heads(q), pos)
    kh = rotary(heads(k), pos) * (d ** -0.5)
    vh = heads(v)
    log_g = jnp.log(1.0 - 2.0 ** (-5.0 - jnp.arange(H, dtype=jnp.float32)))
    idx = jnp.arange(C, dtype=jnp.float32)
    diff = idx[:, None] - idx[None, :]
    inner_decay = jnp.where(diff >= 0, jnp.exp(jnp.maximum(diff, 0.0)[None] * log_g[:, None, None]), 0.0).astype(dt)
    key_decay = jnp.exp((C - 1.0 - idx)[None, :] * log_g[:, None]).astype(dt)
    query_decay = jnp.exp((idx + 1.0)[None, :] * log_g[:, None]).astype(dt)
    chunk_decay = jnp.exp(C * log_g).astype(dt)

    qc = qh.reshape(B, H, nc, C, d)
    kc = kh.reshape(B, H, nc, C, d)
    vc = vh.reshape(B, H, nc, C, d)
    scores = jnp.einsum('bhnid,bhnjd->bhnij', qc, kc) * inner_decay[None, :, None]
    inner = jnp.einsum('bhnij,bhnjd->bhnid', scores, vc)
    kv = jnp.einsum('bhnjd,bhnje->nbhde', kc * key_decay[None, :, None, :, None], vc)

    def step(state, kv_c):
        return state * chunk_decay[None, :, None, None] + kv_c, state

    _, states = lax.scan(step, jnp.zeros((B, H, d, d), dt), kv)
    cross = jnp.einsum('bhnid,nbhde->bhnie', qc, states) * query_decay[None, :, None, :, None]
    y = (inner + cross).reshape(B, H, S, d)
    y = _normalize(y).astype(dt)
    return y.transpose(0, 2, 1, 3).reshape(B, S, RET_WIDTH)

def nsa(xq, k_c, v_c, k_s, v_s, k_w, v_w, gate_logits, cmp_pos, cmp_w):
    B, S, _ = xq.shape
    dt = xq.dtype
    G, R, dh, QB = NSA_KV_HEADS, NSA_GROUP, HEAD_DIM, NSA_QBLOCK
    q = xq.reshape(B, S, G, R, dh).transpose(0, 2, 3, 1, 4) * (dh ** -0.5)

    def kvh(t):
        return t.reshape(B, S, G, dh).transpose(0, 2, 1, 3)

    n_cmp = (S - CMP_LEN) // CMP_STRIDE + 1
    tok = np.arange(n_cmp)[:, None] * CMP_STRIDE + np.arange(CMP_LEN)[None, :]

    def compress(t, pos, w):
        blocks = t[:, :, tok] + pos
        return blocks.reshape(B, G, n_cmp, CMP_LEN * dh) @ w

    kc = compress(kvh(k_c), cmp_pos[0], cmp_w[0])
    vc = compress(kvh(v_c), cmp_pos[1], cmp_w[1])
    cmp_end = np.arange(n_cmp) * CMP_STRIDE + CMP_LEN - 1

    n_sel = S // SEL_LEN
    ci = np.arange(n_cmp)[:, None]
    sj = np.arange(n_sel)[None, :]
    overlap = np.minimum(ci * CMP_STRIDE + CMP_LEN, sj * SEL_LEN + SEL_LEN) - np.maximum(ci * CMP_STRIDE, sj * SEL_LEN)
    sel_map = jnp.asarray(np.clip(overlap, 0, None) / CMP_STRIDE, dtype=jnp.float32)
    top = min(N_SELECT, n_sel)
    ks_blocks = kvh(k_s).reshape(B, G, n_sel, SEL_LEN, dh)
    vs_blocks = kvh(v_s).reshape(B, G, n_sel, SEL_LEN, dh)
    gather = jax.vmap(jax.vmap(lambda blk, ix: blk[ix]))

    pad = ((0, 0), (0, 0), (WINDOW, 0), (0, 0))
    kw = jnp.pad(kvh(k_w), pad)
    vw = jnp.pad(kvh(v_w), pad)

    gates = jax.nn.sigmoid(gate_logits.astype(jnp.float32)).astype(dt)
    gates = gates.reshape(B, S, G, R, N_BRANCH).transpose(0, 2, 3, 1, 4)

    def block(i):
        start = i * QB
        t = start + jnp.arange(QB)
        qb = lax.dynamic_slice_in_dim(q, start, QB, axis=3)
        gb = lax.dynamic_slice_in_dim(gates, start, QB, axis=3)
        m_c = cmp_end[None, :] <= t[:, None]
        p_c = masked_softmax(jnp.einsum('bgrqd,bgnd->bgrqn', qb, kc), m_c)
        p_c = p_c * jnp.any(m_c, axis=-1)[:, None]
        o_c = jnp.einsum('bgrqn,bgnd->bgrqd', p_c.astype(dt), vc)
        imp = jnp.einsum('bgrqn,nj->bgqj', p_c, sel_map)
        j = jnp.arange(n_sel)[None, :]
        cur = (t // SEL_LEN)[:, None]
        forced = (j == 0) | (j == cur) | (j == cur - 1)
        causal = j * SEL_LEN <= t[:, None]
        imp = jnp.where(forced, FORCE_SCORE, jnp.where(causal, imp, -FORCE_SCORE))
        _, idx = lax.top_k(imp, top)
        k_sel = gather(ks_blocks, idx).reshape(B, G, QB, top * SEL_LEN, dh)
        v_sel = gather(vs_blocks, idx).reshape(B, G, QB, top * SEL_LEN, dh)
        kpos = (idx[..., None] * SEL_LEN + jnp.arange(SEL_LEN)).reshape(B, G, QB, top * SEL_LEN)
        m_s = (kpos <= t[:, None])[:, :, None]
        p_s = masked_softmax(jnp.einsum('bgrqd,bgqkd->bgrqk', qb, k_sel), m_s)
        o_s = jnp.einsum('bgrqk,bgqkd->bgrqd', p_s.astype(dt), v_sel)
        kwb = lax.dynamic_slice_in_dim(kw, start, WINDOW + QB, axis=2)
        vwb = lax.dynamic_slice_in_dim(vw, start, WINDOW + QB, axis=2)
        jpos = start - WINDOW + jnp.arange(WINDOW + QB)
        m_w = (jpos[None, :] >= 0) & (jpos[None, :] <= t[:, None]) & (jpos[None, :] > t[:, None] - WINDOW)
        p_w = masked_softmax(jnp.einsum('bgrqd,bgkd->bgrqk', qb, kwb), m_w)
        o_w = jnp.einsum('bgrqk,bgkd->bgrqd', p_w.astype(dt), vwb)
        return gb[..., 0:1] * o_c + gb[..., 1:2] * o_s + gb[..., 2:3] * o_w

    out = lax.map(block, jnp.arange(S // QB))
    return out.transpose(1, 0, 4, 2, 3, 5).reshape(B, S, NSA_WIDTH)

def rg_lru(x, conv_w, conv_b, w_a, b_a, w_x, b_x, lam):
    B, S, C = x.shape
    xc = lax.conv_general_dilated(x, conv_w[:, None, :], window_strides=(1,),
                                  padding=((CONV_WIDTH - 1, 0),),
                                  dimension_numbers=('NWC', 'WIO', 'NWC'),
                                  feature_group_count=C) + conv_b
    xb = xc.reshape(B, S, LRU_BLOCKS, LRU_BLOCK_DIM)
    r = jax.nn.sigmoid((jnp.einsum('bsnd,nde->bsne', xb, w_a).reshape(B, S, C) + b_a).astype(jnp.float32))
    i = jax.nn.sigmoid((jnp.einsum('bsnd,nde->bsne', xb, w_x).reshape(B, S, C) + b_x).astype(jnp.float32))
    log_a = -LRU_C * r * jax.nn.softplus(-lam.astype(jnp.float32))
    a = jnp.exp(log_a)
    u = jnp.sqrt(-jnp.expm1(2.0 * log_a)) * (i * xc.astype(jnp.float32))

    def combine(lhs, rhs):
        a1, b1 = lhs
        a2, b2 = rhs
        return a1 * a2, a2 * b1 + b2

    _, h = lax.associative_scan(combine, (a, u), axis=1)
    return h.astype(x.dtype)

def hybrid_layer(x, w_in, w_out, ln_g, ln_b, cmp_pos, cmp_w, conv_w, conv_b, w_a, b_a, w_x, b_x, lam):
    proj = x @ w_in
    (rq, rk, rv, rg, nq, nkc, nvc, nks, nvs, nkw, nvw, ng, ngl, lx, lg) = jnp.split(proj, IN_SPLIT_POINTS, axis=-1)
    y_ret = retention(rq, rk, rv) * jax.nn.silu(rg)
    y_nsa = nsa(nq, nkc, nvc, nks, nvs, nkw, nvw, ngl, cmp_pos, cmp_w) * jax.nn.silu(ng)
    y_lru = rg_lru(lx, conv_w, conv_b, w_a, b_a, w_x, b_x, lam) * jax.nn.silu(lg)
    y = jnp.concatenate([y_ret, y_nsa, y_lru], axis=-1) @ w_out
    return layer_norm(DEEPNORM_ALPHA * x + y, ln_g, ln_b)

def first_inputs(seed: int = 0) -> dict:
    key = jax.random.key(seed)
    ks = jax.random.split(key, 16)
    f32 = jnp.float32
    x = jax.random.normal(ks[0], (BATCH, SEQ, D_MODEL), f32)
    w_in = jax.random.normal(ks[1], (DEPTH, D_MODEL, D_IN), f32) * D_MODEL ** -0.5
    w_out = jax.random.normal(ks[2], (DEPTH, D_MIX, D_MODEL), f32) * (D_MIX ** -0.5) * DEEPNORM_BETA
    ln_g = 1.0 + 0.02 * jax.random.normal(ks[3], (DEPTH, D_MODEL), f32)
    ln_b = 0.02 * jax.random.normal(ks[4], (DEPTH, D_MODEL), f32)
    nsa_cmp_pos = 0.1 * jax.random.normal(ks[5], (DEPTH, 2, CMP_LEN, HEAD_DIM), f32)
    nsa_cmp_w = jax.random.normal(ks[6], (DEPTH, 2, CMP_LEN * HEAD_DIM, HEAD_DIM), f32) * (CMP_LEN * HEAD_DIM) ** -0.5
    lru_conv_w = jax.random.normal(ks[7], (DEPTH, CONV_WIDTH, LRU_WIDTH), f32) * CONV_WIDTH ** -0.5
    lru_conv_b = 0.02 * jax.random.normal(ks[8], (DEPTH, LRU_WIDTH), f32)
    lru_w_a = jax.random.normal(ks[9], (DEPTH, LRU_BLOCKS, LRU_BLOCK_DIM, LRU_BLOCK_DIM), f32) * LRU_BLOCK_DIM ** -0.5
    lru_b_a = 0.02 * jax.random.normal(ks[10], (DEPTH, LRU_WIDTH), f32)
    lru_w_x = jax.random.normal(ks[11], (DEPTH, LRU_BLOCKS, LRU_BLOCK_DIM, LRU_BLOCK_DIM), f32) * LRU_BLOCK_DIM ** -0.5
    lru_b_x = 0.02 * jax.random.normal(ks[12], (DEPTH, LRU_WIDTH), f32)
    u = jax.random.uniform(ks[13], (DEPTH, LRU_WIDTH), f32, minval=0.9, maxval=0.999)
    a0 = u ** (1.0 / LRU_C)
    lru_lambda = jnp.log(a0) - jnp.log1p(-a0)
    return {"x": x, "w_in": w_in, "w_out": w_out, "ln_g": ln_g, "ln_b": ln_b,
            "nsa_cmp_pos": nsa_cmp_pos, "nsa_cmp_w": nsa_cmp_w,
            "lru_conv_w": lru_conv_w, "lru_conv_b": lru_conv_b,
            "lru_w_a": lru_w_a, "lru_b_a": lru_b_a, "lru_w_x": lru_w_x, "lru_b_x": lru_b_x,
            "lru_lambda": lru_lambda}

def first_block(x, w_in, w_out, ln_g, ln_b, nsa_cmp_pos, nsa_cmp_w, lru_conv_w, lru_conv_b,
              lru_w_a, lru_b_a, lru_w_x, lru_b_x, lru_lambda):
    for l in range(DEPTH):
        x = hybrid_layer(x, w_in[l], w_out[l], ln_g[l], ln_b[l], nsa_cmp_pos[l], nsa_cmp_w[l],
                         lru_conv_w[l], lru_conv_b[l], lru_w_a[l], lru_b_a[l], lru_w_x[l], lru_b_x[l],
                         lru_lambda[l])
    return x


N_MIXERS = 2
DSW_GROUPS = ((128, 1), (512, 4), (2048, 16))
DSW_N_GROUPS = len(DSW_GROUPS)
DSW_HEADS_PER_GROUP = D_MODEL // (2 * HEAD_DIM)
DSW_HEADS = DSW_N_GROUPS * DSW_HEADS_PER_GROUP
DSW_OUT_WIDTH = DSW_HEADS_PER_GROUP * HEAD_DIM
MOBA_HEADS = D_MODEL // HEAD_DIM
MOBA_BLOCK = 256
MOBA_TOPK = 3
MOBA_Q_CHUNK = 32
D_FF = 4 * D_MODEL
REL_BUCKETS = 32
REL_MAX_DISTANCE = 2048
BIAS_HEADS = max(DSW_HEADS, MOBA_HEADS)

N_A_LAYERS = (DEPTH + 1) // 2
N_B_LAYERS = DEPTH // 2
EPS = 1e-6
NEG = -1e30
SCALE = HEAD_DIM ** -0.5


def rmsnorm(x, g):
    xf = x.astype(jnp.float32)
    y = xf * lax.rsqrt(jnp.mean(xf * xf, axis=-1, keepdims=True) + EPS)
    return (y * g.astype(jnp.float32)).astype(x.dtype)

def t5_bucket(dist):
    n = jnp.maximum(dist, 0)
    max_exact = REL_BUCKETS // 2
    nf = jnp.maximum(n, 1).astype(jnp.float32)
    large = max_exact + (jnp.log(nf / max_exact) / math.log(REL_MAX_DISTANCE / max_exact)
                         * (REL_BUCKETS - max_exact)).astype(jnp.int32)
    large = jnp.minimum(large, REL_BUCKETS - 1)
    return jnp.where(n < max_exact, n, large)

def softmax_attend(logits, v, eq):
    m = jnp.max(logits, axis=-1, keepdims=True)
    p = jnp.exp(logits - m)
    den = jnp.sum(p, axis=-1, keepdims=True)
    o = jnp.einsum(eq, p / den, v.astype(jnp.float32))
    return o, (m + jnp.log(den))[..., 0]

def dsw_group(q, k, v, rel_bias, col0, window, dilation):
    B, H, S, hd = q.shape
    n = window // dilation
    blk = n
    L = S // dilation
    nb = -(-L // blk)
    Lp = nb * blk

    def to_sub(t):
        t = t.reshape(B, H, L, dilation, hd).transpose(0, 1, 3, 2, 4)
        return jnp.pad(t, ((0, 0), (0, 0), (0, 0), (0, Lp - L), (0, 0)))

    def band(t):
        t = jnp.pad(t, ((0, 0), (0, 0), (0, 0), (blk, 0), (0, 0))).reshape(B, H, dilation, nb + 1, blk, hd)
        return jnp.concatenate([t[:, :, :, :-1], t[:, :, :, 1:]], axis=4)

    qs, ks, vs = to_sub(q), to_sub(k), to_sub(v)
    qb = qs.reshape(B, H, dilation, nb, blk, hd)
    kb, vb = band(ks), band(vs)
    logits = jnp.einsum('bhrnid,bhrnjd->bhrnij', qb, kb, preferred_element_type=jnp.float32) * SCALE

    i = jnp.arange(blk)[:, None]
    j = jnp.arange(2 * blk)[None, :]
    dist = blk + i - j
    in_band = (dist >= 0) & (dist <= n)
    first = (jnp.arange(nb) == 0)[:, None, None] & (j < blk)[None]
    mask = in_band[None] & ~first
    bias = rel_bias[t5_bucket(dist * dilation)][..., col0:col0 + H].transpose(2, 0, 1)
    logits = jnp.where(mask[None, None, None], logits + bias[None, :, None, None], NEG)

    o, lse = softmax_attend(logits, vb, 'bhrnij,bhrnjd->bhrnid')
    o = o.reshape(B, H, dilation, Lp, hd)[:, :, :, :L].transpose(0, 1, 3, 2, 4).reshape(B, H, S, hd)
    lse = lse.reshape(B, H, dilation, Lp)[..., :L].transpose(0, 1, 3, 2).reshape(B, H, S)
    return o, lse

def dsw_mixer(h, w_qkv, q_gain, k_gain, w_o, rel_bias):
    B, S, _ = h.shape
    G, Hg = DSW_N_GROUPS, DSW_HEADS_PER_GROUP
    qkv = (h @ w_qkv).reshape(B, S, 3, G, Hg, HEAD_DIM)
    q = rmsnorm(qkv[:, :, 0], q_gain)
    k = rmsnorm(qkv[:, :, 1], k_gain)
    v = qkv[:, :, 2]
    outs, lses = [], []
    for g, (window, dilation) in enumerate(DSW_GROUPS):
        o, lse = dsw_group(q[:, :, g].transpose(0, 2, 1, 3), k[:, :, g].transpose(0, 2, 1, 3),
                           v[:, :, g].transpose(0, 2, 1, 3), rel_bias, g * Hg, window, dilation)
        outs.append(o)
        lses.append(lse)
    wts = jax.nn.softmax(jnp.stack(lses), axis=0)
    o = jnp.einsum('gbhs,gbhsd->bshd', wts, jnp.stack(outs)).reshape(B, S, DSW_OUT_WIDTH)
    return o.astype(h.dtype) @ w_o

def gather_blocks(blocks, idx):
    return jax.vmap(jax.vmap(lambda bl, ix: bl[ix]))(blocks, idx)

def moba_mixer(h, w_qkv, q_gain, k_gain, w_o, rel_bias):
    B, S, _ = h.shape
    H, hd, blk = MOBA_HEADS, HEAD_DIM, MOBA_BLOCK
    qkv = (h @ w_qkv).reshape(B, S, 3, H, hd)
    q = rmsnorm(qkv[:, :, 0], q_gain).transpose(0, 2, 1, 3)
    k = rmsnorm(qkv[:, :, 1], k_gain).transpose(0, 2, 1, 3)
    v = qkv[:, :, 2].transpose(0, 2, 1, 3)
    nblk = -(-S // blk)
    Sp = nblk * blk
    pad = ((0, 0), (0, 0), (0, Sp - S), (0, 0))
    q, k, v = jnp.pad(q, pad), jnp.pad(k, pad), jnp.pad(v, pad)
    qb = q.reshape(B, H, nblk, blk, hd)
    kb = k.reshape(B, H, nblk, blk, hd)
    vb = v.reshape(B, H, nblk, blk, hd)
    pos = jnp.arange(Sp)
    qblk = pos // blk
    table_h = rel_bias[:, :H].T

    ii = jnp.arange(blk)
    own_bias = table_h[:, t5_bucket(ii[:, None] - ii[None, :])]
    lo = jnp.einsum('bhnid,bhnjd->bhnij', qb, kb, preferred_element_type=jnp.float32) * SCALE
    lo = jnp.where(ii[:, None] >= ii[None, :], lo + own_bias[None, :, None], NEG)
    o_own, lse_own = softmax_attend(lo, vb, 'bhnij,bhnjd->bhnid')
    o_own = o_own.reshape(B, H, Sp, hd)
    lse_own = lse_own.reshape(B, H, Sp)

    kmean = jnp.mean(kb.astype(jnp.float32), axis=3)
    gate = jnp.einsum('bhsd,bhnd->bhsn', q.astype(jnp.float32), kmean)
    past = jnp.arange(nblk)[None, :] < qblk[:, None]
    gate = jnp.where(past, gate, -jnp.inf)
    topk = min(MOBA_TOPK, nblk)
    _, sel = lax.top_k(gate, topk)
    sel_valid = sel < qblk[:, None]

    C = MOBA_Q_CHUNK
    nC = Sp // C

    def chunk(t):
        return jnp.moveaxis(t.reshape(B, H, nC, C, *t.shape[3:]), 2, 0)

    jj = jnp.arange(blk)
    head_ix = jnp.arange(H)[None, :, None, None]

    def attend(args):
        qc, selc, validc, posc = args
        flat = selc.reshape(B, H, C * topk)
        kg = gather_blocks(kb, flat).reshape(B, H, C, topk * blk, hd)
        vg = gather_blocks(vb, flat).reshape(B, H, C, topk * blk, hd)
        logits = jnp.einsum('bhcd,bhckd->bhck', qc, kg, preferred_element_type=jnp.float32) * SCALE
        kpos = (selc[..., None] * blk + jj).reshape(B, H, C, topk * blk)
        bias = table_h[head_ix, t5_bucket(posc[None, None, :, None] - kpos)]
        valid = jnp.repeat(validc, blk, axis=-1)
        logits = jnp.where(valid, logits + bias, NEG)
        return softmax_attend(logits, vg, 'bhck,bhckd->bhcd')

    o_sel, lse_sel = lax.map(attend, (chunk(q), chunk(sel), chunk(sel_valid), pos.reshape(nC, C)))
    o_sel = jnp.moveaxis(o_sel, 0, 2).reshape(B, H, Sp, hd)
    lse_sel = jnp.moveaxis(lse_sel, 0, 2).reshape(B, H, Sp)

    lse = jnp.logaddexp(lse_own, lse_sel)
    o = jnp.exp(lse_own - lse)[..., None] * o_own + jnp.exp(lse_sel - lse)[..., None] * o_sel
    o = o[:, :, :S].transpose(0, 2, 1, 3).reshape(B, S, H * hd)
    return o.astype(h.dtype) @ w_o

def sq_relu_mlp(h, w1, w2):
    return jnp.square(jax.nn.relu(h @ w1)) @ w2

def second_inputs(seed: int = 0) -> dict:
    key = jax.random.key(seed)
    ks = jax.random.split(key, 16)
    D = D_MODEL
    nrm = lambda k, shape, s: jax.random.normal(k, shape, jnp.float32) * s
    a_qkv_cols = 3 * DSW_HEADS * HEAD_DIM
    b_qkv_cols = 3 * MOBA_HEADS * HEAD_DIM
    return {
        "x": nrm(ks[0], (BATCH, SEQ, D), 1.0),
        "rel_bias": nrm(ks[1], (REL_BUCKETS, BIAS_HEADS), 0.3),
        "norm_mix": 1.0 + nrm(ks[2], (DEPTH, D), 0.02),
        "norm_ffn": 1.0 + nrm(ks[3], (DEPTH, D), 0.02),
        "a_w_qkv": nrm(ks[4], (N_A_LAYERS, D, a_qkv_cols), D ** -0.5),
        "a_q_gain": 1.0 + nrm(ks[5], (N_A_LAYERS, HEAD_DIM), 0.02),
        "a_k_gain": 1.0 + nrm(ks[6], (N_A_LAYERS, HEAD_DIM), 0.02),
        "a_w_o": nrm(ks[7], (N_A_LAYERS, DSW_OUT_WIDTH, D), DSW_OUT_WIDTH ** -0.5),
        "b_w_qkv": nrm(ks[8], (N_B_LAYERS, D, b_qkv_cols), D ** -0.5),
        "b_q_gain": 1.0 + nrm(ks[9], (N_B_LAYERS, HEAD_DIM), 0.02),
        "b_k_gain": 1.0 + nrm(ks[10], (N_B_LAYERS, HEAD_DIM), 0.02),
        "b_w_o": nrm(ks[11], (N_B_LAYERS, MOBA_HEADS * HEAD_DIM, D), (MOBA_HEADS * HEAD_DIM) ** -0.5),
        "ffn_w1": nrm(ks[12], (DEPTH, D, D_FF), D ** -0.5),
        "ffn_w2": nrm(ks[13], (DEPTH, D_FF, D), 0.5 * D_FF ** -0.5),
    }

def second_block(x, rel_bias, norm_mix, norm_ffn, a_w_qkv, a_q_gain, a_k_gain, a_w_o,
              b_w_qkv, b_q_gain, b_k_gain, b_w_o, ffn_w1, ffn_w2):
    h = x
    for i in range(DEPTH):
        u = rmsnorm(h, norm_mix[i])
        li = i // N_MIXERS
        if i % N_MIXERS == 0:
            h = h + dsw_mixer(u, a_w_qkv[li], a_q_gain[li], a_k_gain[li], a_w_o[li], rel_bias)
        else:
            h = h + moba_mixer(u, b_w_qkv[li], b_q_gain[li], b_k_gain[li], b_w_o[li], rel_bias)
        h = h + sq_relu_mlp(rmsnorm(h, norm_ffn[i]), ffn_w1[i], ffn_w2[i])
    return h


def setup_inputs(seed=0):
    out = dict(first_inputs(seed))
    for name, value in second_inputs(seed + 1).items():
        if name != "x":
            out[name + "_2"] = value
    return out


def reference(
    x, w_in, w_out, ln_g, ln_b, nsa_cmp_pos, nsa_cmp_w, lru_conv_w, lru_conv_b, lru_w_a,
    lru_b_a, lru_w_x, lru_b_x, lru_lambda, rel_bias_2, norm_mix_2, norm_ffn_2, a_w_qkv_2,
    a_q_gain_2, a_k_gain_2, a_w_o_2, b_w_qkv_2, b_q_gain_2, b_k_gain_2, b_w_o_2, ffn_w1_2,
    ffn_w2_2,
):
    x = first_block(
        x, w_in, w_out, ln_g, ln_b, nsa_cmp_pos, nsa_cmp_w, lru_conv_w, lru_conv_b, lru_w_a,
        lru_b_a, lru_w_x, lru_b_x, lru_lambda,
    )
    return second_block(
        x, rel_bias_2, norm_mix_2, norm_ffn_2, a_w_qkv_2, a_q_gain_2, a_k_gain_2, a_w_o_2,
        b_w_qkv_2, b_q_gain_2, b_k_gain_2, b_w_o_2, ffn_w1_2, ffn_w2_2,
    )


_drawn_inputs = setup_inputs


def setup_inputs(seed=0):
    import zlib

    import numpy as np

    out = dict(_drawn_inputs(seed))
    spreads = {}
    factors = {'nsa_cmp_pos': 4.6,
     'lru_conv_b': 4.727,
     'lru_b_a': 8.0,
     'lru_b_x': 8.0,
     'norm_mix_2': 6.167,
     'norm_ffn_2': 3.516,
     'a_q_gain_2': 8.0,
     'a_k_gain_2': 8.0,
     'b_q_gain_2': 8.0,
     'b_k_gain_2': 8.0}
    for name, (base, spread) in spreads.items():
        noise = np.random.default_rng([zlib.crc32(name.encode()), seed]).standard_normal(out[name].shape)
        drawn = base * np.exp(spread * noise) if base else spread * noise
        out[name] = __import__('jax').numpy.asarray(drawn.astype(out[name].dtype))
    for name, factor in factors.items():
        out[name] = (out[name] * factor).astype(out[name].dtype)
    return out
```

```python
import math
from contextlib import ExitStack

import numpy as np

import concourse.bass as bass
from concourse import mybir

S = 256
TT = S // 128
D = 1024
KD = D // 128
HD = 64
LAYERS = 2
D_IN = 3352
D_FF = 4096
RET_HEADS, NSA_HEADS, NSA_GROUPS, DSW_GROUPS, DSW_HEADS, MOBA_HEADS = 4, 8, 2, 3, 8, 16
N_CMP = 15
ALPHA = (2.0 * LAYERS) ** 0.25
NEG = -1.0e30
COL = dict(rq=0, rk=256, rv=512, rg=768, nq=1024, nkc=1536, nvc=1664, nks=1792, nvs=1920,
           nkw=2048, nvw=2176, ng=2304, ngl=2816, lx=2840, lg=3096)

PARAMS = ["x", "w_in", "w_out", "ln_g", "ln_b", "nsa_cmp_pos", "nsa_cmp_w", "lru_conv_w", "lru_conv_b",
          "lru_w_a", "lru_b_a", "lru_w_x", "lru_b_x", "lru_lambda", "rel_bias_2", "norm_mix_2",
          "norm_ffn_2", "a_w_qkv_2", "a_q_gain_2", "a_k_gain_2", "a_w_o_2", "b_w_qkv_2", "b_q_gain_2",
          "b_k_gain_2", "b_w_o_2", "ffn_w1_2", "ffn_w2_2"]


def shape_constants():
    half = HD // 2
    inv = (1.0 / (10000.0 ** (np.arange(half, dtype=np.float32) / half))).astype(np.float32)
    ang = (np.arange(S, dtype=np.float32)[:, None] * inv[None, :]).astype(np.float32)
    rope = np.stack([np.cos(ang.astype(np.float64)), np.sin(ang.astype(np.float64))])
    rope = rope.reshape(2, TT, 128, half).transpose(2, 0, 1, 3)
    p, c = np.arange(128)[:, None], np.arange(S)[None, :]
    decay = np.zeros((128, RET_HEADS, S))
    for h in range(RET_HEADS):
        decay[:, h] = np.where(c >= p, (1.0 - 2.0 ** (-5.0 - h)) ** np.maximum(c - p, 0) * HD ** -0.5, 0.0)
    causal = np.where(c <= 128 + p, 0.0, NEG)
    tok = np.arange(S)
    seen = (np.arange(16)[None, :] * 16 + 31 <= tok[:, None]) & (np.arange(16)[None, :] < N_CMP)
    cmp_mask = np.where(seen, 0.0, NEG).reshape(TT, 128, 16).transpose(1, 0, 2)
    cmp_any = seen.any(1).reshape(TT, 128).T
    row = np.arange(128)
    head_of = (row // 16 % 2 * 4 + row // 32)[:, None] == np.arange(8)[None, :]
    rep = np.arange(32)[:, None] == (row % 32)[None, :]
    half_of = (np.arange(128)[:, None] // 64 == np.arange(2)[None, :])
    dist = np.arange(384) - 127
    n = np.maximum(dist, 1)
    large = 16 + (np.log(n / 16) / math.log(2048 / 16) * 16).astype(np.int64)
    bucket = np.where(dist < 16, np.maximum(dist, 0), np.minimum(large, 31))
    hot = np.zeros((33, 4, 384))
    for kind, ok in enumerate([(dist >= 0) & (dist <= 128), (dist >= 0) & (dist % 4 == 0),
                               (dist >= 0) & (dist % 16 == 0), dist >= 0]):
        hot[bucket, kind, np.arange(384)] = 1.0
        hot[32, kind] = np.where(ok, 0.0, NEG)
    f = lambda a: np.ascontiguousarray(a, dtype=np.float32)
    return {"c_rope": f(rope), "c_decay": f(decay), "c_causal": f(causal), "c_cmp_mask": f(cmp_mask),
            "c_cmp_any": f(cmp_any), "c_head_of": f(head_of), "c_half_of": f(half_of), "c_hot": f(hot),
            "c_ident": f(np.eye(128)), "c_rep": f(rep)}


def build(nc, dram, out):
    F = mybir.dt.float32
    FR = mybir.dt.float32r
    I32 = mybir.dt.int32
    ALU = mybir.AluOpType
    ACT = mybir.ActivationFunctionType
    AX = mybir.AxisListType.X

    BLOCKS = []
    FIRST = {}

    def add_blocks(name, w, row0, rows, col_list, form, use):
        FIRST.setdefault(name, len(BLOCKS))
        for c0, n in col_list:
            BLOCKS.append(dict(w=w, row0=row0, kts=rows // 128, c0=c0, n=n, form=form, use=use,
                               first=True, last=True, act0=0, name=name))

    for l in range(LAYERS):
        w = dram["w_in"][l]
        add_blocks(f"in{l}", w, 0, D, [(512 * i, 512) for i in range(5)] + [(2560, COL["lx"] - 2560)], "tok", "proj")
        add_blocks(f"in{l}", w, 0, D, [(COL["lx"], 512)], "feat", "lru")
        add_blocks(f"out{l}", dram["w_out"][l], 0, D, [(0, 512), (512, 512)], "tok", "deepnorm")

    def add_ffn(l):
        add_blocks(f"up{l}", dram["ffn_w1_2"][l], 0, D, [(512 * i, 512) for i in range(8)], "feat", "relu2")
        FIRST[f"down{l}"] = len(BLOCKS)
        for c in range(2):
            for k in range(4):
                BLOCKS.append(dict(w=dram["ffn_w2_2"][l], row0=k * D, kts=8, c0=512 * c, n=512, form="tok",
                                   use="residual", first=k == 0, last=k == 3, act0=8 * k, name=f"down{l}"))

    add_blocks("dsw", dram["a_w_qkv_2"][0], 0, D, [(512 * i, 512) for i in range(6)], "tok", "qk")
    add_blocks("dsw", dram["a_w_qkv_2"][0], 0, D, [(512 * i, 512) for i in range(6, 9)], "tok", "proj")
    add_blocks("dswo", dram["a_w_o_2"][0], 0, 512, [(0, 512), (512, 512)], "tok", "residual")
    add_ffn(0)
    add_blocks("moba", dram["b_w_qkv_2"][0], 0, D, [(512 * i, 512) for i in range(4)], "tok", "qk")
    add_blocks("moba", dram["b_w_qkv_2"][0], 0, D, [(512 * i, 512) for i in range(4, 6)], "tok", "proj")
    add_blocks("mobao", dram["b_w_o_2"][0], 0, D, [(0, 512), (512, 512)], "tok", "residual")
    add_ffn(1)
    NB = len(BLOCKS)
    CHUNKS = [(b, j) for b in range(NB) for j in range(BLOCKS[b]["kts"] // 4)]
    CHUNK0 = [sum(x["kts"] // 4 for x in BLOCKS[:b]) for b in range(NB + 1)]
    RAW = 3
    AHEAD = 2

    ACTS = [8, 8, 8, 8, 8, 4, 8, 8, 8, 8]
    X0, Y0, X1, Y1, DSW_U, DSW_Y, FFN0_U, MOBA_U, MOBA_Y, FFN1_U = range(10)
    LRU_CHUNK = [0, 1, 0, 1, 0, 0, 0, 0, 0, 0]
    ACT0 = [sum(ACTS[:i]) // 2 for i in range(11)]

    TRANS0 = [sum(n // 2 - c for n, c in zip(ACTS[:i], LRU_CHUNK)) for i in range(10)]

    UNIT0 = [0, 16, 32, 40]
    PCH0 = [0, 16, 32, 56]
    STG0 = [0, 8, 16, 40]

    ctx = ExitStack()
    with ctx:
        def sb(name, shape, dt=F):
            return ctx.enter_context(nc.sbuf_tensor(name, shape, dt))

        def sem(name):
            return ctx.enter_context(nc.semaphore(name))

        x = sb("x_res", [128, TT, D])
        y = sb("y_tok", [128, TT, D])
        act_hi = sb("act_hi", [128, KD, S], FR)
        act_lo = sb("act_lo", [128, KD, S], FR)
        w_raw = sb("w_raw", [128, RAW, 4, 512])
        w_hi = sb("w_hi", [128, AHEAD, 8, 512], FR)
        w_lo = sb("w_lo", [128, AHEAD, 8, 512], FR)
        ident = sb("ident", [128, 128])
        rope = sb("rope", [128, 2, TT, HD // 2])
        decay = sb("decay", [128, RET_HEADS, S])
        causal = sb("causal", [128, S])
        cmp_mask = sb("cmp_mask", [128, TT, 16])
        cmp_any = sb("cmp_any", [128, TT])
        head_of = sb("head_of", [128, 8])
        half_of = sb("half_of", [128, 2])
        rep = sb("rep", [32, 128])
        norm_g = sb("norm_g", [128, 4, KD])
        qk_g = sb("qk_g", [128, 4])
        qk_gain = sb("qk_gain", [128, 2])
        conv_w = sb("conv_w", [128, LAYERS, 2, 4])
        lru_v = sb("lru_v", [128, LAYERS, 4, 2])
        lru_hb = sb("lru_hb", [128, LAYERS, 2, 2])
        lru_sp = sb("lru_sp", [128, LAYERS * 2])
        lam_exp = sb("lam_exp", [128, LAYERS * 2])
        lam_p = sb("lam_p", [128, 4, LAYERS * 2])
        bn = sb("bn", [128, TT, 12])
        mv = sb("mv", [128, TT, 2])
        gate_w = sb("gate_w", [128, LAYERS, 2, 2, 128])
        relb = sb("relb", [33, 24])
        st = sb("st", [128, 8, 16])
        ttr = sb("ttr_min", [128, 2, TT])
        den = sb("den", [128, 16, TT])
        rden = sb("rden", [128, 4, TT])
        gate_c = sb("gate_c", [128, TT, 24])
        AREA = 19008
        with nc.sbuf_tensor("area", [128, AREA], F) as area:
            pass
        hid = ctx.enter_context(nc.sbuf_tensor("hid", [128, 2, 32, S], FR))
        pad = sb("area_rest", [128, AREA - 16384])
        h_hi, h_lo = hid[:, 0], hid[:, 1]

        def cut(at, n, pattern=None, **sizes):
            v = area[:, at:at + n]
            return v.rearrange(pattern, **sizes) if pattern else v

        proj = cut(0, TT * 2840, "p (t n) -> p t n", t=TT)
        R = TT * 2840
        rot = cut(R, 1024, "p (t n) -> p t n", t=TT)
        rot_b = cut(R + 1024, 1024, "p (t n) -> p t n", t=TT)
        ret_T = cut(R + 2048, 1024, "p (c n) -> p c n", c=4)
        ret_P = cut(R + 3072, 1536, "p (h n) -> p h n", h=4)
        lru_w = cut(R, 3584, "p (k c n) -> p k c n", k=7, c=2)
        R += 4608
        nT = cut(R, 3072, "p (c n) -> p c n", c=12)
        R += 3072
        blk = cut(R, 1024, "p (v m n) -> p v m n", v=2, m=16)
        R += 1024
        cw = cut(R, 2048, "p (v m n) -> p v m n", v=2, m=16)
        R += 2048
        lru_T = cut(R, 1024, "p (c n) -> p c n", c=4)
        R += 1024
        nsa_P = cut(R, 768, "p (s n) -> p s n", s=2)
        R += 768
        k_dup = cut(R - 768, 1024, "p (v t g n) -> p v t g n", v=2, t=2, g=2)
        nsa_PT = cut(R, 768, "p (s n) -> p s n", s=2)
        assert R + 768 <= AREA
        v_bd = cut(0 + TT * 2840, 512, "p (h n) -> p h n", h=8)
        k_bd = cut(TT * 2840 + 512, 32, "p (g n) -> p g n", g=2)
        k_c2 = cut(TT * 2840 + 544, 128, "p (c n) -> p c n", c=2)
        v_c = cut(TT * 2840 + 672, 64)
        cmp_L = cut(TT * 2840 + 1024, 256)
        cmp_PT = cut(TT * 2840 + 1280, 256)
        cmp_pos = cut(TT * 2840 + 1536, 32, "p (v m) -> p v m", v=2)
        tmp_tok = cut(TT * 2840 + 3072, 1536)
        ln_v = cut(0, 2048, "p (v n) -> p v n", v=2)
        qkv = cut(0, 9216, "p (t n) -> p t n", t=TT)
        sq = cut(9216, 1024, "p (t n) -> p t n", t=TT)
        stage = cut(10240, 3072, "p (s c n) -> p s c n", s=2, c=6)
        big_P = cut(13312, 2304, "p (s n) -> p s n", s=2)
        big_PT = cut(15616, 1536, "p (s n) -> p s n", s=4)
        bias_T = cut(17152, 1536, "p (s n) -> p s n", s=2)
        hot = cut(0, 1536, "p (k n) -> p k n", k=4)
        vec = cut(1536, 1536, "p (k n) -> p k n", k=4)

        ps = [ctx.enter_context(nc.psum_tensor(f"ps{i}", [128, 512], F)) for i in (0, 1)]
        ps23 = ctx.enter_context(nc.psum_tensor("ps23", [128, 1024], F))
        ps4, ps5, ps6, ps7 = [ctx.enter_context(nc.psum_tensor(f"ps{i}", [128, 512], F)) for i in (4, 5, 6, 7)]
        tr_bank = [ps4, ps5]
        bias_vec = nc.dram_tensor("bias_vec", [4, 16, 384], F, kind="Internal").ap()

        w_arrived = [sem(f"w_arrived{i}") for i in range(RAW)]
        w_hi_done = sem("w_hi_done")
        w_lo_done = sem("w_lo_done")
        acc_ready = sem("acc_ready")
        acc_free = [sem("acc_free0"), sem("acc_free1")]
        consts_in = sem("consts_in")
        x_in = sem("x_in")
        hot_in = sem("hot_in")
        gatew_zero = sem("gatew_zero")
        relb_in = sem("relb_in")
        relb_one = sem("relb_one")
        cw_in = sem("cw_in")
        ln_in = sem("ln_in")
        y_ready = sem("y_ready")
        src_ready = sem("src_ready")
        at_ps = sem("at_ps")
        at_hi = sem("at_hi")
        at_lo = sem("at_lo")
        vec_ps = sem("vec_ps")
        vec_sb = sem("vec_sb")
        vec_out = sem("vec_out")
        bias_in = [sem("bias_in0"), sem("bias_in1")]
        stg_ps = sem("stg_ps")
        stg_a = sem("stg_a")
        stg_d = sem("stg_d")
        rot_done = sem("rot_done")
        rs_ps = sem("rs_ps")
        rs_sb = sem("rs_sb")
        ro_ps = sem("ro_ps")
        ro_used = sem("ro_used")
        tanh_done = sem("tanh_done")
        cmp_blk = sem("cmp_blk")
        k_dup_done = sem("k_dup_done")
        cmp_raw = sem("cmp_raw")
        cmp_tok = sem("cmp_tok")
        cmp_kv = sem("cmp_kv")
        cmp_kv_used = sem("cmp_kv_used")
        cmp_s = sem("cmp_s")
        cmp_l = sem("cmp_l")
        cmp_p = sem("cmp_p")
        cmp_t = sem("cmp_t")
        cmp_pt = sem("cmp_pt")
        cmp_o = sem("cmp_o")
        cmp_o_used = sem("cmp_o_used")
        s_ready = sem("s_ready")
        ttr_done = sem("ttr_done")
        p_ready = sem("p_ready")
        t_ready = sem("t_ready")
        pt_a = sem("pt_a")
        pt_d = sem("pt_d")
        o_ready = sem("o_ready")
        o_free = sem("o_free")
        lru_x = sem("lru_x")
        lru_xc = sem("lru_xc")
        lru_z = sem("lru_z")
        lru_th = sem("lru_th")
        lru_nla = sem("lru_nla")
        lru_at = sem("lru_at")
        lru_v2 = sem("lru_v2")
        lru_m = sem("lru_m")
        lru_y = sem("lru_y")
        h_done = sem("h_done")
        hh_done = sem("hh_done")
        hl_done = sem("hl_done")
        qk_norm = sem("qk_norm")
        ssq_done = sem("ssq_done")
        rstd_done = sem("rstd_done")
        x_new = sem("x_new")
        out_done = sem("out_done")
        lam_abs = sem("lam_abs")
        lam_e = sem("lam_e")
        dve_step = sem("dve_step")
        small_in = sem("small_in")

        NEEDS = {"in0": X0, "out0": Y0, "in1": X1, "out1": Y1, "dsw": DSW_U, "dswo": DSW_Y,
                 "up0": FFN0_U, "moba": MOBA_U, "mobao": MOBA_Y, "up1": FFN1_U}
        USED_BY = ["in0", "out0", "in1", "out1", "dsw", "dswo", "up0", "moba", "mobao", "up1"]
        last_block = {}
        for b, d in enumerate(BLOCKS):
            last_block[d["name"]] = b

        def blocks(name):
            return range(FIRST[name], last_block[name] + 1)

        def free_count(b):
            return sum(d["last"] for d in BLOCKS[:b])

        HIDDEN0 = {0: 0, 1: 16}

        block = ctx.enter_context(nc.Block())

        @block.sync
        def _(sp):
            sp.dma_start(x[:, :, :], dram["x"][0].rearrange("(t p) d -> p t d", p=128)).then_inc(x_in, 16)
            for c, (b, j) in enumerate(CHUNKS):
                d = BLOCKS[b]
                if c >= RAW:
                    sp.wait_ge(w_lo_done, c - RAW + 1)
                r0 = d["row0"] + 512 * j
                src = d["w"][r0:r0 + 512, d["c0"]:d["c0"] + d["n"]].rearrange("(k p) n -> p k n", p=128)
                sp.dma_start(w_raw[:, c % RAW, :, 0:d["n"]], src).then_inc(w_arrived[c % RAW], 16)
            for half in range(2):
                sp.wait_ge(acc_free[half], free_count(NB))
            sp.dma_start(out[0].rearrange("(t p) d -> p t d", p=128), x[:, :, :]).then_inc(out_done, 16)
            sp.wait_ge(out_done, 16)

        @block.gpsimd
        def _(pool):
            pool.memset(gate_w[:, :, :, :, :], 0.0).then_inc(gatew_zero, 1)
            pool.wait_ge(gatew_zero, 1)
            pool.memset(relb[32:33, :], 1.0).then_inc(relb_one, 1)
            with nc.allow_non_contiguous_dma(reason="vectors of one element per partition"):
                for dst, src in ((ident, "c_ident"), (rope, "c_rope"), (decay, "c_decay"),
                                 (causal, "c_causal"), (cmp_mask, "c_cmp_mask"), (cmp_any, "c_cmp_any"),
                                 (head_of, "c_head_of"), (half_of, "c_half_of"), (rep, "c_rep")):
                    n = len(dst.shape)
                    pool.dma_start(dst[tuple([slice(None)] * n)], dram[src]).then_inc(consts_in, 16)
                pool.dma_start(hot[0:33], dram["c_hot"]).then_inc(hot_in, 16)
                pool.dma_start(relb[0:32, :], dram["rel_bias_2"]).then_inc(relb_in, 16)
                for l in range(LAYERS):
                    for c in range(2):
                        pool.dma_start(conv_w[:, l, c], dram["lru_conv_w"][l, :, 128 * c:128 * c + 128].rearrange("k p -> p k")).then_inc(small_in, 16)
                    for i, nm in enumerate(("lru_conv_b", "lru_b_a", "lru_b_x", "lru_lambda")):
                        pool.dma_start(lru_v[:, l, i], dram[nm][l].rearrange("(c p) -> p c", p=128)).then_inc(small_in, 16)
                    pool.dma_start(norm_g[:, l], dram["norm_mix_2"][l].rearrange("(c p) -> p c", p=128)).then_inc(small_in, 16)
                    pool.dma_start(norm_g[:, 2 + l], dram["norm_ffn_2"][l].rearrange("(c p) -> p c", p=128)).then_inc(small_in, 16)
                for i, nm in enumerate(("a_q_gain_2", "a_k_gain_2", "b_q_gain_2", "b_k_gain_2")):
                    for e in range(2):
                        pool.dma_start(qk_g[64 * e:64 * e + 64, i:i + 1], dram[nm][0].rearrange("(p o) -> p o", o=1)).then_inc(small_in, 16)
                pool.wait_ge(gatew_zero, 1)
                for l in range(LAYERS):
                    for i, nm in enumerate(("lru_w_a", "lru_w_x")):
                        for n in range(4):
                            e = n % 2
                            pool.dma_start(gate_w[64 * e:64 * e + 64, l, i, n // 2, 64 * e:64 * e + 64],
                                           dram[nm][l, n]).then_inc(small_in, 16)
                pool.wait_ge(vec_sb, 1)
                pool.dma_start(bias_vec[0:3, 0:8].rearrange("k h m -> h k m"), vec[0:8, 0:3, :]).then_inc(vec_out, 16)
                pool.dma_start(bias_vec[3, 0:16], vec[0:16, 3, :]).then_inc(vec_out, 16)
                for l in range(LAYERS):
                    if l:
                        pool.wait_ge(cmp_kv_used, l)
                    for v in range(2):
                        pool.dma_start(cw[:, v], dram["nsa_cmp_w"][l, v].rearrange("(m q) e -> q m e", q=128)).then_inc(cw_in, 16)
                    b = FIRST[f"in{l}"] + 3
                    for half in range(2):
                        pool.wait_ge(acc_free[half], free_count(b) + 1)
                    for v in range(2):
                        c0 = COL[("nkc", "nvc")[v]]
                        for e in range(2):
                            ins = pool.tensor_copy(k_dup[:, v, :, :, 64 * e:64 * e + 64],
                                                   proj[:, :, c0:c0 + 128].rearrange("p t (g d) -> p t g d", g=2))
                    ins.then_inc(k_dup_done, 1)
                    pool.wait_ge(ro_used, l + 1)
                    for v in range(2):
                        for e in range(2):
                            pool.dma_start(cmp_pos[64 * e:64 * e + 64, v, :],
                                           dram["nsa_cmp_pos"][l, v].rearrange("(m e) d -> e d m", e=2)[e]).then_inc(cw_in, 16)
                    pool.wait_ge(y_ready, l + 1)
                    for i, nm in enumerate(("ln_g", "ln_b")):
                        pool.dma_start(ln_v[:, i, :], dram[nm][l].partition_broadcast(128)).then_inc(ln_in, 16)
                for u in range(DSW_HEADS + MOBA_HEADS):
                    g = UNIT0[2] + u
                    if u < 2:
                        pool.wait_ge(x_new, 2)
                        pool.wait_ge(vec_out, 32)
                    elif u == DSW_HEADS or u == DSW_HEADS + 1:
                        for half in range(2):
                            pool.wait_ge(acc_free[half], free_count(FIRST["moba"]))
                    else:
                        pool.wait_ge(ttr_done, g - 2 + 1)
                    if u < DSW_HEADS:
                        src = bass.AP(bias_vec.tensor, u * 384, [[1, 128], [16 * 384, 3], [1, S]])
                        dst = bias_T[:, u % 2, :].rearrange("p (g n) -> p g n", g=3)
                    else:
                        src = bass.AP(bias_vec.tensor, (3 * 16 + u - DSW_HEADS) * 384, [[1, 128], [1, S]])
                        dst = bias_T[:, u % 2, 0:S]
                    pool.dma_start(dst, src).then_inc(bias_in[u % 2], 16)

        SMALL = 16 * (LAYERS * 8 + 8 + LAYERS * 8)

        @block.tensor
        def _(pe):
            def gemm(b):
                d = BLOCKS[b]
                slot, n = b % AHEAD, d["n"]
                hidden = d["name"].startswith("down")
                for half in range(2):
                    bank = ps[half]
                    if d["first"] and free_count(b):
                        pe.wait_ge(acc_free[half], free_count(b))
                    if d["form"] == "tok":
                        for k in range(d["kts"]):
                            if half == 0 and k % 4 == 0:
                                pe.wait_ge(w_lo_done, CHUNK0[b] + k // 4 + 1)
                            if hidden:
                                ah = h_hi[:, d["act0"] + k, 128 * half:128 * half + 128]
                                al = h_lo[:, d["act0"] + k, 128 * half:128 * half + 128]
                            else:
                                ah = act_hi[:, k, 128 * half:128 * half + 128]
                                al = act_lo[:, k, 128 * half:128 * half + 128]
                            wh, wl = w_hi[:, slot, k, 0:n], w_lo[:, slot, k, 0:n]
                            first = d["first"] and k == 0
                            last = d["last"] and k == d["kts"] - 1
                            pe.matmul(bank[:, 0:n], ah, wh, start=first, stop=False)
                            pe.matmul(bank[:, 0:n], ah, wl, start=False, stop=False)
                            mm = pe.matmul(bank[:, 0:n], al, wh, start=False, stop=last)
                    else:
                        for f in (2 * half, 2 * half + 1):
                            o = bank[:, (f % 2) * S:(f % 2) * S + S]
                            cols = slice(128 * f, 128 * f + 128)
                            for k in range(d["kts"]):
                                if f == 0 and k % 4 == 0:
                                    pe.wait_ge(w_lo_done, CHUNK0[b] + k // 4 + 1)
                                wh, wl = w_hi[:, slot, k, cols], w_lo[:, slot, k, cols]
                                pe.matmul(o, wh, act_hi[:, k, :], start=k == 0, stop=False)
                                pe.matmul(o, wh, act_lo[:, k, :], start=False, stop=False)
                                mm = pe.matmul(o, wl, act_hi[:, k, :], start=False, stop=k == d["kts"] - 1)
                    mm.then_inc(acc_ready, 1)

            def gemms(name):
                if name in NEEDS:
                    a = NEEDS[name]
                    pe.wait_ge(at_lo, ACT0[a + 1])
                for b in blocks(name):
                    gemm(b)

            def transpose_acts(a, src, kts):
                if a == X0:
                    pe.wait_ge(x_in, 16)
                elif a == X1:
                    pe.wait_ge(x_new, 1)
                elif a in (Y0, Y1):
                    pe.wait_ge(y_ready, 1 + (a == Y1))
                elif a in (DSW_Y, MOBA_Y):
                    pe.wait_ge(o_free, {DSW_Y: UNIT0[2] + DSW_HEADS, MOBA_Y: UNIT0[3] + MOBA_HEADS}[a] // 4)
                else:
                    pe.wait_ge(src_ready, (DSW_U, FFN0_U, MOBA_U, FFN1_U).index(a) + 1)
                for i in range(kts // 2):
                    if i >= 2:
                        pe.wait_ge(at_lo, ACT0[a] + LRU_CHUNK[a] + i - 1)
                    for q in range(4):
                        k, t = 2 * i + q // 2, q % 2
                        mm = pe.transpose(tr_bank[i % 2][:, 128 * q:128 * q + 128],
                                          src[:, t, 128 * k:128 * k + 128], ident[:, :])
                    mm.then_inc(at_ps, 1)

            def retention(l):
                pe.wait_ge(rot_done, l + 1)
                for c in range(2):
                    for q in range(4):
                        p, t = q // 2, q % 2
                        mm = pe.transpose(tr_bank[c][:, 128 * q:128 * q + 128],
                                          rot[:, t, 256 * c + 128 * p:256 * c + 128 * p + 128], ident[:, :])
                    mm.then_inc(stg_ps, 1)
                pe.wait_ge(stg_a, STG0[l] // 2 + 1)
                pe.wait_ge(stg_d, STG0[l] // 2 + 1)
                for h in range(RET_HEADS):
                    p, e = h // 2, 64 * (h % 2)
                    q = ret_T[e:e + 64, p, :]
                    k = ret_T[e:e + 64, 2 + p, :]
                    o = ps23[:, 512 * (h % 2):512 * (h % 2) + 384]
                    if h >= 2:
                        pe.wait_ge(rs_sb, RET_HEADS * l + h - 1)
                    pe.matmul(o[:, 0:S], k[:, 0:128], q[:, :], start=True, stop=True)
                    pe.matmul(o[:, S:384], k[:, 128:256], q[:, 128:256], start=True, stop=True).then_inc(rs_ps, 1)
                for h in range(RET_HEADS):
                    pe.wait_ge(rs_sb, RET_HEADS * l + h + 1)
                    v = lambda t: proj[:, t, COL["rv"] + 64 * h:COL["rv"] + 64 * h + 64]
                    o1 = ps6[:, 128 * h + 64:128 * h + 128]
                    pe.matmul(o1, ret_P[:, h, 128:256], v(0), start=True, stop=False)
                    pe.matmul(o1, ret_P[:, h, 256:384], v(1), start=False, stop=True)
                    mm = pe.matmul(ps6[:, 128 * h:128 * h + 64], ret_P[:, h, 0:128], v(0), start=True, stop=True)
                mm.then_inc(ro_ps, 1)

            def unit(ph, u, what):
                kind = ("nsa", "nsa", "dsw", "moba")[ph]
                gu = UNIT0[ph] + u
                parts = 3 if kind == "dsw" else 1
                if kind == "nsa":
                    br, h = u // 8, u % 8
                    e = 64 * (h // 4)
                    q = [nT[e:e + 64, h % 4, :]]
                    k = [nT[e:e + 64, 8 + br, :]]
                    c0 = COL[("nvs", "nvw")[br]] + e
                    v = [lambda t: proj[:, t, c0:c0 + 64]]
                    P, PT, slots = nsa_P, nsa_PT, 2
                else:
                    p, e = u // 2, 64 * (u % 2)
                    q = [stage[e:e + 64, p % 2, 2 * g, :] for g in range(parts)]
                    k = [stage[e:e + 64, p % 2, 2 * g + 1, :] for g in range(parts)]
                    if kind == "dsw":
                        v = [lambda t, g=g: qkv[:, t, 512 * (6 + g) + 64 * u:512 * (6 + g) + 64 * u + 64] for g in range(3)]
                    else:
                        v = [lambda t: qkv[:, t, 2048 + 64 * u:2048 + 64 * u + 64]]
                    P, PT, slots = big_P, big_PT, 4
                if what == "scores":
                    if kind == "dsw":
                        if u >= 1:
                            pe.wait_ge(ttr_done, gu)
                        for g in range(3):
                            pe.matmul(ps23[:, S * g:S * g + S], q[g][:, 128:256], k[g][:, :], start=True, stop=True)
                        for g in range(3):
                            mm = pe.matmul(ps7[:, 128 * g:128 * g + 128], q[g][:, 0:128], k[g][:, 0:128], start=True, stop=True)
                    else:
                        if u >= 2:
                            pe.wait_ge(ttr_done, gu - 1)
                        o = ps23[:, 512 * (u % 2):512 * (u % 2) + 384]
                        pe.matmul(o[:, 0:S], q[0][:, 128:256], k[0][:, :], start=True, stop=True)
                        mm = pe.matmul(o[:, S:384], q[0][:, 0:128], k[0][:, 0:128], start=True, stop=True)
                    mm.then_inc(s_ready, 1)
                if what == "transposes":
                    pe.wait_ge(p_ready, gu + 1)
                    for g in range(parts):
                        c = PCH0[ph] + parts * u + g
                        if g >= 2:
                            pe.wait_ge((pt_a, pt_d)[c % 2], c // 2)
                        at = (S * g, S * g + 128, S * parts + 128 * g)
                        for i in range(3):
                            mm = pe.transpose(tr_bank[c % 2][:, 128 * i:128 * i + 128],
                                              P[:, u % 2, at[i]:at[i] + 128], ident[:, :])
                        mm.then_inc(t_ready, 1)
                if what == "output":
                    if u % 4 == 0 and gu:
                        pe.wait_ge(o_free, gu // 4)
                    c = PCH0[ph] + parts * u
                    for g in range(min(parts, 2)):
                        last = c + g + (2 if g + 2 < parts else 0)
                        pe.wait_ge((pt_a, pt_d)[last % 2], last // 2 + 1)
                    sl = lambda g: PT[:, (c - PCH0[ph] + g) % slots, :]
                    at = 128 * (u % 4)
                    for g in range(parts):
                        pe.matmul(ps6[:, at + 64:at + 128], sl(g)[:, 0:128], v[g](0), start=g == 0, stop=False)
                        pe.matmul(ps6[:, at + 64:at + 128], sl(g)[:, 128:256], v[g](1), start=False, stop=g == parts - 1)
                    for g in range(parts):
                        mm = pe.matmul(ps6[:, at:at + 64], sl(g)[:, 256:384], v[g](0), start=g == 0, stop=g == parts - 1)
                    if u % 4 == 3:
                        mm.then_inc(o_ready, 1)

            def stage_pair(ph, p):
                parts = 3 if ph == 2 else 1
                for g in range(parts):
                    for c in range(2):
                        if g:
                            s = STG0[ph] + 2 * parts * p + 2 * (g - 1) + c
                            pe.wait_ge((stg_a, stg_d)[c], s // 2 + 1)
                        c0 = 512 * (3 * c + g) + 128 * p if ph == 2 else 1024 * c + 128 * p
                        for t in range(2):
                            mm = pe.transpose(tr_bank[c][:, 128 * t:128 * t + 128],
                                              qkv[:, t, c0:c0 + 128], ident[:, :])
                        mm.then_inc(stg_ps, 1)
                s = STG0[ph] + 2 * parts * (p + 1)
                pe.wait_ge(stg_a, s // 2)
                pe.wait_ge(stg_d, s // 2)

            def attention(ph, units):
                if ph >= 2:
                    stage_pair(ph, 0)
                unit(ph, 0, "scores")
                for u in range(units):
                    if u + 1 < units:
                        if ph >= 2 and (u + 1) % 2 == 0:
                            stage_pair(ph, (u + 1) // 2)
                        unit(ph, u + 1, "scores")
                    unit(ph, u, "transposes")
                    unit(ph, u, "output")

            def nsa(l):
                s0 = STG0[l] + 2
                for c in range(6):
                    if c >= 2:
                        pe.wait_ge((stg_a, stg_d)[c % 2], (s0 + c) // 2)
                    if c == 2:
                        pe.wait_ge(k_dup_done, l + 1)
                    for q in range(4 if c < 4 else 2):
                        i, t = q // 2, q % 2
                        if c < 2:
                            src = proj[:, t, COL["nq"] + 128 * (2 * c + i):COL["nq"] + 128 * (2 * c + i) + 128]
                        elif c < 4:
                            src = k_dup[:, c - 2, t, i, :]
                        else:
                            src = proj[:, t, COL[("nks", "nkw")[c - 4]]:COL[("nks", "nkw")[c - 4]] + 128]
                        mm = pe.transpose(tr_bank[c % 2][:, 128 * q:128 * q + 128], src, ident[:, :])
                    mm.then_inc(stg_ps, 1)
                pe.wait_ge(stg_a, (s0 + 6) // 2)
                pe.wait_ge(stg_d, (s0 + 6) // 2)
                pe.wait_ge(cmp_blk, 2 * l + 2)
                for v in range(2):
                    for m in range(16):
                        mm = pe.matmul(ps23[0:32, 512 * v:512 * v + 64], blk[:, v, m, :], cw[:, v, m, :], start=m == 0, stop=m == 15)
                mm.then_inc(cmp_raw, 1)
                pe.wait_ge(cmp_tok, l + 1)
                pe.transpose(ps23[:, 0:32], k_c2[0:32].rearrange("p c n -> p (c n)"), ident[0:32, 0:32])
                pe.matmul(ps23[:, 512:576], rep[:, :], v_c[0:32], start=True, stop=True).then_inc(cmp_kv, 1)
                pe.wait_ge(cmp_kv_used, l + 1)
                for t in range(TT):
                    for p in range(4):
                        mm = pe.matmul(ps7[:, 128 * t + 32 * p:128 * t + 32 * p + 32],
                                       nT[:, p, 128 * t:128 * t + 128],
                                       k_bd.rearrange("p g n -> p (g n)"), start=True, stop=True)
                mm.then_inc(cmp_s, 1)
                pe.wait_ge(cmp_p, l + 1)
                for t in range(TT):
                    mm = pe.transpose(ps4[:, 128 * t:128 * t + 128], cmp_L[:, 128 * t:128 * t + 128], ident[:, :])
                mm.then_inc(cmp_t, 1)
                pe.wait_ge(cmp_pt, l + 1)
                for t in range(TT):
                    mm = pe.matmul(ps23[:, 512 * t:512 * t + 512], cmp_PT[:, 128 * t:128 * t + 128],
                                   v_bd.rearrange("p h n -> p (h n)"), start=True, stop=True)
                mm.then_inc(cmp_o, 1)
                pe.wait_ge(cmp_o_used, l + 1)
                pe.wait_ge(ro_used, l + 1)
                attention(l, 16)

            def lru(l):
                pe.wait_ge(lru_xc, 2 * l + 2)
                for i in range(2):
                    for c in range(2):
                        mm = pe.matmul(ps23[:, 512 * i + S * c:512 * i + S * c + S], gate_w[:, l, i, c, :],
                                       lru_w[:, 0, c, :], start=True, stop=True)
                mm.then_inc(lru_z, 1)

            pe.wait_ge(consts_in, 16 * 9)
            pe.wait_ge(small_in, SMALL)
            pe.wait_ge(hot_in, 16)
            pe.wait_ge(relb_in, 16)
            pe.wait_ge(relb_one, 1)
            for k in range(4):
                cols = slice(8 * k, 8 * k + 8) if k < 3 else slice(0, 16)
                o = (ps23[:, 0:512], ps23[:, 512:1024], ps6, ps7)[k]
                mm = pe.matmul(o[0:8 if k < 3 else 16, 0:384], relb[:, cols], hot[0:33, k, :], start=True, stop=True)
            mm.then_inc(vec_ps, 1)
            for l in range(LAYERS):
                transpose_acts(2 * l, x, KD)
                gemms(f"in{l}")
                retention(l)
                nsa(l)
                lru(l)
                transpose_acts(2 * l + 1, y, 6)
                gemms(f"out{l}")
            transpose_acts(DSW_U, y, KD)
            gemms("dsw")
            pe.wait_ge(qk_norm, 6)
            attention(2, DSW_HEADS)
            transpose_acts(DSW_Y, y, 4)
            gemms("dswo")
            transpose_acts(FFN0_U, y, KD)
            gemms("up0")
            pe.wait_ge(hl_done, 16)
            gemms("down0")
            transpose_acts(MOBA_U, y, KD)
            gemms("moba")
            pe.wait_ge(qk_norm, 10)
            attention(3, MOBA_HEADS)
            transpose_acts(MOBA_Y, y, KD)
            gemms("mobao")
            transpose_acts(FFN1_U, y, KD)
            gemms("up1")
            pe.wait_ge(hl_done, 32)
            gemms("down1")

        @block.scalar
        def _(act):
            def split_hi(c):
                b, j = CHUNKS[c]
                n = BLOCKS[b]["n"]
                act.wait_ge(w_arrived[c % RAW], 16 * (c // RAW + 1))
                if b >= AHEAD:
                    act.wait_ge(acc_ready, 2 * (b - AHEAD) + 2)
                act.activation(w_hi[:, b % AHEAD, 4 * j:4 * j + 4, 0:n], w_raw[:, c % RAW, :, 0:n], ACT.Copy).then_inc(w_hi_done, 1)

            def hidden_hi(g):
                act.wait_ge(h_done, g + 1)
                k = (2 * (g % 16))
                act.activation(h_hi[:, k:k + 2, :].rearrange("p k n -> p (k n)"), y[:, 1, 512 * (g % 2):512 * (g % 2) + 512], ACT.Copy).then_inc(hh_done, 1)

            def take(b, half):
                d = BLOCKS[b]
                n = d["n"]
                if not d["last"] or d["use"] in ("deepnorm", "residual"):
                    return
                act.wait_ge(acc_ready, 2 * b + half + 1)
                if d["use"] == "proj":
                    dst = proj if d["name"].startswith("in") else qkv
                    if dst is proj and d["c0"] == COL["nq"]:
                        act.activation(dst[:, half, d["c0"]:d["c0"] + n].rearrange("p (j g d) -> p g j d", j=4, g=2),
                                       ps[half].rearrange("p (g j d) -> p g j d", j=4, g=2), ACT.Copy).then_inc(acc_free[half], 1)
                    else:
                        act.activation(dst[:, half, d["c0"]:d["c0"] + n], ps[half][:, 0:n], ACT.Copy).then_inc(acc_free[half], 1)
                if d["use"] == "qk":
                    i = b - FIRST["dsw"] if d["name"] == "dsw" else 6 + b - FIRST["moba"]
                    if i:
                        act.wait_ge(qk_norm, i)
                    act.activation(qkv[:, half, d["c0"]:d["c0"] + n], ps[half][:, :], ACT.Copy)
                    act.activation(sq[:, half, :], ps[half][:, :], ACT.Square).then_inc(acc_free[half], 1)
                if d["use"] == "lru":
                    act.activation(lru_T[:, 2 * half:2 * half + 2, :].rearrange("p c n -> p (c n)"), ps[half][:, :], ACT.Copy).then_inc(acc_free[half], 1)
                if d["use"] == "relu2":
                    l = int(d["name"][-1])
                    g = HIDDEN0[l] + 2 * (b - FIRST[d["name"]]) + half
                    if g >= 2:
                        act.wait_ge(h_done, g - 1)
                    act.activation(y[:, 0, 512 * (g % 2):512 * (g % 2) + 512], ps[half][:, :], ACT.Relu).then_inc(acc_free[half], 1)

            def after_block(b):
                nxt = list(range(CHUNK0[b + AHEAD], CHUNK0[b + AHEAD + 1])) if b + AHEAD < NB else []
                for half in range(2):
                    take(b, half)
                    if half < len(nxt):
                        split_hi(nxt[half])
                    if BLOCKS[b]["use"] == "relu2":
                        l = int(BLOCKS[b]["name"][-1])
                        hidden_hi(HIDDEN0[l] + 2 * (b - FIRST[BLOCKS[b]["name"]]) + half)

            def gemms(name):
                for b in blocks(name):
                    after_block(b)

            def acts_hi(a, kts, gain=None):
                if a:
                    act.wait_ge(acc_ready, 2 * last_block[USED_BY[a - 1]] + 2)
                for i in range(kts // 2):
                    act.wait_ge(at_ps, TRANS0[a] + i + 1)
                    if gain is None:
                        act.activation(act_hi[:, 2 * i:2 * i + 2, :].rearrange("p k n -> p (k n)"), tr_bank[i % 2][:, :], ACT.Copy).then_inc(at_hi, 1)
                    else:
                        for k in range(2):
                            ins = act.activation(act_hi[:, 2 * i + k, :], tr_bank[i % 2][:, S * k:S * k + S], ACT.Copy,
                                                 scale=norm_g[:, gain, 2 * i + k:2 * i + k + 1])
                        ins.then_inc(at_hi, 1)

            def retention(l):
                act.wait_ge(stg_ps, STG0[l] + 1)
                act.activation(ret_T[:, 0:2, :].rearrange("p c n -> p (c n)"), ps4[:, :], ACT.Copy).then_inc(stg_a, 1)
                act.activation(y[:, :, 0:256], proj[:, :, COL["rg"]:COL["rg"] + 256], ACT.Tanh, scale=0.5)
                act.activation(y[:, :, 256:768], proj[:, :, COL["ng"]:COL["ng"] + 512], ACT.Tanh, scale=0.5)
                act.activation(gate_c[:, :, :], proj[:, :, COL["ngl"]:COL["ngl"] + 24], ACT.Tanh, scale=0.5).then_inc(tanh_done, 1)

            def units(ph, n):
                kind = ("nsa", "nsa", "dsw", "moba")[ph]
                parts = 3 if kind == "dsw" else 1
                P, PT, slots = (nsa_P, nsa_PT, 2) if kind == "nsa" else (big_P, big_PT, 4)

                def staged(p):
                    for g in range(parts):
                        s = STG0[ph] + 2 * parts * p + 2 * g
                        act.wait_ge(stg_ps, s + 1)
                        act.activation(stage[:, p % 2, 2 * g, :], ps4[:, 0:S], ACT.Copy,
                                       scale=qk_gain[:, ph - 2:ph - 1]).then_inc(stg_a, 1)

                if ph >= 2:
                    staged(0)
                for u in range(n):
                    if ph >= 2 and (u + 1) % 2 == 0 and u + 1 < n:
                        staged((u + 1) // 2)
                    gu = UNIT0[ph] + u
                    act.wait_ge(ttr_done, gu + 1)
                    if gu >= 16 and gu % 4 == 0:
                        act.wait_ge(o_free, gu // 4 - 3)
                    w1, w0 = S * parts, 128 * parts
                    dn = den[:, gu % 16, :]
                    act.activation(P[:, u % 2, 0:w1], P[:, u % 2, 0:w1], ACT.Exp, bias=ttr[:, u % 2, 1:2], scale=-1.0,
                                   accum_out=dn[:, 1:2])
                    act.activation(P[:, u % 2, w1:w1 + w0], P[:, u % 2, w1:w1 + w0], ACT.Exp, bias=ttr[:, u % 2, 0:1],
                                   scale=-1.0, accum_out=dn[:, 0:1]).then_inc(p_ready, 1)
                    for g in range(parts):
                        c = PCH0[ph] + parts * u + g
                        if c % 2 == 0:
                            act.wait_ge(t_ready, c + 1)
                            act.activation(PT[:, (c - PCH0[ph]) % slots, :], ps4[:, 0:384], ACT.Copy).then_inc(pt_a, 1)

            def nsa(l):
                for c in (0, 2, 4):
                    act.wait_ge(stg_ps, STG0[l] + 2 + c + 1)
                    at, k = ((0, 2), None, (4, 2), None, (8, 1))[c]
                    act.activation(nT[:, at:at + k, :].rearrange("p c n -> p (c n)"), ps4[:, 0:S * k], ACT.Copy,
                                   scale=HD ** -0.5 if c == 0 else 1.0).then_inc(stg_a, 1)
                act.wait_ge(cmp_l, l + 1)
                act.activation(cmp_L, cmp_L, ACT.Exp).then_inc(cmp_p, 1)
                act.wait_ge(cmp_t, l + 1)
                act.activation(cmp_PT, ps4[:, 0:256], ACT.Copy).then_inc(cmp_pt, 1)
                units(l, 16)

            def lru(l):
                act.wait_ge(lru_z, l + 1)
                for c in range(2):
                    act.activation(lru_w[:, 1, c, :], ps23[:, S * c:S * c + S], ACT.Tanh, bias=lru_hb[:, l, 0, c:c + 1], scale=0.5)
                for c in range(2):
                    act.activation(lru_w[:, 2, c, :], ps23[:, 512 + S * c:512 + S * c + S], ACT.Tanh, bias=lru_hb[:, l, 1, c:c + 1], scale=0.5)
                act.activation(lru_w[:, 6, :, :].rearrange("p c n -> p (c n)"), lru_T[:, 2:4, :].rearrange("p c n -> p (c n)"), ACT.Tanh, scale=0.5).then_inc(lru_th, 1)
                act.wait_ge(lru_nla, l + 1)
                nla = lru_w[:, 1, :, :].rearrange("p c n -> p (c n)")
                act.activation(lru_w[:, 3, :, :].rearrange("p c n -> p (c n)"), nla, ACT.Exp, scale=-1.0)
                act.activation(lru_w[:, 4, :, :].rearrange("p c n -> p (c n)"), nla, ACT.Tanh).then_inc(lru_at, 1)
                act.wait_ge(lru_v2, l + 1)
                v2 = lru_w[:, 4, :, :].rearrange("p c n -> p (c n)")
                act.activation(v2, v2, ACT.Sqrt).then_inc(lru_m, 1)
                act.wait_ge(lru_y, l + 1)
                act.wait_ge(acc_ready, 2 * last_block[f"in{l}"] + 2)
                act.activation(act_hi[:, 6:8, :].rearrange("p c n -> p (c n)"), lru_w[:, 5, :, :].rearrange("p c n -> p (c n)"), ACT.Copy).then_inc(at_hi, 1)

            def rms(i):
                if i == 0:
                    act.wait_ge(x_new, LAYERS)
                else:
                    for half in range(2):
                        act.wait_ge(acc_free[half], free_count(FIRST[("", "up0", "moba", "up1")[i]]))
                for t in range(TT):
                    ins = act.activation(y[:, t, :], x[:, t, :], ACT.Square, accum_out=st[:, 0, t:t + 1])
                ins.then_inc(ssq_done, 1)
                act.wait_ge(rstd_done, i + 1)
                for t in range(TT):
                    ins = act.activation(y[:, t, :], x[:, t, :], ACT.Copy, scale=st[:, 1, t:t + 1])
                ins.then_inc(src_ready, 1)

            act.wait_ge(small_in, SMALL)
            act.wait_ge(vec_ps, 1)
            for k in range(4):
                n = 8 if k < 3 else 16
                o = (ps23[:, 0:512], ps23[:, 512:1024], ps6, ps7)[k]
                ins = act.activation(vec[0:n, k, :], o[0:n, 0:384], ACT.Copy)
            ins.then_inc(vec_sb, 1)
            act.wait_ge(vec_out, 32)
            act.wait_ge(lam_abs, 1)
            act.activation(lam_exp[:, :], lam_exp[:, :], ACT.Exp, scale=-1.0).then_inc(lam_e, 1)
            for c in range(CHUNK0[AHEAD]):
                split_hi(c)
            for l in range(LAYERS):
                acts_hi(2 * l, KD)
                gemms(f"in{l}")
                retention(l)
                nsa(l)
                lru(l)
                acts_hi(2 * l + 1, 6)
                gemms(f"out{l}")
            rms(0)
            acts_hi(DSW_U, KD, gain=0)
            gemms("dsw")
            units(2, DSW_HEADS)
            acts_hi(DSW_Y, 4)
            gemms("dswo")
            rms(1)
            acts_hi(FFN0_U, KD, gain=2)
            gemms("up0")
            gemms("down0")
            rms(2)
            acts_hi(MOBA_U, KD, gain=1)
            gemms("moba")
            units(3, MOBA_HEADS)
            acts_hi(MOBA_Y, KD)
            gemms("mobao")
            rms(3)
            acts_hi(FFN1_U, KD, gain=3)
            gemms("up1")
            gemms("down1")

        @block.vector
        def _(dve):
            steps = [0]

            def done(ins):
                steps[0] += 1
                ins.then_inc(dve_step, 1)
                dve.wait_ge(dve_step, steps[0])

            def spread(ap, dims):
                return bass.AP(ap.tensor, ap.offset, [ap.ap[0], *[list(d) for d in dims]])

            def split_lo(c):
                b, j = CHUNKS[c]
                n = BLOCKS[b]["n"]
                dve.wait_ge(w_hi_done, c + 1)
                hi = w_hi[:, b % AHEAD, 4 * j:4 * j + 4, 0:n]
                lo = w_lo[:, b % AHEAD, 4 * j:4 * j + 4, 0:n]
                dve.tensor_tensor(lo, w_raw[:, c % RAW, :, 0:n], hi.bitcast(F), ALU.subtract).then_inc(w_lo_done, 1)

            def rsqrt(v, scale, eps, o, finish=None):
                n = v.shape[-1]
                m, a, c = st[:, 2, 0:n], st[:, 3, 0:n], st[:, 4, 0:n]
                done(dve.tensor_scalar(m, v, scale, eps, ALU.mult, ALU.add))
                done(dve.tensor_scalar(a.bitcast(I32), m.bitcast(I32), 1, None, ALU.logical_shift_right))
                done(dve.tensor_scalar(o.bitcast(I32), a.bitcast(I32), -1.0, float(0x5F3759DF), ALU.mult, ALU.add))
                for i in range(3):
                    done(dve.tensor_tensor(a, o, o, ALU.mult))
                    done(dve.scalar_tensor_tensor(out=c, in0=a, scalar=-0.5, in1=m, op0=ALU.mult, op1=ALU.mult))
                    (finish if finish and i == 2 else done)(dve.scalar_tensor_tensor(out=o, in0=c, scalar=1.5, in1=o, op0=ALU.add, op1=ALU.mult))

            def take(b, half):
                d = BLOCKS[b]
                n = d["n"]
                if not d["last"]:
                    return
                ready = free_count(b) + 1
                if d["use"] in ("deepnorm", "residual"):
                    dve.wait_ge(acc_ready, 2 * b + half + 1)
                    r = x[:, half, d["c0"]:d["c0"] + n]
                    dve.scalar_tensor_tensor(out=r, in0=r, scalar=ALPHA if d["use"] == "deepnorm" else 1.0,
                                             in1=ps[half][:, 0:n], op0=ALU.mult, op1=ALU.add).then_inc(acc_free[half], 1)
                if d["use"] == "qk" and half == 1:
                    dve.wait_ge(acc_free[0], ready)
                    dve.wait_ge(acc_free[1], ready)
                    done(dve.tensor_reduce(out=st[:, 5, 0:16], in_=sq.rearrange("p t (h d) -> p (t h) d", d=HD), axis=AX, op=ALU.add))
                    rsqrt(st[:, 5, 0:16], 1.0 / HD, 1e-6, st[:, 6, 0:16])
                    v = qkv[:, :, d["c0"]:d["c0"] + 512].rearrange("p t (h d) -> p t h d", d=HD)
                    dve.tensor_tensor(v, v, spread(st[:, 6, 0:1], [(8, 2), (1, 8), (0, HD)]), ALU.mult).then_inc(qk_norm, 1)
                if d["use"] == "relu2":
                    l = int(d["name"][-1])
                    g = HIDDEN0[l] + 2 * (b - FIRST[d["name"]]) + half
                    dve.wait_ge(acc_free[half], ready)
                    r = y[:, 0, 512 * (g % 2):512 * (g % 2) + 512]
                    dve.tensor_tensor(y[:, 1, 512 * (g % 2):512 * (g % 2) + 512], r, r, ALU.mult).then_inc(h_done, 1)

            def hidden_lo(g):
                k = 2 * (g % 16)
                dve.wait_ge(hh_done, g + 1)
                flat = "p k n -> p (k n)"
                dve.tensor_tensor(h_lo[:, k:k + 2, :].rearrange(flat), y[:, 1, 512 * (g % 2):512 * (g % 2) + 512],
                                  h_hi[:, k:k + 2, :].rearrange(flat).bitcast(F), ALU.subtract).then_inc(hl_done, 1)

            def after_block(b):
                nxt = list(range(CHUNK0[b + AHEAD], CHUNK0[b + AHEAD + 1])) if b + AHEAD < NB else []
                for half in range(2):
                    take(b, half)
                    if half < len(nxt):
                        split_lo(nxt[half])
                    if BLOCKS[b]["use"] == "relu2":
                        l = int(BLOCKS[b]["name"][-1])
                        hidden_lo(HIDDEN0[l] + 2 * (b - FIRST[BLOCKS[b]["name"]]) + half)

            def gemms(name):
                for b in blocks(name):
                    after_block(b)

            def acts_lo(a, kts, gain=None):
                for i in range(kts // 2):
                    dve.wait_ge(at_hi, ACT0[a] + LRU_CHUNK[a] + i + 1)
                    if gain is None:
                        hi = act_hi[:, 2 * i:2 * i + 2, :].rearrange("p k n -> p (k n)").bitcast(F)
                        lo = act_lo[:, 2 * i:2 * i + 2, :].rearrange("p k n -> p (k n)")
                        dve.tensor_tensor(lo, tr_bank[i % 2][:, :], hi, ALU.subtract).then_inc(at_lo, 1)
                    else:
                        for k in (2 * i, 2 * i + 1):
                            ins = dve.scalar_tensor_tensor(
                                out=act_lo[:, k, :], in0=tr_bank[i % 2][:, S * (k % 2):S * (k % 2) + S],
                                scalar=norm_g[:, gain, k:k + 1], in1=act_hi[:, k, :].bitcast(F),
                                op0=ALU.mult, op1=ALU.subtract)
                        ins.then_inc(at_lo, 1)

            def rotate():
                half = HD // 2

                def part(v, c0, e):
                    base = v[:, :, c0 + half * e:c0 + half * e + 1]
                    return spread(base, [(v.ap[1][0], 2), (HD, 8), (1, half)])

                for e in range(2):
                    cos, sin = [spread(rope[:, i, 0, 0:1], [(half, 2), (0, 8), (1, half)]) for i in range(2)]
                    dve.tensor_tensor(part(rot, 0, e), part(proj, COL["rq"], e), cos, ALU.mult)
                    done(dve.tensor_tensor(part(rot_b, 0, e), part(proj, COL["rq"], 1 - e), sin, ALU.mult))
                for e in range(2):
                    ins = dve.tensor_tensor(part(rot, 0, e), part(rot, 0, e), part(rot_b, 0, e), (ALU.subtract, ALU.add)[e])
                ins.then_inc(rot_done, 1)

            def retention(l):
                rotate()
                dve.wait_ge(stg_ps, STG0[l] + 2)
                dve.tensor_copy(ret_T[:, 2:4, :].rearrange("p c n -> p (c n)"), ps5[:, :]).then_inc(stg_d, 1)
                for h in range(RET_HEADS):
                    dve.wait_ge(rs_ps, RET_HEADS * l + h + 1)
                    o = ps23[:, 512 * (h % 2):512 * (h % 2) + 384]
                    dve.tensor_tensor(ret_P[:, h, 0:S], o[:, 0:S], decay[:, h, :], ALU.mult)
                    dve.tensor_tensor(ret_P[:, h, S:384], o[:, S:384], decay[:, h, 0:128], ALU.mult).then_inc(rs_sb, 1)
                dve.wait_ge(tanh_done, l + 1)
                for c0, n, g0 in ((0, 256, COL["rg"]), (256, 512, COL["ng"])):
                    g = proj[:, :, g0:g0 + n]
                    dve.scalar_tensor_tensor(out=g, in0=y[:, :, c0:c0 + n], scalar=1.0, in1=g, op0=ALU.add, op1=ALU.mult)
                done(dve.tensor_scalar(gate_c[:, :, :], gate_c[:, :, :], 1.0, 0.25, ALU.add, ALU.mult))
                dve.wait_ge(ro_ps, l + 1)
                o = ps6.rearrange("p (h d) -> p h d", d=HD)
                cen = tmp_tok[:, 0:512].rearrange("p (h d) -> p h d", d=HD)
                squ = tmp_tok[:, 512:1024].rearrange("p (h d) -> p h d", d=HD)
                done(dve.tensor_reduce(out=st[:, 0, 0:8], in_=o, axis=AX, op=ALU.add))
                done(dve.tensor_scalar(st[:, 1, 0:8], st[:, 0, 0:8], 1.0 / HD, None, ALU.mult))
                done(dve.tensor_tensor(cen, o, spread(st[:, 1, 0:1], [(1, 8), (0, HD)]), ALU.subtract))
                done(dve.tensor_tensor(squ, cen, cen, ALU.mult))
                done(dve.tensor_reduce(out=st[:, 5, 0:8], in_=squ, axis=AX, op=ALU.add))
                rsqrt(st[:, 5, 0:8], 1.0 / HD, 1e-5, st[:, 6, 0:8])
                done(dve.tensor_scalar(st[:, 7, 0:8], st[:, 6, 0:8], 0.5, None, ALU.mult))
                done(dve.tensor_tensor(cen, cen, spread(st[:, 7, 0:1], [(1, 8), (0, HD)]), ALU.mult))
                dve.tensor_tensor(spread(y[:, 0, 0:1], [(HD, 4), (D, 2), (1, HD)]), cen.rearrange("p (h t) d -> p h t d", t=2),
                                  spread(proj[:, 0, COL["rg"]:COL["rg"] + 1], [(HD, 4), (2840, 2), (1, HD)]), ALU.mult).then_inc(ro_used, 1)

            def units(ph, n):
                kind = ("nsa", "nsa", "dsw", "moba")[ph]
                parts = 3 if kind == "dsw" else 1
                P, PT, slots = (nsa_P, nsa_PT, 2) if kind == "nsa" else (big_P, big_PT, 4)
                w1 = S * parts

                def staged(p):
                    for g in range(parts):
                        s = STG0[ph] + 2 * parts * p + 2 * g + 1
                        dve.wait_ge(stg_ps, s + 1)
                        dve.tensor_copy(stage[:, p % 2, 2 * g + 1, :], ps5[:, 0:S]).then_inc(stg_d, 1)

                def logits(u):
                    gu = UNIT0[ph] + u
                    dve.wait_ge(s_ready, gu + 1)
                    if u >= 2:
                        dve.wait_ge(t_ready, PCH0[ph] + parts * (u - 1))
                    if kind == "nsa":
                        m1, m0 = causal[:, :], causal[:, 128:256]
                    else:
                        bu = u + (DSW_HEADS if kind == "moba" else 0)
                        dve.wait_ge(bias_in[bu % 2], 16 * (bu // 2 + 1))
                        m1 = spread(bias_T[:, bu % 2, 255:256], [(S, parts), (-1, S)])
                        m0 = spread(bias_T[:, bu % 2, 127:128], [(S, parts), (-1, 128)])
                    if kind == "dsw":
                        s1, s0 = ps23[:, 0:w1].rearrange("p (g n) -> p g n", g=3), ps7[:, 0:384].rearrange("p (g n) -> p g n", g=3)
                        o0 = P[:, u % 2, w1:w1 + 384].rearrange("p (g n) -> p g n", g=3)
                    else:
                        s1, s0 = [ps23[:, 512 * (u % 2) + a:512 * (u % 2) + b] for a, b in ((0, S), (S, 384))]
                        o0 = P[:, u % 2, S:384]
                        if kind == "moba":
                            m1, m0 = spread(bias_T[:, bu % 2, 255:256], [(-1, S)]), spread(bias_T[:, bu % 2, 127:128], [(-1, 128)])
                    o1 = P[:, u % 2, 0:w1]
                    if kind == "dsw":
                        o1 = o1.rearrange("p (g n) -> p g n", g=3)
                    dve.tensor_tensor_reduce(out=o1, in0=s1, in1=m1, scale=-1.0, scalar=3.0e38,
                                             op0=ALU.add, op1=ALU.min, accum_out=ttr[:, u % 2, 1:2])
                    dve.tensor_tensor_reduce(out=o0, in0=s0, in1=m0, scale=-1.0, scalar=3.0e38,
                                             op0=ALU.add, op1=ALU.min, accum_out=ttr[:, u % 2, 0:1]).then_inc(ttr_done, 1)

                if ph >= 2:
                    staged(0)
                logits(0)
                for u in range(n):
                    gu = UNIT0[ph] + u
                    if u + 1 < n:
                        if ph >= 2 and (u + 1) % 2 == 0:
                            staged((u + 1) // 2)
                        logits(u + 1)
                    for g in range(parts):
                        c = PCH0[ph] + parts * u + g
                        if c % 2 == 1:
                            dve.wait_ge(t_ready, c + 1)
                            dve.tensor_copy(PT[:, (c - PCH0[ph]) % slots, :], ps5[:, 0:384]).then_inc(pt_d, 1)
                    if u % 4 == 3:
                        u0 = u - 3
                        dve.wait_ge(o_ready, gu // 4 + 1)
                        sums = den[:, (gu - 3) % 16:(gu - 3) % 16 + 4, :]
                        done(dve.reciprocal(rden[:, :, :], sums))
                        o = ps6.rearrange("p (h d) -> p h d", d=HD)
                        co = spread(rden[:, 0, 0:1], [(1, 8), (0, HD)])
                        if kind == "nsa":
                            br, h = u0 // 8, u0 % 8
                            gc = spread(gate_c[:, 0, 3 * h + 1 + br:3 * h + 2 + br], [(3, 4), (24, 2)])
                            done(dve.tensor_tensor(rden[:, :, :], rden[:, :, :], gc, ALU.mult))
                            part = tmp_tok[:, 0:512].rearrange("p (h d) -> p h d", d=HD)
                            dve.tensor_tensor(part, o, co, ALU.mult).then_inc(o_free, 1)
                            dve.wait_ge(o_free, gu // 4 + 1)
                            yv = spread(y[:, 0, 256 + HD * h:257 + HD * h], [(HD, 4), (D, 2), (1, HD)])
                            done(dve.tensor_tensor(yv, yv, part.rearrange("p (h t) d -> p h t d", t=2), ALU.add))
                        else:
                            yv = spread(y[:, 0, HD * u0:HD * u0 + 1], [(HD, 4), (D, 2), (1, HD)])
                            dve.tensor_tensor(yv, o.rearrange("p (h t) d -> p h t d", t=2),
                                              spread(rden[:, 0, 0:1], [(2, 4), (1, 2), (0, HD)]), ALU.mult).then_inc(o_free, 1)

            def nsa(l):
                if l == 0:
                    for v in range(2):
                        dve.memset(spread(blk[:, v, 0, 15:16], [(32, 16), (16, 2), (1, 1)]), 0.0)
                for c in (1, 3, 5):
                    dve.wait_ge(stg_ps, STG0[l] + 2 + c + 1)
                    at, k = (None, (2, 2), None, (6, 2), None, (9, 1))[c]
                    dve.tensor_scalar(nT[:, at:at + k, :].rearrange("p c n -> p (c n)"), ps5[:, 0:S * k],
                                      HD ** -0.5 if c == 1 else 1.0, None, ALU.mult).then_inc(stg_d, 1)
                dve.wait_ge(stg_a, (STG0[l] + 8) // 2)
                dve.wait_ge(stg_d, (STG0[l] + 8) // 2)
                dve.wait_ge(cw_in, 16 * 6 * (l + 1))
                for v in range(2):
                    for e in range(2):
                        r = slice(64 * e, 64 * e + 64)
                        ins = dve.tensor_tensor(
                            spread(blk[r, v, 0, 0:1], [(32, 16), (16, 2), (1, N_CMP)]),
                            spread(nT[r, 4 + 2 * v, e:e + 1], [(2, 16), (S, 2), (16, N_CMP)]),
                            spread(cmp_pos[r, v, 0:1], [(1, 16), (0, 2), (0, N_CMP)]), ALU.add)
                    ins.then_inc(cmp_blk, 1)
                dve.wait_ge(cmp_raw, l + 1)
                dve.tensor_copy(k_c2[0:32], spread(ps23[0:32, 0:1], [(0, 2), (1, HD)]))
                dve.tensor_copy(v_c[0:32], ps23[0:32, 512:576]).then_inc(cmp_tok, 1)
                dve.wait_ge(cmp_kv, l + 1)
                dve.tensor_tensor(k_bd, spread(ps23[:, 0:1], [(16, 2), (1, 16)]),
                                  spread(half_of[:, 0:1], [(1, 2), (0, 16)]), ALU.mult)
                dve.tensor_tensor(v_bd, spread(ps23[:, 512:513], [(0, 8), (1, HD)]),
                                  spread(head_of[:, 0:1], [(1, 8), (0, HD)]), ALU.mult).then_inc(cmp_kv_used, 1)
                dve.wait_ge(cmp_s, l + 1)
                lv = cmp_L.rearrange("p (t h n) -> p t h n", t=2, h=8)
                rows = cmp_L.rearrange("p (r n) -> p r n", n=16)
                done(dve.tensor_tensor(lv, ps7[:, 0:256].rearrange("p (t h n) -> p t h n", t=2, h=8),
                                       spread(cmp_mask[:, 0, 0:1], [(16, 2), (0, 8), (1, 16)]), ALU.add))
                done(dve.tensor_reduce(out=st[:, 0, 0:16], in_=rows, axis=AX, op=ALU.max))
                dve.tensor_tensor(rows, rows, spread(st[:, 0, 0:1], [(1, 16), (0, 16)]), ALU.subtract).then_inc(cmp_l, 1)
                dve.wait_ge(cmp_p, l + 1)
                done(dve.tensor_reduce(out=st[:, 1, 0:16], in_=rows, axis=AX, op=ALU.add))
                done(dve.reciprocal(st[:, 2, 0:16], st[:, 1, 0:16]))
                co = st[:, 3, 0:16].rearrange("p (t h) -> p t h", t=2)
                done(dve.tensor_tensor(spread(st[:, 3, 0:1], [(8, 2), (1, 4), (4, 2)]),
                                       spread(st[:, 2, 0:1], [(8, 2), (2, 4), (1, 2)]),
                                       spread(gate_c[:, 0, 0:1], [(24, 2), (3, 4), (12, 2)]), ALU.mult))
                done(dve.tensor_tensor(co, co, spread(cmp_any[:, 0:1], [(1, 2), (0, 8)]), ALU.mult))
                dve.wait_ge(cmp_o, l + 1)
                ins = dve.tensor_tensor(spread(y[:, 0, 256:257], [(D, 2), (HD, 8), (1, HD)]),
                                        spread(ps23[:, 0:1], [(512, 2), (HD, 8), (1, HD)]),
                                        spread(st[:, 3, 0:1], [(8, 2), (1, 8), (0, HD)]), ALU.mult)
                ins.then_inc(cmp_o_used, 1)
                dve.wait_ge(cmp_o_used, l + 1)
                units(l, 16)
                g = y[:, :, 256:768]
                dve.tensor_tensor(g, g, proj[:, :, COL["ng"]:COL["ng"] + 512], ALU.mult).then_inc(y_ready, 1)

            def lru(l):
                flat = "p c n -> p (c n)"
                xc, th_r, th_i, a, t, res, th_g = [lru_w[:, i] for i in range(7)]
                for c in range(2):
                    w = conv_w[:, l, c]
                    xv = lru_T[:, c, :]
                    done(dve.tensor_scalar(xc[:, c, :], xv, w[:, 3:4], lru_v[:, l, 0, c:c + 1], ALU.mult, ALU.add))
                    for s in (1, 2, 3):
                        ins = dve.scalar_tensor_tensor(out=xc[:, c, s:S], in0=xv[:, 0:S - s], scalar=w[:, 3 - s:4 - s],
                                                       in1=xc[:, c, s:S], op0=ALU.mult, op1=ALU.add)
                        if s < 3:
                            done(ins)
                    ins.then_inc(lru_xc, 1)
                dve.wait_ge(lru_th, l + 1)
                for c in range(2):
                    ins = dve.tensor_scalar(th_r[:, c, :], th_r[:, c, :], 1.0, lru_sp[:, 2 * l + c:2 * l + c + 1], ALU.add, ALU.mult)
                ins.then_inc(lru_nla, 1)
                xf = xc.rearrange(flat)
                ti = th_i.rearrange(flat)
                tg = th_g.rearrange(flat)
                dve.scalar_tensor_tensor(out=ti, in0=ti, scalar=1.0, in1=xf, op0=ALU.add, op1=ALU.mult)
                done(dve.scalar_tensor_tensor(out=tg, in0=tg, scalar=1.0, in1=lru_T[:, 2:4, :].rearrange(flat), op0=ALU.add, op1=ALU.mult))
                dve.wait_ge(lru_at, l + 1)
                af, tf, rf = a.rearrange(flat), t.rearrange(flat), res.rearrange(flat)
                done(dve.tensor_tensor(rf, af, af, ALU.mult))
                dve.scalar_tensor_tensor(out=tf, in0=rf, scalar=1.0, in1=tf, op0=ALU.add, op1=ALU.mult).then_inc(lru_v2, 1)
                dve.wait_ge(lru_m, l + 1)
                done(dve.scalar_tensor_tensor(out=tf, in0=tf, scalar=0.5, in1=ti, op0=ALU.mult, op1=ALU.mult))
                for c in range(2):
                    done(dve.tensor_tensor_scan(res[:, c, :], a[:, c, :], t[:, c, :], 0.0, ALU.mult, ALU.add))
                dve.scalar_tensor_tensor(out=rf, in0=rf, scalar=0.5, in1=tg, op0=ALU.mult, op1=ALU.mult).then_inc(lru_y, 1)
                dve.wait_ge(at_hi, ACT0[2 * l + 1] + 1)
                dve.wait_ge(lru_y, l + 1)
                dve.tensor_tensor(act_lo[:, 6:8, :].rearrange(flat), rf, act_hi[:, 6:8, :].rearrange(flat).bitcast(F), ALU.subtract).then_inc(at_lo, 1)

            def layer_norm(l):
                for half in range(2):
                    dve.wait_ge(acc_free[half], free_count(last_block[f"out{l}"]) + 1)
                for t in range(TT):
                    for i in range(2):
                        ins = dve.bn_stats(bn[:, t, 6 * i:6 * i + 6], x[:, t, 512 * i:512 * i + 512])
                done(ins)
                for t in range(TT):
                    ins = dve.bn_aggr(mv[:, t, :], bn[:, t, :])
                done(ins)
                rsqrt(mv[:, :, 1], 1.0, 1e-5, st[:, 1, 0:2])
                for t in range(TT):
                    ins = dve.tensor_scalar(x[:, t, :], x[:, t, :], mv[:, t, 0:1], st[:, 1, t:t + 1], ALU.subtract, ALU.mult)
                done(ins)
                dve.wait_ge(ln_in, 32 * (l + 1))
                done(dve.tensor_tensor(x[:, :, :], x[:, :, :], spread(ln_v[:, 0, 0:1], [(0, 2), (1, D)]), ALU.mult))
                dve.tensor_tensor(x[:, :, :], x[:, :, :], spread(ln_v[:, 1, 0:1], [(0, 2), (1, D)]), ALU.add).then_inc(x_new, 1)

            def rms(i):
                dve.wait_ge(ssq_done, i + 1)
                rsqrt(st[:, 0, 0:2], 1.0 / D, 1e-6, st[:, 1, 0:2], lambda ins: ins.then_inc(rstd_done, 1))

            dve.memset(st[:, :, :], 0.0)
            dve.wait_ge(small_in, SMALL)
            done(dve.tensor_tensor(qk_gain[:, :], qk_g[:, 0:4:2], qk_g[:, 1:4:2], ALU.mult))
            done(dve.tensor_scalar(qk_gain[:, :], qk_gain[:, :], HD ** -0.5, None, ALU.mult))
            done(dve.tensor_scalar(lru_hb[:, :, :, :], lru_v[:, :, 1:3, :], 0.5, None, ALU.mult))
            lam = lru_v[:, :, 3, :]
            le = lam_exp[:, :].rearrange("p (l c) -> p l c", l=LAYERS)
            dve.scalar_tensor_tensor(out=le, in0=lam, scalar=-1.0, in1=lam, op0=ALU.mult, op1=ALU.max).then_inc(lam_abs, 1)
            dve.wait_ge(lam_e, 1)
            e, s1, s2, pl = lam_exp[:, :], lam_p[:, 0], lam_p[:, 1], lam_p[:, 2]
            done(dve.tensor_scalar(s2, e, 2.0, None, ALU.add))
            done(dve.reciprocal(s1, s2))
            done(dve.tensor_tensor(s1, s1, e, ALU.mult))
            done(dve.tensor_tensor(s2, s1, s1, ALU.mult))
            done(dve.tensor_scalar(pl, s2, 1.0 / 15, None, ALU.mult))
            for k in (13, 11, 9, 7, 5, 3):
                done(dve.scalar_tensor_tensor(out=pl, in0=pl, scalar=1.0 / k, in1=s2, op0=ALU.add, op1=ALU.mult))
            done(dve.scalar_tensor_tensor(out=pl, in0=pl, scalar=1.0, in1=s1, op0=ALU.add, op1=ALU.mult))
            done(dve.tensor_scalar(lam_p[:, 3].rearrange("p (l c) -> p l c", l=LAYERS), lam, -1.0, 0.0, ALU.mult, ALU.max))
            done(dve.tensor_scalar(lam_p[:, 3], lam_p[:, 3], 4.0, None, ALU.mult))
            done(dve.scalar_tensor_tensor(out=lru_sp[:, :], in0=pl, scalar=8.0, in1=lam_p[:, 3], op0=ALU.mult, op1=ALU.add))
            dve.wait_ge(consts_in, 16 * 9)
            for c in range(CHUNK0[AHEAD]):
                split_lo(c)
            for l in range(LAYERS):
                acts_lo(2 * l, KD)
                gemms(f"in{l}")
                retention(l)
                nsa(l)
                lru(l)
                acts_lo(2 * l + 1, 6)
                gemms(f"out{l}")
                layer_norm(l)
            rms(0)
            acts_lo(DSW_U, KD, gain=0)
            gemms("dsw")
            units(2, DSW_HEADS)
            acts_lo(DSW_Y, 4)
            gemms("dswo")
            rms(1)
            acts_lo(FFN0_U, KD, gain=2)
            gemms("up0")
            gemms("down0")
            rms(2)
            acts_lo(MOBA_U, KD, gain=1)
            gemms("moba")
            units(3, MOBA_HEADS)
            acts_lo(MOBA_Y, KD)
            gemms("mobao")
            rms(3)
            acts_lo(FFN1_U, KD, gain=3)
            gemms("up1")
            gemms("down1")


def kernel(**inputs):
    import concourse.bacc as bacc
    from concourse.bass_utils import run_bass_kernel_spmd

    nc = bacc.Bacc("TRN2", target_bir_lowering=False, num_devices=1)
    arrays, dram = {}, {}
    for name, a in [(n, inputs[n]) for n in PARAMS] + list(shape_constants().items()):
        a = np.ascontiguousarray(a)
        arrays[f"in_{name}"] = a
        dram[name] = nc.dram_tensor(f"in_{name}", a.shape, mybir.dt.from_np(a.dtype), kind="ExternalInput").ap()
    out = nc.dram_tensor("out_0", (1, S, D), mybir.dt.float32, kind="ExternalOutput").ap()
    build(nc, dram, out)
    r = run_bass_kernel_spmd(nc, [arrays], core_ids=[0])
    return r.results[0]["out_0"]
```

```python
import math
from contextlib import ExitStack

import numpy as np

import concourse.bass as bass
from concourse import mybir

S = 256
TT = S // 128
D = 1024
KD = D // 128
HD = 64
LAYERS = 2
D_IN = 3352
D_FF = 4096
RET_HEADS, NSA_HEADS, NSA_GROUPS, DSW_GROUPS, DSW_HEADS, MOBA_HEADS = 4, 8, 2, 3, 8, 16
N_CMP = 15
ALPHA = (2.0 * LAYERS) ** 0.25
NEG = -1.0e30
COL = dict(rq=0, rk=256, rv=512, rg=768, nq=1024, nkc=1536, nvc=1664, nks=1792, nvs=1920,
           nkw=2048, nvw=2176, ng=2304, ngl=2816, lx=2840, lg=3096)

PARAMS = ["x", "w_in", "w_out", "ln_g", "ln_b", "nsa_cmp_pos", "nsa_cmp_w", "lru_conv_w", "lru_conv_b",
          "lru_w_a", "lru_b_a", "lru_w_x", "lru_b_x", "lru_lambda", "rel_bias_2", "norm_mix_2",
          "norm_ffn_2", "a_w_qkv_2", "a_q_gain_2", "a_k_gain_2", "a_w_o_2", "b_w_qkv_2", "b_q_gain_2",
          "b_k_gain_2", "b_w_o_2", "ffn_w1_2", "ffn_w2_2"]


def shape_constants():
    half = HD // 2
    inv = (1.0 / (10000.0 ** (np.arange(half, dtype=np.float32) / half))).astype(np.float32)
    ang = (np.arange(S, dtype=np.float32)[:, None] * inv[None, :]).astype(np.float32)
    rope = np.stack([np.cos(ang.astype(np.float64)), np.sin(ang.astype(np.float64))])
    rope = rope.reshape(2, TT, 128, half).transpose(2, 0, 1, 3)
    p, c = np.arange(128)[:, None], np.arange(S)[None, :]
    decay = np.zeros((128, RET_HEADS, S))
    for h in range(RET_HEADS):
        decay[:, h] = np.where(c >= p, (1.0 - 2.0 ** (-5.0 - h)) ** np.maximum(c - p, 0) * HD ** -0.5, 0.0)
    causal = np.where(c <= 128 + p, 0.0, NEG)
    tok = np.arange(S)
    seen = (np.arange(16)[None, :] * 16 + 31 <= tok[:, None]) & (np.arange(16)[None, :] < N_CMP)
    cmp_mask = np.where(seen, 0.0, NEG).reshape(TT, 128, 16).transpose(1, 0, 2)
    cmp_any = seen.any(1).reshape(TT, 128).T
    row = np.arange(128)
    head_of = (row // 16 % 2 * 4 + row // 32)[:, None] == np.arange(8)[None, :]
    rep = np.arange(32)[:, None] == (row % 32)[None, :]
    half_of = (np.arange(128)[:, None] // 64 == np.arange(2)[None, :])
    dist = np.arange(384) - 127
    n = np.maximum(dist, 1)
    large = 16 + (np.log(n / 16) / math.log(2048 / 16) * 16).astype(np.int64)
    bucket = np.where(dist < 16, np.maximum(dist, 0), np.minimum(large, 31))
    hot = np.zeros((33, 4, 384))
    for kind, ok in enumerate([(dist >= 0) & (dist <= 128), (dist >= 0) & (dist % 4 == 0),
                               (dist >= 0) & (dist % 16 == 0), dist >= 0]):
        hot[bucket, kind, np.arange(384)] = 1.0
        hot[32, kind] = np.where(ok, 0.0, NEG)
    f = lambda a: np.ascontiguousarray(a, dtype=np.float32)
    return {"c_rope": f(rope), "c_decay": f(decay), "c_causal": f(causal), "c_cmp_mask": f(cmp_mask),
            "c_cmp_any": f(cmp_any), "c_head_of": f(head_of), "c_half_of": f(half_of), "c_hot": f(hot),
            "c_ident": f(np.eye(128)), "c_rep": f(rep)}


def build(nc, dram, out):
    F = mybir.dt.float32
    FR = mybir.dt.float32r
    I32 = mybir.dt.int32
    ALU = mybir.AluOpType
    ACT = mybir.ActivationFunctionType
    AX = mybir.AxisListType.X

    BLOCKS = []
    FIRST = {}

    def add_blocks(name, w, row0, rows, col_list, form, use):
        FIRST.setdefault(name, len(BLOCKS))
        for c0, n in col_list:
            BLOCKS.append(dict(w=w, row0=row0, kts=rows // 128, c0=c0, n=n, form=form, use=use,
                               first=True, last=True, act0=0, name=name))

    IN_COLS = [(COL["nq"], 512), (COL["nkc"], 512), (2560, COL["lx"] - 2560), (COL["nkw"], 512),
               (COL["rq"], 512), (COL["rv"], 512)]
    for l in range(LAYERS):
        w = dram["w_in"][l]
        add_blocks(f"in{l}", w, 0, D, IN_COLS, "tok", "proj")
        add_blocks(f"in{l}", w, 0, D, [(COL["lx"], 512)], "feat", "lru")
        add_blocks(f"out{l}", dram["w_out"][l], 0, D, [(0, 512), (512, 512)], "tok", "deepnorm")

    def add_ffn(l):
        add_blocks(f"up{l}", dram["ffn_w1_2"][l], 0, D, [(512 * i, 512) for i in range(8)], "feat", "relu2")
        FIRST[f"down{l}"] = len(BLOCKS)
        for c in range(2):
            for k in range(4):
                BLOCKS.append(dict(w=dram["ffn_w2_2"][l], row0=k * D, kts=8, c0=512 * c, n=512, form="tok",
                                   use="residual", first=k == 0, last=k == 3, act0=8 * k, name=f"down{l}"))

    add_blocks("dsw", dram["a_w_qkv_2"][0], 0, D, [(512 * i, 512) for i in range(6)], "tok", "qk")
    add_blocks("dsw", dram["a_w_qkv_2"][0], 0, D, [(512 * i, 512) for i in range(6, 9)], "tok", "proj")
    add_blocks("dswo", dram["a_w_o_2"][0], 0, 512, [(0, 512), (512, 512)], "tok", "residual")
    add_ffn(0)
    add_blocks("moba", dram["b_w_qkv_2"][0], 0, D, [(512 * i, 512) for i in range(4)], "tok", "qk")
    add_blocks("moba", dram["b_w_qkv_2"][0], 0, D, [(512 * i, 512) for i in range(4, 6)], "tok", "proj")
    add_blocks("mobao", dram["b_w_o_2"][0], 0, D, [(0, 512), (512, 512)], "tok", "residual")
    add_ffn(1)
    NB = len(BLOCKS)
    CHUNKS = [(b, j) for b in range(NB) for j in range(BLOCKS[b]["kts"] // 4)]
    CHUNK0 = [sum(x["kts"] // 4 for x in BLOCKS[:b]) for b in range(NB + 1)]
    RAW = 3
    AHEAD = 2

    ACTS = [8, 8, 8, 8, 8, 4, 8, 8, 8, 8]
    X0, Y0, X1, Y1, DSW_U, DSW_Y, FFN0_U, MOBA_U, MOBA_Y, FFN1_U = range(10)
    LRU_CHUNK = [0, 1, 0, 1, 0, 0, 0, 0, 0, 0]
    ACT0 = [sum(ACTS[:i]) // 2 for i in range(11)]

    TRANS0 = [sum(n // 2 - c for n, c in zip(ACTS[:i], LRU_CHUNK)) for i in range(10)]

    UNIT0 = [0, 16, 32, 40]
    PCH0 = [0, 16, 32, 56]
    STG0 = [0, 8, 16, 40]

    ctx = ExitStack()
    with ctx:
        def sb(name, shape, dt=F):
            return ctx.enter_context(nc.sbuf_tensor(name, shape, dt))

        def sem(name):
            return ctx.enter_context(nc.semaphore(name))

        x = sb("x_res", [128, TT, D])
        y = sb("y_tok", [128, TT, D])
        act_hi = sb("act_hi", [128, KD, S], FR)
        act_lo = sb("act_lo", [128, KD, S], FR)
        w_raw = sb("w_raw", [128, RAW, 4, 512])
        w_hi = sb("w_hi", [128, AHEAD, 8, 512], FR)
        w_lo = sb("w_lo", [128, AHEAD, 8, 512], FR)
        ident = sb("ident", [128, 128])
        rope = sb("rope", [128, 2, TT, HD // 2])
        decay = sb("decay", [128, RET_HEADS, S])
        causal = sb("causal", [128, S])
        cmp_mask = sb("cmp_mask", [128, TT, 16])
        cmp_any = sb("cmp_any", [128, TT])
        head_of = sb("head_of", [128, 8])
        half_of = sb("half_of", [128, 2])
        rep = sb("rep", [32, 128])
        norm_g = sb("norm_g", [128, 4, KD])
        qk_g = sb("qk_g", [128, 4])
        qk_gain = sb("qk_gain", [128, 2])
        conv_w = sb("conv_w", [128, LAYERS, 2, 4])
        lru_v = sb("lru_v", [128, LAYERS, 4, 2])
        lru_hb = sb("lru_hb", [128, LAYERS, 2, 2])
        lru_sp = sb("lru_sp", [128, LAYERS * 2])
        lam_exp = sb("lam_exp", [128, LAYERS * 2])
        lam_p = sb("lam_p", [128, 4, LAYERS * 2])
        bn = sb("bn", [128, TT, 12])
        mv = sb("mv", [128, TT, 2])
        gate_w = sb("gate_w", [128, LAYERS, 2, 2, 128])
        relb = sb("relb", [33, 24])
        st = sb("st", [128, 8, 16])
        cmp_w = sb("cmp_weights", [128, 16])
        ttr = sb("ttr_min", [128, 2, TT])
        den = sb("den", [128, 16, TT])
        rden = sb("rden", [128, 4, TT])
        gate_c = sb("gate_c", [128, TT, 24])
        AREA = 19008
        with nc.sbuf_tensor("area", [128, AREA], F) as area:
            pass
        hid = ctx.enter_context(nc.sbuf_tensor("hid", [128, 2, 32, S], FR))
        pad = sb("area_rest", [128, AREA - 16384])
        h_hi, h_lo = hid[:, 0], hid[:, 1]

        def cut(at, n, pattern=None, **sizes):
            v = area[:, at:at + n]
            return v.rearrange(pattern, **sizes) if pattern else v

        proj = cut(0, TT * 2840, "p (t n) -> p t n", t=TT)
        R = TT * 2840
        rot = cut(R, 1024, "p (t n) -> p t n", t=TT)
        rot_b = cut(R + 1024, 1024, "p (t n) -> p t n", t=TT)
        ret_T = cut(R + 2048, 1024, "p (c n) -> p c n", c=4)
        ret_P = cut(R + 3072, 1536, "p (h n) -> p h n", h=4)
        lru_w = cut(R, 3584, "p (k c n) -> p k c n", k=7, c=2)
        R += 4608
        nT = cut(R, 3072, "p (c n) -> p c n", c=12)
        R += 3072
        blk = cut(R, 1024, "p (v m n) -> p v m n", v=2, m=16)
        R += 1024
        cw = cut(R, 2048, "p (v m n) -> p v m n", v=2, m=16)
        R += 2048
        lru_T = cut(R, 1024, "p (c n) -> p c n", c=4)
        R += 1024
        nsa_P = cut(R, 768, "p (s n) -> p s n", s=2)
        R += 768
        k_dup = cut(R - 768, 1024, "p (v t g n) -> p v t g n", v=2, t=2, g=2)
        nsa_PT = cut(R, 768, "p (s n) -> p s n", s=2)
        assert R + 768 <= AREA
        BLK, CW, LRU_T = R - 4864, R - 3840, R - 1792
        v_bd = cut(BLK, 512, "p (h n) -> p h n", h=8)
        k_bd = cut(BLK + 512, 32, "p (g n) -> p g n", g=2)
        k_c2 = cut(BLK + 544, 128, "p (c n) -> p c n", c=2)
        v_c = cut(BLK + 672, 64)
        cmp_L = cut(BLK + 736, 256)
        tmp_tok = cut(CW, 1024)
        o_part = cut(CW + 1024, 512)
        cmp_PT = cut(CW + 1536, 256)
        cmp_pos = cut(LRU_T, 32, "p (v m) -> p v m", v=2)
        ln_v = cut(0, 2048, "p (v n) -> p v n", v=2)
        qkv = cut(0, 9216, "p (t n) -> p t n", t=TT)
        sq = cut(9216, 1024, "p (t n) -> p t n", t=TT)
        stage = cut(10240, 3072, "p (s c n) -> p s c n", s=2, c=6)
        big_P = cut(13312, 2304, "p (s n) -> p s n", s=2)
        big_PT = cut(15616, 1536, "p (s n) -> p s n", s=4)
        bias_T = cut(17152, 1536, "p (s n) -> p s n", s=2)
        hot = cut(TT * 2840 + 4608, 1536, "p (k n) -> p k n", k=4)
        vec = cut(TT * 2840 + 6144, 1536, "p (k n) -> p k n", k=4)

        ps = [ctx.enter_context(nc.psum_tensor(f"ps{i}", [128, 512], F)) for i in (0, 1)]
        ps23 = ctx.enter_context(nc.psum_tensor("ps23", [128, 1024], F))
        ps4, ps5, ps6, ps7 = [ctx.enter_context(nc.psum_tensor(f"ps{i}", [128, 512], F)) for i in (4, 5, 6, 7)]
        tr_bank = [ps4, ps5]
        bias_vec = nc.dram_tensor("bias_vec", [4, 16, 384], F, kind="Internal").ap()

        w_arrived = [sem(f"w_arrived{i}") for i in range(RAW)]
        w_hi_done = sem("w_hi_done")
        w_lo_done = sem("w_lo_done")
        acc_ready = sem("acc_ready")
        acc_free = [sem("acc_free0"), sem("acc_free1")]
        consts_in = sem("consts_in")
        ident_in = sem("ident_in")
        x_in = sem("x_in")
        hot_in = sem("hot_in")
        gatew_zero = sem("gatew_zero")
        relb_in = sem("relb_in")
        relb_one = sem("relb_one")
        cw_in = sem("cw_in")
        ln_in = sem("ln_in")
        y_ready = sem("y_ready")
        src_ready = sem("src_ready")
        at_ps = sem("at_ps")
        at_hi = sem("at_hi")
        at_lo = sem("at_lo")
        vec_ps = sem("vec_ps")
        vec_sb = sem("vec_sb")
        vec_out = sem("vec_out")
        bias_in = [sem("bias_in0"), sem("bias_in1")]
        stg_ps = sem("stg_ps")
        stg_a = sem("stg_a")
        stg_d = sem("stg_d")
        rot_done = sem("rot_done")
        rs_ps = sem("rs_ps")
        rs_sb = sem("rs_sb")
        ro_ps = sem("ro_ps")
        ro_used = sem("ro_used")
        tanh_done = sem("tanh_done")
        cmp_blk = sem("cmp_blk")
        k_dup_done = sem("k_dup_done")
        cmp_raw = sem("cmp_raw")
        cmp_tok = sem("cmp_tok")
        cmp_kv = sem("cmp_kv")
        cmp_kv_used = sem("cmp_kv_used")
        cmp_s = sem("cmp_s")
        cmp_l = sem("cmp_l")
        cmp_p = sem("cmp_p")
        cmp_t = sem("cmp_t")
        cmp_pt = sem("cmp_pt")
        cmp_o = sem("cmp_o")
        cmp_o_used = sem("cmp_o_used")
        s_ready = sem("s_ready")
        ttr_done = sem("ttr_done")
        p_ready = sem("p_ready")
        t_ready = sem("t_ready")
        pt_a = sem("pt_a")
        pt_d = sem("pt_d")
        o_ready = sem("o_ready")
        o_free = sem("o_free")
        lru_x = sem("lru_x")
        lru_xc = sem("lru_xc")
        lru_z = sem("lru_z")
        lru_th = sem("lru_th")
        lru_nla = sem("lru_nla")
        lru_at = sem("lru_at")
        lru_v2 = sem("lru_v2")
        lru_m = sem("lru_m")
        lru_y = sem("lru_y")
        h_done = sem("h_done")
        hh_done = sem("hh_done")
        hl_done = sem("hl_done")
        qk_norm = sem("qk_norm")
        ssq_done = sem("ssq_done")
        rstd_done = sem("rstd_done")
        x_new = sem("x_new")
        out_done = sem("out_done")
        lam_abs = sem("lam_abs")
        lam_e = sem("lam_e")
        dve_step = sem("dve_step")
        small_in = sem("small_in")

        NEEDS = {"in0": X0, "out0": Y0, "in1": X1, "out1": Y1, "dsw": DSW_U, "dswo": DSW_Y,
                 "up0": FFN0_U, "moba": MOBA_U, "mobao": MOBA_Y, "up1": FFN1_U}
        USED_BY = ["in0", "out0", "in1", "out1", "dsw", "dswo", "up0", "moba", "mobao", "up1"]
        last_block = {}
        for b, d in enumerate(BLOCKS):
            last_block[d["name"]] = b

        def blocks(name):
            return range(FIRST[name], last_block[name] + 1)

        def free_count(b):
            return sum(d["last"] for d in BLOCKS[:b])

        BIAS_BLOCK = 1
        def split_after(b, half):
            nxt = b + (AHEAD if half else AHEAD - 1)
            j = 1 - half
            return [CHUNK0[nxt] + j] if nxt < NB and j < BLOCKS[nxt]["kts"] // 4 else []

        HIDDEN0 = {0: 0, 1: 16}

        block = ctx.enter_context(nc.Block())

        @block.sync
        def _(sp):
            for c, (b, j) in enumerate(CHUNKS):
                d = BLOCKS[b]
                if c >= RAW:
                    sp.wait_ge(w_lo_done, c - RAW + 1)
                r0 = d["row0"] + 512 * j
                src = d["w"][r0:r0 + 512, d["c0"]:d["c0"] + d["n"]].rearrange("(k p) n -> p k n", p=128)
                sp.dma_start(w_raw[:, c % RAW, :, 0:d["n"]], src).then_inc(w_arrived[c % RAW], 16)
            for half in range(2):
                sp.wait_ge(acc_free[half], free_count(NB))
            sp.dma_start(out[0].rearrange("(t p) d -> p t d", p=128), x[:, :, :]).then_inc(out_done, 16)
            sp.wait_ge(out_done, 16)

        @block.gpsimd
        def _(pool):
            def compression_operands(l):
                if l:
                    pool.wait_ge(y_ready, l)
                    pool.wait_ge(lru_y, l)
                for v in range(2):
                    pool.dma_start(cw[:, v], dram["nsa_cmp_w"][l, v].rearrange("(m q) e -> q m e", q=128)).then_inc(cw_in, 16)
                for v in range(2):
                    for e in range(2):
                        pool.dma_start(cmp_pos[64 * e:64 * e + 64, v, :],
                                       dram["nsa_cmp_pos"][l, v].rearrange("(m e) d -> e d m", e=2)[e]).then_inc(cw_in, 16)
                b = FIRST[f"in{l}"] + 1
                for half in range(2):
                    pool.wait_ge(acc_free[half], free_count(b) + 1)
                pool.wait_ge(relb_one, 1)
                for v in range(2):
                    c0 = COL[("nkc", "nvc")[v]]
                    for e in range(2):
                        ins = pool.tensor_copy(k_dup[:, v, :, :, 64 * e:64 * e + 64],
                                               proj[:, :, c0:c0 + 128].rearrange("p t (g d) -> p t g d", g=2))
                ins.then_inc(k_dup_done, 1)

            pool.dma_start(ident[:, :], dram["c_ident"]).then_inc(ident_in, 16)
            pool.memset(gate_w[:, :, :, :, :], 0.0).then_inc(gatew_zero, 1)
            pool.wait_ge(gatew_zero, 1)
            pool.memset(relb[32:33, :], 1.0).then_inc(relb_one, 1)
            with nc.allow_non_contiguous_dma(reason="vectors of one element per partition"):
                pool.dma_start(hot[0:33], dram["c_hot"]).then_inc(hot_in, 16)
                pool.dma_start(relb[0:32, :], dram["rel_bias_2"]).then_inc(relb_in, 16)
                for dst, src in ((rope, "c_rope"), (decay, "c_decay"),
                                 (causal, "c_causal"), (cmp_mask, "c_cmp_mask"), (cmp_any, "c_cmp_any"),
                                 (head_of, "c_head_of"), (half_of, "c_half_of"), (rep, "c_rep")):
                    n = len(dst.shape)
                    pool.dma_start(dst[tuple([slice(None)] * n)], dram[src]).then_inc(consts_in, 16)
                compression_operands(0)
                pool.wait_ge(vec_sb, 1)
                pool.dma_start(bias_vec[0:3, 0:8].rearrange("k h m -> h k m"), vec[0:8, 0:3, :]).then_inc(vec_out, 16)
                pool.dma_start(bias_vec[3, 0:16], vec[0:16, 3, :]).then_inc(vec_out, 16)
                for l in range(LAYERS):
                    for c in range(2):
                        pool.dma_start(conv_w[:, l, c], dram["lru_conv_w"][l, :, 128 * c:128 * c + 128].rearrange("k p -> p k")).then_inc(small_in, 16)
                    for i, nm in enumerate(("lru_conv_b", "lru_b_a", "lru_b_x", "lru_lambda")):
                        pool.dma_start(lru_v[:, l, i], dram[nm][l].rearrange("(c p) -> p c", p=128)).then_inc(small_in, 16)
                    pool.dma_start(norm_g[:, l], dram["norm_mix_2"][l].rearrange("(c p) -> p c", p=128)).then_inc(small_in, 16)
                    pool.dma_start(norm_g[:, 2 + l], dram["norm_ffn_2"][l].rearrange("(c p) -> p c", p=128)).then_inc(small_in, 16)
                for i, nm in enumerate(("a_q_gain_2", "a_k_gain_2", "b_q_gain_2", "b_k_gain_2")):
                    for e in range(2):
                        pool.dma_start(qk_g[64 * e:64 * e + 64, i:i + 1], dram[nm][0].rearrange("(p o) -> p o", o=1)).then_inc(small_in, 16)
                pool.wait_ge(gatew_zero, 1)
                for l in range(LAYERS):
                    for i, nm in enumerate(("lru_w_a", "lru_w_x")):
                        for n in range(4):
                            e = n % 2
                            pool.dma_start(gate_w[64 * e:64 * e + 64, l, i, n // 2, 64 * e:64 * e + 64],
                                           dram[nm][l, n]).then_inc(small_in, 16)
                for l in range(LAYERS):
                    if l:
                        compression_operands(l)
                    pool.wait_ge(y_ready, l + 1)
                    for i, nm in enumerate(("ln_g", "ln_b")):
                        pool.dma_start(ln_v[:, i, :], dram[nm][l].partition_broadcast(128)).then_inc(ln_in, 16)
                for u in range(DSW_HEADS + MOBA_HEADS):
                    g = UNIT0[2] + u
                    if u < 2:
                        pool.wait_ge(x_new, 2)
                        pool.wait_ge(vec_out, 32)
                    elif u == DSW_HEADS or u == DSW_HEADS + 1:
                        for half in range(2):
                            pool.wait_ge(acc_free[half], free_count(FIRST["moba"]))
                    else:
                        pool.wait_ge(ttr_done, g - 2 + 1)
                    if u < DSW_HEADS:
                        src = bass.AP(bias_vec.tensor, u * 384, [[1, 128], [16 * 384, 3], [1, S]])
                        dst = bias_T[:, u % 2, :].rearrange("p (g n) -> p g n", g=3)
                    else:
                        src = bass.AP(bias_vec.tensor, (3 * 16 + u - DSW_HEADS) * 384, [[1, 128], [1, S]])
                        dst = bias_T[:, u % 2, 0:S]
                    pool.dma_start(dst, src).then_inc(bias_in[u % 2], 16)

        SMALL = 16 * (LAYERS * 8 + 8 + LAYERS * 8)

        @block.tensor
        def _(pe):
            def gemm(b, halves=(0, 1)):
                d = BLOCKS[b]
                slot, n = b % AHEAD, d["n"]
                hidden = d["name"].startswith("down")
                for half in halves:
                    bank = ps[half]
                    if d["first"] and free_count(b):
                        pe.wait_ge(acc_free[half], free_count(b))
                    if d["form"] == "tok":
                        for k in range(d["kts"]):
                            if half == 0 and k % 4 == 0:
                                pe.wait_ge(w_lo_done, CHUNK0[b] + k // 4 + 1)
                            if hidden:
                                ah = h_hi[:, d["act0"] + k, 128 * half:128 * half + 128]
                                al = h_lo[:, d["act0"] + k, 128 * half:128 * half + 128]
                            else:
                                ah = act_hi[:, k, 128 * half:128 * half + 128]
                                al = act_lo[:, k, 128 * half:128 * half + 128]
                            wh, wl = w_hi[:, slot, k, 0:n], w_lo[:, slot, k, 0:n]
                            first = d["first"] and k == 0
                            last = d["last"] and k == d["kts"] - 1
                            pe.matmul(bank[:, 0:n], ah, wh, start=first, stop=False)
                            pe.matmul(bank[:, 0:n], ah, wl, start=False, stop=False)
                            mm = pe.matmul(bank[:, 0:n], al, wh, start=False, stop=last)
                    else:
                        for f in (2 * half, 2 * half + 1):
                            o = bank[:, (f % 2) * S:(f % 2) * S + S]
                            cols = slice(128 * f, 128 * f + 128)
                            for k in range(d["kts"]):
                                if f == 0 and k % 4 == 0:
                                    pe.wait_ge(w_lo_done, CHUNK0[b] + k // 4 + 1)
                                wh, wl = w_hi[:, slot, k, cols], w_lo[:, slot, k, cols]
                                pe.matmul(o, wh, act_hi[:, k, :], start=k == 0, stop=False)
                                pe.matmul(o, wh, act_lo[:, k, :], start=False, stop=False)
                                mm = pe.matmul(o, wl, act_hi[:, k, :], start=False, stop=k == d["kts"] - 1)
                    mm.then_inc(acc_ready, 1)

            def gemms(name, count=None):
                if name in NEEDS:
                    a = NEEDS[name]
                    pe.wait_ge(at_lo, ACT0[a + 1])
                for b in blocks(name)[:count]:
                    gemm(b)
                    if b == BIAS_BLOCK:
                        bias_vectors()

            def bias_vectors():
                pe.wait_ge(hot_in, 16)
                pe.wait_ge(relb_in, 16)
                pe.wait_ge(relb_one, 1)
                for k in range(4):
                    cols = slice(8 * k, 8 * k + 8) if k < 3 else slice(0, 16)
                    o = (ps23[:, 0:512], ps23[:, 512:1024], ps6, ps7)[k]
                    mm = pe.matmul(o[0:8 if k < 3 else 16, 0:384], relb[:, cols], hot[0:33, k, :], start=True, stop=True)
                mm.then_inc(vec_ps, 1)

            def transpose_acts(a, src, kts):
                if a == X0:
                    pe.wait_ge(x_in, 16)
                elif a == X1:
                    pe.wait_ge(x_new, 1)
                elif a in (Y0, Y1):
                    pe.wait_ge(y_ready, 1 + (a == Y1))
                elif a in (DSW_Y, MOBA_Y):
                    pe.wait_ge(o_free, {DSW_Y: UNIT0[2] + DSW_HEADS, MOBA_Y: UNIT0[3] + MOBA_HEADS}[a] // 4)
                else:
                    pe.wait_ge(src_ready, (DSW_U, FFN0_U, MOBA_U, FFN1_U).index(a) + 1)
                for i in range(kts // 2):
                    if i >= 2:
                        pe.wait_ge(at_lo, ACT0[a] + LRU_CHUNK[a] + i - 1)
                    for q in range(4):
                        k, t = 2 * i + q // 2, q % 2
                        mm = pe.transpose(tr_bank[i % 2][:, 128 * q:128 * q + 128],
                                          src[:, t, 128 * k:128 * k + 128], ident[:, :])
                    mm.then_inc(at_ps, 1)

            def retention_transposes(l):
                pe.wait_ge(rot_done, l + 1)
                for c in range(2):
                    for q in range(4):
                        p, t = q // 2, q % 2
                        mm = pe.transpose(tr_bank[c][:, 128 * q:128 * q + 128],
                                          rot[:, t, 256 * c + 128 * p:256 * c + 128 * p + 128], ident[:, :])
                    mm.then_inc(stg_ps, 1)

            def retention_scores(l, heads):
                pe.wait_ge(stg_a, STG0[l] // 2 + 4)
                pe.wait_ge(stg_d, STG0[l] // 2 + 4)
                for h in heads:
                    p, e = h // 2, 64 * (h % 2)
                    q = ret_T[e:e + 64, p, :]
                    k = ret_T[e:e + 64, 2 + p, :]
                    o = ps23[:, 512 * (h % 2):512 * (h % 2) + 384]
                    if h >= 2:
                        pe.wait_ge(rs_sb, RET_HEADS * l + h - 1)
                    pe.matmul(o[:, 0:S], k[:, 0:128], q[:, :], start=True, stop=True)
                    pe.matmul(o[:, S:384], k[:, 128:256], q[:, 128:256], start=True, stop=True).then_inc(rs_ps, 1)

            def retention_output(l):
                pe.wait_ge(cmp_o_used, l + 1)
                for h in range(RET_HEADS):
                    pe.wait_ge(rs_sb, RET_HEADS * l + h + 1)
                    v = lambda t: proj[:, t, COL["rv"] + 64 * h:COL["rv"] + 64 * h + 64]
                    o1 = ps6[:, 128 * h + 64:128 * h + 128]
                    pe.matmul(o1, ret_P[:, h, 128:256], v(0), start=True, stop=False)
                    pe.matmul(o1, ret_P[:, h, 256:384], v(1), start=False, stop=True)
                    mm = pe.matmul(ps6[:, 128 * h:128 * h + 64], ret_P[:, h, 0:128], v(0), start=True, stop=True)
                mm.then_inc(ro_ps, 1)

            def unit(ph, u, what):
                kind = ("nsa", "nsa", "dsw", "moba")[ph]
                gu = UNIT0[ph] + u
                parts = 3 if kind == "dsw" else 1
                if kind == "nsa":
                    br, h = u // 8, u % 8
                    e = 64 * (h // 4)
                    q = [nT[e:e + 64, h % 4, :]]
                    k = [nT[e:e + 64, 8 + br, :]]
                    c0 = COL[("nvs", "nvw")[br]] + e
                    v = [lambda t: proj[:, t, c0:c0 + 64]]
                    P, PT, slots = nsa_P, nsa_PT, 2
                else:
                    p, e = u // 2, 64 * (u % 2)
                    q = [stage[e:e + 64, p % 2, 2 * g, :] for g in range(parts)]
                    k = [stage[e:e + 64, p % 2, 2 * g + 1, :] for g in range(parts)]
                    if kind == "dsw":
                        v = [lambda t, g=g: qkv[:, t, 512 * (6 + g) + 64 * u:512 * (6 + g) + 64 * u + 64] for g in range(3)]
                    else:
                        v = [lambda t: qkv[:, t, 2048 + 64 * u:2048 + 64 * u + 64]]
                    P, PT, slots = big_P, big_PT, 4
                if what == "scores":
                    if kind == "dsw":
                        if u >= 1:
                            pe.wait_ge(ttr_done, gu)
                        for g in range(3):
                            pe.matmul(ps23[:, S * g:S * g + S], q[g][:, 128:256], k[g][:, :], start=True, stop=True)
                        for g in range(3):
                            mm = pe.matmul(ps7[:, 128 * g:128 * g + 128], q[g][:, 0:128], k[g][:, 0:128], start=True, stop=True)
                    else:
                        if u >= 2:
                            pe.wait_ge(ttr_done, gu - 1)
                        o = ps23[:, 512 * (u % 2):512 * (u % 2) + 384]
                        pe.matmul(o[:, 0:S], q[0][:, 128:256], k[0][:, :], start=True, stop=True)
                        mm = pe.matmul(o[:, S:384], q[0][:, 0:128], k[0][:, 0:128], start=True, stop=True)
                    mm.then_inc(s_ready, 1)
                if what == "transposes":
                    pe.wait_ge(p_ready, gu + 1)
                    for g in range(parts):
                        c = PCH0[ph] + parts * u + g
                        if g >= 2:
                            pe.wait_ge((pt_a, pt_d)[c % 2], c // 2)
                        at = (S * g, S * g + 128, S * parts + 128 * g)
                        for i in range(3):
                            mm = pe.transpose(tr_bank[c % 2][:, 128 * i:128 * i + 128],
                                              P[:, u % 2, at[i]:at[i] + 128], ident[:, :])
                        mm.then_inc(t_ready, 1)
                if what == "output":
                    quad = gu // 4
                    o = ps6 if kind == "dsw" else (ps7, ps6)[quad % 2]
                    if u % 4 == 0 and kind == "dsw":
                        pe.wait_ge(o_free, quad)
                    elif u % 4 == 0 and quad >= 2:
                        pe.wait_ge(o_free, quad - 1)
                    if kind == "nsa" and u == 4:
                        pe.wait_ge(ro_used, ph + 1)
                    c = PCH0[ph] + parts * u
                    for g in range(min(parts, 2)):
                        last = c + g + (2 if g + 2 < parts else 0)
                        pe.wait_ge((pt_a, pt_d)[last % 2], last // 2 + 1)
                    sl = lambda g: PT[:, (c - PCH0[ph] + g) % slots, :]
                    at = 128 * (u % 4)
                    for g in range(parts):
                        pe.matmul(o[:, at + 64:at + 128], sl(g)[:, 0:128], v[g](0), start=g == 0, stop=False)
                        pe.matmul(o[:, at + 64:at + 128], sl(g)[:, 128:256], v[g](1), start=False, stop=g == parts - 1)
                    for g in range(parts):
                        mm = pe.matmul(o[:, at:at + 64], sl(g)[:, 256:384], v[g](0), start=g == 0, stop=g == parts - 1)
                    if u % 4 == 3:
                        mm.then_inc(o_ready, 1)

            def stage_pair(ph, p):
                parts = 3 if ph == 2 else 1
                for g in range(parts):
                    for c in range(2):
                        if g:
                            s = STG0[ph] + 2 * parts * p + 2 * (g - 1) + c
                            pe.wait_ge((stg_a, stg_d)[c], s // 2 + 1)
                        c0 = 512 * (3 * c + g) + 128 * p if ph == 2 else 1024 * c + 128 * p
                        for t in range(2):
                            mm = pe.transpose(tr_bank[c][:, 128 * t:128 * t + 128],
                                              qkv[:, t, c0:c0 + 128], ident[:, :])
                        mm.then_inc(stg_ps, 1)

            def staged(ph, p):
                s = STG0[ph] + 2 * (3 if ph == 2 else 1) * (p + 1)
                pe.wait_ge(stg_a, s // 2)
                pe.wait_ge(stg_d, s // 2)

            def attention(ph, units, hooks={}):
                pairs = units // 2 if ph >= 2 else 0
                if pairs:
                    stage_pair(ph, 0)
                    staged(ph, 0)
                unit(ph, 0, "scores")
                unit(ph, 1, "scores")
                if pairs:
                    stage_pair(ph, 1)
                for u in range(units):
                    if pairs and u % 2 == 0 and u // 2 + 1 < pairs:
                        staged(ph, u // 2 + 1)
                    unit(ph, u, "transposes")
                    if u + 2 < units:
                        unit(ph, u + 2, "scores")
                    if pairs and u % 2 and (u + 3) // 2 < pairs:
                        c = PCH0[ph] + u
                        pe.wait_ge((pt_a, pt_d)[c % 2], c // 2 + 1)
                        stage_pair(ph, (u + 3) // 2)
                    unit(ph, u, "output")
                    if u in hooks:
                        hooks[u]()

            def dsw_attention(ph, units):
                stage_pair(ph, 0)
                staged(ph, 0)
                unit(ph, 0, "scores")
                for u in range(units):
                    if u + 1 < units:
                        if (u + 1) % 2 == 0:
                            stage_pair(ph, (u + 1) // 2)
                            staged(ph, (u + 1) // 2)
                        unit(ph, u + 1, "scores")
                    unit(ph, u, "transposes")
                    unit(ph, u, "output")

            def nsa_transposes(l):
                s0 = STG0[l]
                for half in range(2):
                    pe.wait_ge(acc_free[half], free_count(FIRST[f"in{l}"] + 3) + 1)
                for c in range(6):
                    if c >= 2:
                        pe.wait_ge((stg_a, stg_d)[c % 2], (s0 + c) // 2)
                    if c == 2:
                        pe.wait_ge(k_dup_done, l + 1)
                    for q in range(4 if c < 4 else 2):
                        i, t = q // 2, q % 2
                        if c < 2:
                            src = proj[:, t, COL["nq"] + 128 * (2 * c + i):COL["nq"] + 128 * (2 * c + i) + 128]
                        elif c < 4:
                            src = k_dup[:, c - 2, t, i, :]
                        else:
                            src = proj[:, t, COL[("nks", "nkw")[c - 4]]:COL[("nks", "nkw")[c - 4]] + 128]
                        mm = pe.transpose(tr_bank[c % 2][:, 128 * q:128 * q + 128], src, ident[:, :])
                    mm.then_inc(stg_ps, 1)

            def compress(l):
                pe.wait_ge(consts_in, 16 * 8)
                pe.wait_ge(cmp_blk, 2 * l + 2)
                for v in range(2):
                    for m in range(16):
                        mm = pe.matmul(ps23[0:32, 512 * v:512 * v + 64], blk[:, v, m, :], cw[:, v, m, :], start=m == 0, stop=m == 15)
                mm.then_inc(cmp_raw, 1)

            def compressed_operands(l):
                pe.wait_ge(cmp_tok, l + 1)
                pe.transpose(ps23[:, 0:32], k_c2[0:32].rearrange("p c n -> p (c n)"), ident[0:32, 0:32])
                pe.matmul(ps23[:, 512:576], rep[:, :], v_c[0:32], start=True, stop=True).then_inc(cmp_kv, 1)

            def compressed_scores(l):
                pe.wait_ge(cmp_kv_used, l + 1)
                for t in range(TT):
                    for p in range(4):
                        mm = pe.matmul(ps7[:, 128 * t + 32 * p:128 * t + 32 * p + 32],
                                       nT[:, p, 128 * t:128 * t + 128],
                                       k_bd.rearrange("p g n -> p (g n)"), start=True, stop=True)
                mm.then_inc(cmp_s, 1)

            def compressed_transposes(l):
                pe.wait_ge(cmp_p, l + 1)
                for t in range(TT):
                    mm = pe.transpose(ps4[:, 128 * t:128 * t + 128], cmp_L[:, 128 * t:128 * t + 128], ident[:, :])
                mm.then_inc(cmp_t, 1)

            def compressed_output(l):
                pe.wait_ge(cmp_pt, l + 1)
                for t in range(TT):
                    mm = pe.matmul((ps6, ps7)[t][:, :], cmp_PT[:, 128 * t:128 * t + 128],
                                   v_bd.rearrange("p h n -> p (h n)"), start=True, stop=True)
                mm.then_inc(cmp_o, 1)

            def hybrid(l):
                gemms(f"in{l}", 4)
                b = FIRST[f"in{l}"] + 4
                nsa_transposes(l)
                gemm(b, [0])
                compress(l)
                gemm(b, [1])
                compressed_operands(l)
                gemm(b + 1, [0])
                compressed_scores(l)
                retention_transposes(l)
                gemm(b + 1, [1])
                retention_scores(l, (0, 1))
                compressed_transposes(l)
                gemm(b + 2, [0])
                compressed_output(l)
                retention_scores(l, (2, 3))
                gemm(b + 2, [1])
                retention_output(l)
                attention(l, 16, {6: lambda: lru(l)})

            def lru(l):
                pe.wait_ge(small_in, SMALL)
                pe.wait_ge(lru_xc, 2 * l + 2)
                for half in range(2):
                    pe.wait_ge(acc_free[half], free_count(FIRST[f"out{l}"]))
                for i in range(2):
                    for c in range(2):
                        mm = pe.matmul(ps[i][:, S * c:S * c + S], gate_w[:, l, i, c, :],
                                       lru_w[:, 0, c, :], start=True, stop=True)
                mm.then_inc(lru_z, 1)

            pe.wait_ge(ident_in, 16)
            for l in range(LAYERS):
                transpose_acts(2 * l, x, KD)
                hybrid(l)
                transpose_acts(2 * l + 1, y, 6)
                gemms(f"out{l}")
            transpose_acts(DSW_U, y, KD)
            gemms("dsw")
            pe.wait_ge(qk_norm, 6)
            dsw_attention(2, DSW_HEADS)
            transpose_acts(DSW_Y, y, 4)
            gemms("dswo")
            transpose_acts(FFN0_U, y, KD)
            gemms("up0")
            pe.wait_ge(hl_done, 16)
            gemms("down0")
            transpose_acts(MOBA_U, y, KD)
            gemms("moba")
            pe.wait_ge(qk_norm, 10)
            attention(3, MOBA_HEADS)
            transpose_acts(MOBA_Y, y, KD)
            gemms("mobao")
            transpose_acts(FFN1_U, y, KD)
            gemms("up1")
            pe.wait_ge(hl_done, 32)
            gemms("down1")

        @block.scalar
        def _(act):
            def split_hi(c):
                b, j = CHUNKS[c]
                n = BLOCKS[b]["n"]
                act.wait_ge(w_arrived[c % RAW], 16 * (c // RAW + 1))
                if b >= AHEAD:
                    act.wait_ge(acc_ready, 2 * (b - AHEAD) + 2)
                act.activation(w_hi[:, b % AHEAD, 4 * j:4 * j + 4, 0:n], w_raw[:, c % RAW, :, 0:n], ACT.Copy).then_inc(w_hi_done, 1)

            def hidden_hi(g):
                act.wait_ge(h_done, g + 1)
                k = (2 * (g % 16))
                act.activation(h_hi[:, k:k + 2, :].rearrange("p k n -> p (k n)"), y[:, 1, 512 * (g % 2):512 * (g % 2) + 512], ACT.Copy).then_inc(hh_done, 1)

            def take(b, half):
                d = BLOCKS[b]
                n = d["n"]
                if not d["last"] or d["use"] in ("deepnorm", "residual"):
                    return
                act.wait_ge(acc_ready, 2 * b + half + 1)
                if d["use"] == "proj":
                    dst = proj if d["name"].startswith("in") else qkv
                    if dst is proj and d["c0"] == COL["nq"]:
                        act.activation(dst[:, half, d["c0"]:d["c0"] + n].rearrange("p (j g d) -> p g j d", j=4, g=2),
                                       ps[half].rearrange("p (g j d) -> p g j d", j=4, g=2), ACT.Copy).then_inc(acc_free[half], 1)
                    else:
                        act.activation(dst[:, half, d["c0"]:d["c0"] + n], ps[half][:, 0:n], ACT.Copy).then_inc(acc_free[half], 1)
                if d["use"] == "qk":
                    i = b - FIRST["dsw"] if d["name"] == "dsw" else 6 + b - FIRST["moba"]
                    if i:
                        act.wait_ge(qk_norm, i)
                    act.activation(qkv[:, half, d["c0"]:d["c0"] + n], ps[half][:, :], ACT.Copy)
                    act.activation(sq[:, half, :], ps[half][:, :], ACT.Square).then_inc(acc_free[half], 1)
                if d["use"] == "lru":
                    act.activation(lru_T[:, 2 * half:2 * half + 2, :].rearrange("p c n -> p (c n)"), ps[half][:, :], ACT.Copy).then_inc(acc_free[half], 1)
                if d["use"] == "relu2":
                    l = int(d["name"][-1])
                    g = HIDDEN0[l] + 2 * (b - FIRST[d["name"]]) + half
                    if g >= 2:
                        act.wait_ge(h_done, g - 1)
                    act.activation(y[:, 0, 512 * (g % 2):512 * (g % 2) + 512], ps[half][:, :], ACT.Relu).then_inc(acc_free[half], 1)

            def after_half(b, half):
                take(b, half)
                for c in split_after(b, half):
                    split_hi(c)
                if BLOCKS[b]["use"] == "relu2":
                    l = int(BLOCKS[b]["name"][-1])
                    hidden_hi(HIDDEN0[l] + 2 * (b - FIRST[BLOCKS[b]["name"]]) + half)

            def gemms(name, count=None):
                for b in blocks(name)[:count]:
                    for half in range(2):
                        after_half(b, half)
                    if b == BIAS_BLOCK:
                        bias_vectors()

            def bias_vectors():
                act.wait_ge(vec_ps, 1)
                for k in range(4):
                    n = 8 if k < 3 else 16
                    o = (ps23[:, 0:512], ps23[:, 512:1024], ps6, ps7)[k]
                    ins = act.activation(vec[0:n, k, :], o[0:n, 0:384], ACT.Copy)
                ins.then_inc(vec_sb, 1)

            def acts_hi(a, kts, gain=None):
                if a:
                    act.wait_ge(acc_ready, 2 * last_block[USED_BY[a - 1]] + 2)
                for i in range(kts // 2):
                    act.wait_ge(at_ps, TRANS0[a] + i + 1)
                    if gain is None:
                        act.activation(act_hi[:, 2 * i:2 * i + 2, :].rearrange("p k n -> p (k n)"), tr_bank[i % 2][:, :], ACT.Copy).then_inc(at_hi, 1)
                    else:
                        for k in range(2):
                            ins = act.activation(act_hi[:, 2 * i + k, :], tr_bank[i % 2][:, S * k:S * k + S], ACT.Copy,
                                                 scale=norm_g[:, gain, 2 * i + k:2 * i + k + 1])
                        ins.then_inc(at_hi, 1)

            def units(ph, n, hooks={}):
                kind = ("nsa", "nsa", "dsw", "moba")[ph]
                parts = 3 if kind == "dsw" else 1
                P, PT, slots = (nsa_P, nsa_PT, 2) if kind == "nsa" else (big_P, big_PT, 4)

                def staged(p):
                    for g in range(parts):
                        s = STG0[ph] + 2 * parts * p + 2 * g
                        act.wait_ge(stg_ps, s + 1)
                        act.activation(stage[:, p % 2, 2 * g, :], ps4[:, 0:S], ACT.Copy,
                                       scale=qk_gain[:, ph - 2:ph - 1]).then_inc(stg_a, 1)

                def softmax(u):
                    gu = UNIT0[ph] + u
                    act.wait_ge(ttr_done, gu + 1)
                    if gu >= 16 and gu % 4 == 0:
                        act.wait_ge(o_free, gu // 4 - 3)
                    w1, w0 = S * parts, 128 * parts
                    dn = den[:, gu % 16, :]
                    act.activation(P[:, u % 2, 0:w1], P[:, u % 2, 0:w1], ACT.Exp, bias=ttr[:, u % 2, 1:2], scale=-1.0,
                                   accum_out=dn[:, 1:2])
                    act.activation(P[:, u % 2, w1:w1 + w0], P[:, u % 2, w1:w1 + w0], ACT.Exp, bias=ttr[:, u % 2, 0:1],
                                   scale=-1.0, accum_out=dn[:, 0:1]).then_inc(p_ready, 1)

                def transposed(u):
                    for g in range(parts):
                        c = PCH0[ph] + parts * u + g
                        if c % 2 == 0:
                            act.wait_ge(t_ready, c + 1)
                            act.activation(PT[:, (c - PCH0[ph]) % slots, :], ps4[:, 0:384], ACT.Copy).then_inc(pt_a, 1)

                if ph >= 2:
                    staged(0)
                softmax(0)
                if parts == 1:
                    if ph >= 2:
                        staged(1)
                    softmax(1)
                for u in range(n):
                    if parts == 1:
                        transposed(u)
                        if ph >= 2 and u % 2 and u + 3 < n:
                            staged((u + 3) // 2)
                        if u + 2 < n:
                            softmax(u + 2)
                    else:
                        if (u + 1) % 2 == 0 and u + 1 < n:
                            staged((u + 1) // 2)
                        transposed(u)
                        if u + 1 < n:
                            softmax(u + 1)
                    if u in hooks:
                        hooks[u]()

            def nsa_transposed(l):
                for c in (0, 2, 4):
                    act.wait_ge(stg_ps, STG0[l] + c + 1)
                    at, k = ((0, 2), None, (4, 2), None, (8, 1))[c]
                    act.activation(nT[:, at:at + k, :].rearrange("p c n -> p (c n)"), ps4[:, 0:S * k], ACT.Copy,
                                   scale=HD ** -0.5 if c == 0 else 1.0).then_inc(stg_a, 1)

            def hybrid(l):
                gemms(f"in{l}", 4)
                b = FIRST[f"in{l}"] + 4
                act.wait_ge(vec_out, 32)
                nsa_transposed(l)
                act.activation(y[:, :, 256:768], proj[:, :, COL["ng"]:COL["ng"] + 512], ACT.Tanh, scale=0.5)
                act.activation(gate_c[:, :, :], proj[:, :, COL["ngl"]:COL["ngl"] + 24], ACT.Tanh, scale=0.5).then_inc(tanh_done, 1)
                after_half(b, 0)
                after_half(b, 1)
                after_half(b + 1, 0)
                act.wait_ge(stg_ps, STG0[l] + 7)
                act.activation(ret_T[:, 0:2, :].rearrange("p c n -> p (c n)"), ps4[:, :], ACT.Copy).then_inc(stg_a, 1)
                act.wait_ge(cmp_l, l + 1)
                act.activation(cmp_L, cmp_L, ACT.Exp).then_inc(cmp_p, 1)
                after_half(b + 1, 1)
                for half in range(2):
                    act.wait_ge(acc_free[half], free_count(b + 1) + 1)
                act.activation(y[:, :, 0:256], proj[:, :, COL["rg"]:COL["rg"] + 256], ACT.Tanh, scale=0.5).then_inc(tanh_done, 1)
                act.wait_ge(cmp_t, l + 1)
                act.activation(cmp_PT, ps4[:, 0:256], ACT.Copy).then_inc(cmp_pt, 1)
                act.wait_ge(cmp_blk, 2 * l + 2)
                after_half(b + 2, 0)
                if l == 0:
                    act.wait_ge(lam_abs, 1)
                    act.activation(lam_exp[:, :], lam_exp[:, :], ACT.Exp, scale=-1.0).then_inc(lam_e, 1)
                after_half(b + 2, 1)
                units(l, 16, {6: lambda: lru_gates(l), 8: lambda: lru_decay(l), 10: lambda: lru_root(l),
                              13: lambda: lru_operand(l)})

            def lru_gates(l):
                act.wait_ge(lru_z, l + 1)
                for c in range(2):
                    act.activation(lru_w[:, 1, c, :], ps[0][:, S * c:S * c + S], ACT.Tanh, bias=lru_hb[:, l, 0, c:c + 1], scale=0.5)
                for c in range(2):
                    act.activation(lru_w[:, 2, c, :], ps[1][:, S * c:S * c + S], ACT.Tanh, bias=lru_hb[:, l, 1, c:c + 1], scale=0.5)
                act.activation(lru_w[:, 6, :, :].rearrange("p c n -> p (c n)"), lru_T[:, 2:4, :].rearrange("p c n -> p (c n)"), ACT.Tanh, scale=0.5).then_inc(lru_th, 1)

            def lru_decay(l):
                act.wait_ge(lru_nla, l + 1)
                nla = lru_w[:, 1, :, :].rearrange("p c n -> p (c n)")
                act.activation(lru_w[:, 3, :, :].rearrange("p c n -> p (c n)"), nla, ACT.Exp, scale=-1.0)
                act.activation(lru_w[:, 4, :, :].rearrange("p c n -> p (c n)"), nla, ACT.Tanh).then_inc(lru_at, 1)

            def lru_root(l):
                act.wait_ge(lru_v2, l + 1)
                v2 = lru_w[:, 4, :, :].rearrange("p c n -> p (c n)")
                act.activation(v2, v2, ACT.Sqrt).then_inc(lru_m, 1)

            def lru_operand(l):
                act.wait_ge(lru_y, l + 1)
                act.wait_ge(acc_ready, 2 * last_block[f"in{l}"] + 2)
                act.activation(act_hi[:, 6:8, :].rearrange("p c n -> p (c n)"), lru_w[:, 5, :, :].rearrange("p c n -> p (c n)"), ACT.Copy).then_inc(at_hi, 1)

            def rms(i):
                if i == 0:
                    act.wait_ge(x_new, LAYERS)
                else:
                    for half in range(2):
                        act.wait_ge(acc_free[half], free_count(FIRST[("", "up0", "moba", "up1")[i]]))
                for t in range(TT):
                    ins = act.activation(y[:, t, :], x[:, t, :], ACT.Square, accum_out=st[:, 0, t:t + 1])
                ins.then_inc(ssq_done, 1)
                act.wait_ge(rstd_done, i + 1)
                for t in range(TT):
                    ins = act.activation(y[:, t, :], x[:, t, :], ACT.Copy, scale=st[:, 1, t:t + 1])
                ins.then_inc(src_ready, 1)

            act.dma_start(x[:, :, :], dram["x"][0].rearrange("(t p) d -> p t d", p=128)).then_inc(x_in, 16)
            acts_hi(X0, KD)
            for c in range(CHUNK0[AHEAD - 1] + 1):
                split_hi(c)
            for l in range(LAYERS):
                if l:
                    acts_hi(X1, KD)
                hybrid(l)
                acts_hi(2 * l + 1, 6)
                gemms(f"out{l}")
            rms(0)
            acts_hi(DSW_U, KD, gain=0)
            gemms("dsw")
            units(2, DSW_HEADS)
            acts_hi(DSW_Y, 4)
            gemms("dswo")
            rms(1)
            acts_hi(FFN0_U, KD, gain=2)
            gemms("up0")
            gemms("down0")
            rms(2)
            acts_hi(MOBA_U, KD, gain=1)
            gemms("moba")
            units(3, MOBA_HEADS)
            acts_hi(MOBA_Y, KD)
            gemms("mobao")
            rms(3)
            acts_hi(FFN1_U, KD, gain=3)
            gemms("up1")
            gemms("down1")

        @block.vector
        def _(dve):
            steps = [0]

            def done(ins):
                steps[0] += 1
                ins.then_inc(dve_step, 1)
                dve.wait_ge(dve_step, steps[0])

            def spread(ap, dims):
                return bass.AP(ap.tensor, ap.offset, [ap.ap[0], *[list(d) for d in dims]])

            def split_lo(c):
                b, j = CHUNKS[c]
                n = BLOCKS[b]["n"]
                dve.wait_ge(w_hi_done, c + 1)
                hi = w_hi[:, b % AHEAD, 4 * j:4 * j + 4, 0:n]
                lo = w_lo[:, b % AHEAD, 4 * j:4 * j + 4, 0:n]
                dve.tensor_tensor(lo, w_raw[:, c % RAW, :, 0:n], hi.bitcast(F), ALU.subtract).then_inc(w_lo_done, 1)

            def rsqrt(v, scale, eps, o, finish=None):
                n = v.shape[-1]
                m, a, c = st[:, 2, 0:n], st[:, 3, 0:n], st[:, 4, 0:n]
                done(dve.tensor_scalar(m, v, scale, eps, ALU.mult, ALU.add))
                done(dve.tensor_scalar(a.bitcast(I32), m.bitcast(I32), 1, None, ALU.logical_shift_right))
                done(dve.tensor_scalar(o.bitcast(I32), a.bitcast(I32), -1.0, float(0x5F3759DF), ALU.mult, ALU.add))
                for i in range(3):
                    done(dve.tensor_tensor(a, o, o, ALU.mult))
                    done(dve.scalar_tensor_tensor(out=c, in0=a, scalar=-0.5, in1=m, op0=ALU.mult, op1=ALU.mult))
                    (finish if finish and i == 2 else done)(dve.scalar_tensor_tensor(out=o, in0=c, scalar=1.5, in1=o, op0=ALU.add, op1=ALU.mult))

            def take(b, half):
                d = BLOCKS[b]
                n = d["n"]
                if not d["last"]:
                    return
                ready = free_count(b) + 1
                if d["use"] in ("deepnorm", "residual"):
                    dve.wait_ge(acc_ready, 2 * b + half + 1)
                    r = x[:, half, d["c0"]:d["c0"] + n]
                    dve.scalar_tensor_tensor(out=r, in0=r, scalar=ALPHA if d["use"] == "deepnorm" else 1.0,
                                             in1=ps[half][:, 0:n], op0=ALU.mult, op1=ALU.add).then_inc(acc_free[half], 1)
                if d["use"] == "qk" and half == 1:
                    dve.wait_ge(acc_free[0], ready)
                    dve.wait_ge(acc_free[1], ready)
                    done(dve.tensor_reduce(out=st[:, 5, 0:16], in_=sq.rearrange("p t (h d) -> p (t h) d", d=HD), axis=AX, op=ALU.add))
                    rsqrt(st[:, 5, 0:16], 1.0 / HD, 1e-6, st[:, 6, 0:16])
                    v = qkv[:, :, d["c0"]:d["c0"] + 512].rearrange("p t (h d) -> p t h d", d=HD)
                    dve.tensor_tensor(v, v, spread(st[:, 6, 0:1], [(8, 2), (1, 8), (0, HD)]), ALU.mult).then_inc(qk_norm, 1)
                if d["use"] == "relu2":
                    l = int(d["name"][-1])
                    g = HIDDEN0[l] + 2 * (b - FIRST[d["name"]]) + half
                    dve.wait_ge(acc_free[half], ready)
                    r = y[:, 0, 512 * (g % 2):512 * (g % 2) + 512]
                    dve.tensor_tensor(y[:, 1, 512 * (g % 2):512 * (g % 2) + 512], r, r, ALU.mult).then_inc(h_done, 1)

            def hidden_lo(g):
                k = 2 * (g % 16)
                dve.wait_ge(hh_done, g + 1)
                flat = "p k n -> p (k n)"
                dve.tensor_tensor(h_lo[:, k:k + 2, :].rearrange(flat), y[:, 1, 512 * (g % 2):512 * (g % 2) + 512],
                                  h_hi[:, k:k + 2, :].rearrange(flat).bitcast(F), ALU.subtract).then_inc(hl_done, 1)

            def after_half(b, half):
                take(b, half)
                for c in split_after(b, half):
                    split_lo(c)
                if BLOCKS[b]["use"] == "relu2":
                    l = int(BLOCKS[b]["name"][-1])
                    hidden_lo(HIDDEN0[l] + 2 * (b - FIRST[BLOCKS[b]["name"]]) + half)

            def gemms(name, count=None):
                for b in blocks(name)[:count]:
                    for half in range(2):
                        after_half(b, half)

            def small_params():
                dve.wait_ge(small_in, SMALL)
                done(dve.tensor_tensor(qk_gain[:, :], qk_g[:, 0:4:2], qk_g[:, 1:4:2], ALU.mult))
                done(dve.tensor_scalar(qk_gain[:, :], qk_gain[:, :], HD ** -0.5, None, ALU.mult))
                done(dve.tensor_scalar(lru_hb[:, :, :, :], lru_v[:, :, 1:3, :], 0.5, None, ALU.mult))
                lam = lru_v[:, :, 3, :]
                le = lam_exp[:, :].rearrange("p (l c) -> p l c", l=LAYERS)
                dve.scalar_tensor_tensor(out=le, in0=lam, scalar=-1.0, in1=lam, op0=ALU.mult, op1=ALU.max).then_inc(lam_abs, 1)
                dve.wait_ge(lam_e, 1)
                e, s1, s2, pl = lam_exp[:, :], lam_p[:, 0], lam_p[:, 1], lam_p[:, 2]
                done(dve.tensor_scalar(s2, e, 2.0, None, ALU.add))
                done(dve.reciprocal(s1, s2))
                done(dve.tensor_tensor(s1, s1, e, ALU.mult))
                done(dve.tensor_tensor(s2, s1, s1, ALU.mult))
                done(dve.tensor_scalar(pl, s2, 1.0 / 15, None, ALU.mult))
                for k in (13, 11, 9, 7, 5, 3):
                    done(dve.scalar_tensor_tensor(out=pl, in0=pl, scalar=1.0 / k, in1=s2, op0=ALU.add, op1=ALU.mult))
                done(dve.scalar_tensor_tensor(out=pl, in0=pl, scalar=1.0, in1=s1, op0=ALU.add, op1=ALU.mult))
                done(dve.tensor_scalar(lam_p[:, 3].rearrange("p (l c) -> p l c", l=LAYERS), lam, -1.0, 0.0, ALU.mult, ALU.max))
                done(dve.tensor_scalar(lam_p[:, 3], lam_p[:, 3], 4.0, None, ALU.mult))
                done(dve.scalar_tensor_tensor(out=lru_sp[:, :], in0=pl, scalar=8.0, in1=lam_p[:, 3], op0=ALU.mult, op1=ALU.add))

            def acts_lo(a, kts, gain=None):
                for i in range(kts // 2):
                    dve.wait_ge(at_hi, ACT0[a] + LRU_CHUNK[a] + i + 1)
                    if gain is None:
                        hi = act_hi[:, 2 * i:2 * i + 2, :].rearrange("p k n -> p (k n)").bitcast(F)
                        lo = act_lo[:, 2 * i:2 * i + 2, :].rearrange("p k n -> p (k n)")
                        dve.tensor_tensor(lo, tr_bank[i % 2][:, :], hi, ALU.subtract).then_inc(at_lo, 1)
                    else:
                        for k in (2 * i, 2 * i + 1):
                            ins = dve.scalar_tensor_tensor(
                                out=act_lo[:, k, :], in0=tr_bank[i % 2][:, S * (k % 2):S * (k % 2) + S],
                                scalar=norm_g[:, gain, k:k + 1], in1=act_hi[:, k, :].bitcast(F),
                                op0=ALU.mult, op1=ALU.subtract)
                        ins.then_inc(at_lo, 1)

            def rotate():
                half = HD // 2

                def part(v, c0, e):
                    base = v[:, :, c0 + half * e:c0 + half * e + 1]
                    return spread(base, [(v.ap[1][0], 2), (HD, 8), (1, half)])

                for e in range(2):
                    cos, sin = [spread(rope[:, i, 0, 0:1], [(half, 2), (0, 8), (1, half)]) for i in range(2)]
                    dve.tensor_tensor(part(rot, 0, e), part(proj, COL["rq"], e), cos, ALU.mult)
                    done(dve.tensor_tensor(part(rot_b, 0, e), part(proj, COL["rq"], 1 - e), sin, ALU.mult))
                for e in range(2):
                    ins = dve.tensor_tensor(part(rot, 0, e), part(rot, 0, e), part(rot_b, 0, e), (ALU.subtract, ALU.add)[e])
                ins.then_inc(rot_done, 1)

            def units(ph, n, hooks={}):
                kind = ("nsa", "nsa", "dsw", "moba")[ph]
                parts = 3 if kind == "dsw" else 1
                P, PT, slots = (nsa_P, nsa_PT, 2) if kind == "nsa" else (big_P, big_PT, 4)
                w1 = S * parts

                def staged(p):
                    for g in range(parts):
                        s = STG0[ph] + 2 * parts * p + 2 * g + 1
                        dve.wait_ge(stg_ps, s + 1)
                        dve.tensor_copy(stage[:, p % 2, 2 * g + 1, :], ps5[:, 0:S]).then_inc(stg_d, 1)

                def logits(u):
                    gu = UNIT0[ph] + u
                    dve.wait_ge(s_ready, gu + 1)
                    if u >= 2:
                        dve.wait_ge(t_ready, PCH0[ph] + parts * (u - 1))
                    if kind == "nsa":
                        m1, m0 = causal[:, :], causal[:, 128:256]
                    else:
                        bu = u + (DSW_HEADS if kind == "moba" else 0)
                        dve.wait_ge(bias_in[bu % 2], 16 * (bu // 2 + 1))
                        m1 = spread(bias_T[:, bu % 2, 255:256], [(S, parts), (-1, S)])
                        m0 = spread(bias_T[:, bu % 2, 127:128], [(S, parts), (-1, 128)])
                    if kind == "dsw":
                        s1, s0 = ps23[:, 0:w1].rearrange("p (g n) -> p g n", g=3), ps7[:, 0:384].rearrange("p (g n) -> p g n", g=3)
                        o0 = P[:, u % 2, w1:w1 + 384].rearrange("p (g n) -> p g n", g=3)
                    else:
                        s1, s0 = [ps23[:, 512 * (u % 2) + a:512 * (u % 2) + b] for a, b in ((0, S), (S, 384))]
                        o0 = P[:, u % 2, S:384]
                        if kind == "moba":
                            m1, m0 = spread(bias_T[:, bu % 2, 255:256], [(-1, S)]), spread(bias_T[:, bu % 2, 127:128], [(-1, 128)])
                    o1 = P[:, u % 2, 0:w1]
                    if kind == "dsw":
                        o1 = o1.rearrange("p (g n) -> p g n", g=3)
                    dve.tensor_tensor_reduce(out=o1, in0=s1, in1=m1, scale=-1.0, scalar=3.0e38,
                                             op0=ALU.add, op1=ALU.min, accum_out=ttr[:, u % 2, 1:2])
                    dve.tensor_tensor_reduce(out=o0, in0=s0, in1=m0, scale=-1.0, scalar=3.0e38,
                                             op0=ALU.add, op1=ALU.min, accum_out=ttr[:, u % 2, 0:1]).then_inc(ttr_done, 1)

                def transposed(u):
                    for g in range(parts):
                        c = PCH0[ph] + parts * u + g
                        if c % 2 == 1:
                            dve.wait_ge(t_ready, c + 1)
                            dve.tensor_copy(PT[:, (c - PCH0[ph]) % slots, :], ps5[:, 0:384]).then_inc(pt_d, 1)

                def quad_output(u0):
                    quad = (UNIT0[ph] + u0) // 4
                    dve.wait_ge(o_ready, quad + 1)
                    sums = den[:, 4 * quad % 16:4 * quad % 16 + 4, :]
                    done(dve.reciprocal(rden[:, :, :], sums))
                    o = (ps6 if kind == "dsw" else (ps7, ps6)[quad % 2]).rearrange("p (h d) -> p h d", d=HD)
                    if kind == "nsa":
                        br, h = u0 // 8, u0 % 8
                        gc = spread(gate_c[:, 0, 3 * h + 1 + br:3 * h + 2 + br], [(3, 4), (24, 2)])
                        done(dve.tensor_tensor(rden[:, :, :], rden[:, :, :], gc, ALU.mult))
                        part = o_part.rearrange("p (h d) -> p h d", d=HD)
                        dve.tensor_tensor(part, o, spread(rden[:, 0, 0:1], [(1, 8), (0, HD)]), ALU.mult).then_inc(o_free, 1)
                        dve.wait_ge(o_free, quad + 1)
                        yv = spread(y[:, 0, 256 + HD * h:257 + HD * h], [(HD, 4), (D, 2), (1, HD)])
                        done(dve.tensor_tensor(yv, yv, part.rearrange("p (h t) d -> p h t d", t=2), ALU.add))
                    else:
                        yv = spread(y[:, 0, HD * u0:HD * u0 + 1], [(HD, 4), (D, 2), (1, HD)])
                        dve.tensor_tensor(yv, o.rearrange("p (h t) d -> p h t d", t=2),
                                          spread(rden[:, 0, 0:1], [(2, 4), (1, 2), (0, HD)]), ALU.mult).then_inc(o_free, 1)

                if ph >= 2:
                    staged(0)
                logits(0)
                if parts == 1:
                    logits(1)
                    if ph >= 2:
                        staged(1)
                for u in range(n):
                    if parts == 1:
                        transposed(u)
                        if u + 2 < n:
                            logits(u + 2)
                        if ph >= 2 and u % 2 and u + 3 < n:
                            staged((u + 3) // 2)
                        if u % 4 == 0 and u:
                            quad_output(u - 4)
                    else:
                        if u + 1 < n:
                            if (u + 1) % 2 == 0:
                                staged((u + 1) // 2)
                            logits(u + 1)
                        transposed(u)
                        if u % 4 == 3:
                            quad_output(u - 3)
                    if u in hooks:
                        hooks[u]()
                if parts == 1:
                    quad_output(n - 4)

            def decay_scores(l, heads):
                for h in heads:
                    dve.wait_ge(rs_ps, RET_HEADS * l + h + 1)
                    o = ps23[:, 512 * (h % 2):512 * (h % 2) + 384]
                    dve.tensor_tensor(ret_P[:, h, 0:S], o[:, 0:S], decay[:, h, :], ALU.mult)
                    dve.tensor_tensor(ret_P[:, h, S:384], o[:, S:384], decay[:, h, 0:128], ALU.mult).then_inc(rs_sb, 1)

            def gate_silu(l, c0, n, g0):
                g = proj[:, :, g0:g0 + n]
                return dve.scalar_tensor_tensor(out=g, in0=y[:, :, c0:c0 + n], scalar=1.0, in1=g, op0=ALU.add, op1=ALU.mult)

            ret_o = ps6.rearrange("p (h d) -> p h d", d=HD)
            cen = tmp_tok[:, 0:512].rearrange("p (h d) -> p h d", d=HD)
            squ = tmp_tok[:, 512:1024].rearrange("p (h d) -> p h d", d=HD)

            def retention_norm(l, step):
                if step == 0:
                    dve.wait_ge(ro_ps, l + 1)
                    done(dve.tensor_reduce(out=st[:, 0, 0:8], in_=ret_o, axis=AX, op=ALU.add))
                    done(dve.tensor_scalar(st[:, 1, 0:8], st[:, 0, 0:8], 1.0 / HD, None, ALU.mult))
                    dve.tensor_tensor(cen, ret_o, spread(st[:, 1, 0:1], [(1, 8), (0, HD)]), ALU.subtract).then_inc(ro_used, 1)
                    dve.wait_ge(ro_used, l + 1)
                if step == 1:
                    done(dve.tensor_tensor(squ, cen, cen, ALU.mult))
                    done(dve.tensor_reduce(out=st[:, 5, 0:8], in_=squ, axis=AX, op=ALU.add))
                if step == 2:
                    rsqrt(st[:, 5, 0:8], 1.0 / HD, 1e-5, st[:, 6, 0:8])
                    done(dve.tensor_scalar(st[:, 7, 0:8], st[:, 6, 0:8], 0.5, None, ALU.mult))
                if step == 3:
                    done(dve.tensor_tensor(cen, cen, spread(st[:, 7, 0:1], [(1, 8), (0, HD)]), ALU.mult))
                    done(dve.tensor_tensor(spread(y[:, 0, 0:1], [(HD, 4), (D, 2), (1, HD)]), cen.rearrange("p (h t) d -> p h t d", t=2),
                                           spread(proj[:, 0, COL["rg"]:COL["rg"] + 1], [(HD, 4), (2840, 2), (1, HD)]), ALU.mult))

            def nsa_operands(l):
                dve.wait_ge(vec_out, 32)
                for v in range(2):
                    dve.memset(spread(blk[:, v, 0, 15:16], [(32, 16), (16, 2), (1, 1)]), 0.0)
                for c in (1, 3, 5):
                    dve.wait_ge(stg_ps, STG0[l] + c + 1)
                    at, k = (None, (2, 2), None, (6, 2), None, (9, 1))[c]
                    dve.tensor_scalar(nT[:, at:at + k, :].rearrange("p c n -> p (c n)"), ps5[:, 0:S * k],
                                      HD ** -0.5 if c == 1 else 1.0, None, ALU.mult).then_inc(stg_d, 1)
                dve.wait_ge(stg_a, (STG0[l] + 6) // 2)
                dve.wait_ge(stg_d, (STG0[l] + 6) // 2)
                dve.wait_ge(cw_in, 16 * 6 * (l + 1))
                for v in range(2):
                    for e in range(2):
                        r = slice(64 * e, 64 * e + 64)
                        ins = dve.tensor_tensor(
                            spread(blk[r, v, 0, 0:1], [(32, 16), (16, 2), (1, N_CMP)]),
                            spread(nT[r, 4 + 2 * v, e:e + 1], [(2, 16), (S, 2), (16, N_CMP)]),
                            spread(cmp_pos[r, v, 0:1], [(1, 16), (0, 2), (0, N_CMP)]), ALU.add)
                    ins.then_inc(cmp_blk, 1)

            def compressed_rows(l):
                dve.wait_ge(cmp_raw, l + 1)
                dve.tensor_copy(k_c2[0:32], spread(ps23[0:32, 0:1], [(0, 2), (1, HD)]))
                dve.tensor_copy(v_c[0:32], ps23[0:32, 512:576]).then_inc(cmp_tok, 1)

            def compressed_operands(l):
                dve.wait_ge(cmp_kv, l + 1)
                dve.tensor_tensor(k_bd, spread(ps23[:, 0:1], [(16, 2), (1, 16)]),
                                  spread(half_of[:, 0:1], [(1, 2), (0, 16)]), ALU.mult)
                dve.tensor_tensor(v_bd, spread(ps23[:, 512:513], [(0, 8), (1, HD)]),
                                  spread(head_of[:, 0:1], [(1, 8), (0, HD)]), ALU.mult).then_inc(cmp_kv_used, 1)

            def compressed_logits(l):
                dve.wait_ge(cmp_s, l + 1)
                lv = cmp_L.rearrange("p (t h n) -> p t h n", t=2, h=8)
                rows = cmp_L.rearrange("p (r n) -> p r n", n=16)
                done(dve.tensor_tensor(lv, ps7[:, 0:256].rearrange("p (t h n) -> p t h n", t=2, h=8),
                                       spread(cmp_mask[:, 0, 0:1], [(16, 2), (0, 8), (1, 16)]), ALU.add))
                done(dve.tensor_reduce(out=st[:, 0, 0:16], in_=rows, axis=AX, op=ALU.max))
                dve.tensor_tensor(rows, rows, spread(st[:, 0, 0:1], [(1, 16), (0, 16)]), ALU.subtract).then_inc(cmp_l, 1)

            def compressed_weights(l):
                rows = cmp_L.rearrange("p (r n) -> p r n", n=16)
                dve.wait_ge(cmp_p, l + 1)
                done(dve.tensor_reduce(out=st[:, 1, 0:16], in_=rows, axis=AX, op=ALU.add))
                done(dve.reciprocal(st[:, 2, 0:16], st[:, 1, 0:16]))
                co = cmp_w[:, 0:16].rearrange("p (t h) -> p t h", t=2)
                done(dve.tensor_tensor(spread(cmp_w[:, 0:1], [(8, 2), (1, 4), (4, 2)]),
                                       spread(st[:, 2, 0:1], [(8, 2), (2, 4), (1, 2)]),
                                       spread(gate_c[:, 0, 0:1], [(24, 2), (3, 4), (12, 2)]), ALU.mult))
                done(dve.tensor_tensor(co, co, spread(cmp_any[:, 0:1], [(1, 2), (0, 8)]), ALU.mult))

            def compressed_output(l):
                dve.wait_ge(cmp_o, l + 1)
                for t in range(TT):
                    ins = dve.tensor_tensor(y[:, t, 256:768].rearrange("p (h d) -> p h d", d=HD),
                                            (ps6, ps7)[t].rearrange("p (h d) -> p h d", d=HD),
                                            spread(cmp_w[:, 8 * t:8 * t + 1], [(1, 8), (0, HD)]), ALU.mult)
                ins.then_inc(cmp_o_used, 1)
                dve.wait_ge(cmp_o_used, l + 1)

            def hybrid(l):
                gemms(f"in{l}", 4)
                b = FIRST[f"in{l}"] + 4
                nsa_operands(l)
                dve.wait_ge(tanh_done, 2 * l + 1)
                gate_silu(l, 256, 512, COL["ng"])
                done(dve.tensor_scalar(gate_c[:, :, :], gate_c[:, :, :], 1.0, 0.25, ALU.add, ALU.mult))
                after_half(b, 0)
                compressed_rows(l)
                after_half(b, 1)
                compressed_operands(l)
                for half in range(2):
                    dve.wait_ge(acc_free[half], free_count(b) + 1)
                dve.wait_ge(consts_in, 16 * 8)
                rotate()
                after_half(b + 1, 0)
                compressed_logits(l)
                dve.wait_ge(stg_ps, STG0[l] + 8)
                dve.tensor_copy(ret_T[:, 2:4, :].rearrange("p c n -> p (c n)"), ps5[:, :]).then_inc(stg_d, 1)
                after_half(b + 1, 1)
                compressed_weights(l)
                decay_scores(l, (0, 1))
                dve.wait_ge(tanh_done, 2 * l + 2)
                done(gate_silu(l, 0, 256, COL["rg"]))
                after_half(b + 2, 0)
                compressed_output(l)
                decay_scores(l, (2, 3))
                if l == 0:
                    small_params()
                after_half(b + 2, 1)
                units(l, 16, {**{i: (lambda i=i: retention_norm(l, i)) for i in range(4)},
                              4: lambda: lru_conv(l, 0), 5: lambda: lru_conv(l, 1), 7: lambda: lru_gate(l),
                              9: lambda: lru_square(l), 11: lambda: lru_scan(l, 0), 12: lambda: lru_scan(l, 1),
                              14: lambda: lru_operand(l)})
                g = y[:, :, 256:768]
                dve.tensor_tensor(g, g, proj[:, :, COL["ng"]:COL["ng"] + 512], ALU.mult).then_inc(y_ready, 1)

            def lru_views():
                return [lru_w[:, i] for i in range(7)], [lru_w[:, i].rearrange("p c n -> p (c n)") for i in range(7)]

            def lru_conv(l, c):
                xc = lru_w[:, 0]
                w = conv_w[:, l, c]
                xv = lru_T[:, c, :]
                done(dve.tensor_scalar(xc[:, c, :], xv, w[:, 3:4], lru_v[:, l, 0, c:c + 1], ALU.mult, ALU.add))
                for s in (1, 2, 3):
                    ins = dve.scalar_tensor_tensor(out=xc[:, c, s:S], in0=xv[:, 0:S - s], scalar=w[:, 3 - s:4 - s],
                                                   in1=xc[:, c, s:S], op0=ALU.mult, op1=ALU.add)
                    if s < 3:
                        done(ins)
                ins.then_inc(lru_xc, 1)

            def lru_gate(l):
                (xc, th_r, *_), (xf, _, ti, _, _, _, tg) = lru_views()
                dve.wait_ge(lru_th, l + 1)
                for c in range(2):
                    ins = dve.tensor_scalar(th_r[:, c, :], th_r[:, c, :], 1.0, lru_sp[:, 2 * l + c:2 * l + c + 1], ALU.add, ALU.mult)
                ins.then_inc(lru_nla, 1)
                dve.scalar_tensor_tensor(out=ti, in0=ti, scalar=1.0, in1=xf, op0=ALU.add, op1=ALU.mult)
                done(dve.scalar_tensor_tensor(out=tg, in0=tg, scalar=1.0, in1=lru_T[:, 2:4, :].rearrange("p c n -> p (c n)"), op0=ALU.add, op1=ALU.mult))

            def lru_square(l):
                _, (_, _, _, af, tf, rf, _) = lru_views()
                dve.wait_ge(lru_at, l + 1)
                done(dve.tensor_tensor(rf, af, af, ALU.mult))
                dve.scalar_tensor_tensor(out=tf, in0=rf, scalar=1.0, in1=tf, op0=ALU.add, op1=ALU.mult).then_inc(lru_v2, 1)

            def lru_scan(l, c):
                (_, _, _, a, t, res, _), (_, _, ti, _, tf, rf, tg) = lru_views()
                if c == 0:
                    dve.wait_ge(lru_m, l + 1)
                    done(dve.scalar_tensor_tensor(out=tf, in0=tf, scalar=0.5, in1=ti, op0=ALU.mult, op1=ALU.mult))
                done(dve.tensor_tensor_scan(res[:, c, :], a[:, c, :], t[:, c, :], 0.0, ALU.mult, ALU.add))
                if c == 1:
                    dve.scalar_tensor_tensor(out=rf, in0=rf, scalar=0.5, in1=tg, op0=ALU.mult, op1=ALU.mult).then_inc(lru_y, 1)

            def lru_operand(l):
                _, (_, _, _, _, _, rf, _) = lru_views()
                dve.wait_ge(at_hi, ACT0[2 * l + 1] + 1)
                dve.wait_ge(lru_y, l + 1)
                dve.tensor_tensor(act_lo[:, 6:8, :].rearrange("p c n -> p (c n)"), rf,
                                  act_hi[:, 6:8, :].rearrange("p c n -> p (c n)").bitcast(F), ALU.subtract).then_inc(at_lo, 1)

            def layer_norm(l):
                for half in range(2):
                    dve.wait_ge(acc_free[half], free_count(last_block[f"out{l}"]) + 1)
                for t in range(TT):
                    for i in range(2):
                        ins = dve.bn_stats(bn[:, t, 6 * i:6 * i + 6], x[:, t, 512 * i:512 * i + 512])
                done(ins)
                for t in range(TT):
                    ins = dve.bn_aggr(mv[:, t, :], bn[:, t, :])
                done(ins)
                rsqrt(mv[:, :, 1], 1.0, 1e-5, st[:, 1, 0:2])
                for t in range(TT):
                    ins = dve.tensor_scalar(x[:, t, :], x[:, t, :], mv[:, t, 0:1], st[:, 1, t:t + 1], ALU.subtract, ALU.mult)
                done(ins)
                dve.wait_ge(ln_in, 32 * (l + 1))
                done(dve.tensor_tensor(x[:, :, :], x[:, :, :], spread(ln_v[:, 0, 0:1], [(0, 2), (1, D)]), ALU.mult))
                dve.tensor_tensor(x[:, :, :], x[:, :, :], spread(ln_v[:, 1, 0:1], [(0, 2), (1, D)]), ALU.add).then_inc(x_new, 1)

            def rms(i):
                dve.wait_ge(ssq_done, i + 1)
                rsqrt(st[:, 0, 0:2], 1.0 / D, 1e-6, st[:, 1, 0:2], lambda ins: ins.then_inc(rstd_done, 1))

            dve.memset(st[:, :, :], 0.0)
            acts_lo(X0, KD)
            for c in range(CHUNK0[AHEAD - 1] + 1):
                split_lo(c)
            for l in range(LAYERS):
                if l:
                    acts_lo(X1, KD)
                hybrid(l)
                acts_lo(2 * l + 1, 6)
                gemms(f"out{l}")
                layer_norm(l)
            rms(0)
            acts_lo(DSW_U, KD, gain=0)
            gemms("dsw")
            units(2, DSW_HEADS)
            acts_lo(DSW_Y, 4)
            gemms("dswo")
            rms(1)
            acts_lo(FFN0_U, KD, gain=2)
            gemms("up0")
            gemms("down0")
            rms(2)
            acts_lo(MOBA_U, KD, gain=1)
            gemms("moba")
            units(3, MOBA_HEADS)
            acts_lo(MOBA_Y, KD)
            gemms("mobao")
            rms(3)
            acts_lo(FFN1_U, KD, gain=3)
            gemms("up1")
            gemms("down1")


def kernel(**inputs):
    import concourse.bacc as bacc
    from concourse.bass_utils import run_bass_kernel_spmd

    nc = bacc.Bacc("TRN2", target_bir_lowering=False, num_devices=1)
    arrays, dram = {}, {}
    for name, a in [(n, inputs[n]) for n in PARAMS] + list(shape_constants().items()):
        a = np.ascontiguousarray(a)
        arrays[f"in_{name}"] = a
        dram[name] = nc.dram_tensor(f"in_{name}", a.shape, mybir.dt.from_np(a.dtype), kind="ExternalInput").ap()
    out = nc.dram_tensor("out_0", (1, S, D), mybir.dt.float32, kind="ExternalOutput").ap()
    build(nc, dram, out)
    r = run_bass_kernel_spmd(nc, [arrays], core_ids=[0])
    return r.results[0]["out_0"]
```

```python
import math
from contextlib import ExitStack

import numpy as np

import concourse.bass as bass
from concourse import mybir

S = 256
TT = S // 128
D = 1024
KD = D // 128
HD = 64
LAYERS = 2
D_IN = 3352
D_FF = 4096
RET_HEADS, NSA_HEADS, NSA_GROUPS, DSW_GROUPS, DSW_HEADS, MOBA_HEADS = 4, 8, 2, 3, 8, 16
N_CMP = 15
ALPHA = (2.0 * LAYERS) ** 0.25
NEG = -1.0e30
COL = dict(rq=0, rk=256, rv=512, rg=768, nq=1024, nkc=1536, nvc=1664, nks=1792, nvs=1920,
           nkw=2048, nvw=2176, ng=2304, ngl=2816, lx=2840, lg=3096)

PARAMS = ["x", "w_in", "w_out", "ln_g", "ln_b", "nsa_cmp_pos", "nsa_cmp_w", "lru_conv_w", "lru_conv_b",
          "lru_w_a", "lru_b_a", "lru_w_x", "lru_b_x", "lru_lambda", "rel_bias_2", "norm_mix_2",
          "norm_ffn_2", "a_w_qkv_2", "a_q_gain_2", "a_k_gain_2", "a_w_o_2", "b_w_qkv_2", "b_q_gain_2",
          "b_k_gain_2", "b_w_o_2", "ffn_w1_2", "ffn_w2_2"]


def shape_constants():
    half = HD // 2
    inv = (1.0 / (10000.0 ** (np.arange(half, dtype=np.float32) / half))).astype(np.float32)
    ang = (np.arange(S, dtype=np.float32)[:, None] * inv[None, :]).astype(np.float32)
    rope = np.stack([np.cos(ang.astype(np.float64)), np.sin(ang.astype(np.float64))])
    rope = rope.reshape(2, TT, 128, half).transpose(2, 0, 1, 3)
    p, c = np.arange(128)[:, None], np.arange(S)[None, :]
    decay = np.zeros((128, RET_HEADS, S))
    for h in range(RET_HEADS):
        decay[:, h] = np.where(c >= p, (1.0 - 2.0 ** (-5.0 - h)) ** np.maximum(c - p, 0) * HD ** -0.5, 0.0)
    causal = np.where(c <= 128 + p, 0.0, NEG)
    tok = np.arange(S)
    seen = (np.arange(16)[None, :] * 16 + 31 <= tok[:, None]) & (np.arange(16)[None, :] < N_CMP)
    cmp_mask = np.where(seen, 0.0, NEG).reshape(TT, 128, 16).transpose(1, 0, 2)
    cmp_any = seen.any(1).reshape(TT, 128).T
    row = np.arange(128)
    head_of = (row // 16 % 2 * 4 + row // 32)[:, None] == np.arange(8)[None, :]
    rep = np.arange(32)[:, None] == (row % 32)[None, :]
    half_of = (np.arange(128)[:, None] // 64 == np.arange(2)[None, :])
    dist = np.arange(384) - 127
    n = np.maximum(dist, 1)
    large = 16 + (np.log(n / 16) / math.log(2048 / 16) * 16).astype(np.int64)
    bucket = np.where(dist < 16, np.maximum(dist, 0), np.minimum(large, 31))
    hot = np.zeros((33, 4, 384))
    for kind, ok in enumerate([(dist >= 0) & (dist <= 128), (dist >= 0) & (dist % 4 == 0),
                               (dist >= 0) & (dist % 16 == 0), dist >= 0]):
        hot[bucket, kind, np.arange(384)] = 1.0
        hot[32, kind] = np.where(ok, 0.0, NEG)
    f = lambda a: np.ascontiguousarray(a, dtype=np.float32)
    return {"c_rope": f(rope), "c_decay": f(decay), "c_causal": f(causal), "c_cmp_mask": f(cmp_mask),
            "c_cmp_any": f(cmp_any), "c_head_of": f(head_of), "c_half_of": f(half_of), "c_hot": f(hot),
            "c_ident": f(np.eye(128)), "c_rep": f(rep)}


def build(nc, dram, out):
    F = mybir.dt.float32
    FR = mybir.dt.float32r
    I32 = mybir.dt.int32
    ALU = mybir.AluOpType
    ACT = mybir.ActivationFunctionType
    AX = mybir.AxisListType.X

    BLOCKS = []
    FIRST = {}

    def add_blocks(name, w, row0, rows, col_list, form, use):
        FIRST.setdefault(name, len(BLOCKS))
        for c0, n in col_list:
            BLOCKS.append(dict(w=w, row0=row0, kts=rows // 128, c0=c0, n=n, form=form, use=use,
                               first=True, last=True, act0=0, name=name))

    IN_COLS = [(COL["nq"], 512), (COL["nkc"], 512), (2560, COL["lx"] - 2560), (COL["nkw"], 512),
               (COL["rq"], 512), (COL["rv"], 512)]
    for l in range(LAYERS):
        w = dram["w_in"][l]
        add_blocks(f"in{l}", w, 0, D, IN_COLS, "tok", "proj")
        add_blocks(f"in{l}", w, 0, D, [(COL["lx"], 512)], "feat", "lru")
        add_blocks(f"out{l}", dram["w_out"][l], 0, D, [(0, 512), (512, 512)], "tok", "deepnorm")

    def add_ffn(l):
        add_blocks(f"up{l}", dram["ffn_w1_2"][l], 0, D, [(512 * i, 512) for i in range(8)], "feat", "relu2")
        FIRST[f"down{l}"] = len(BLOCKS)
        for c in range(2):
            for k in range(4):
                BLOCKS.append(dict(w=dram["ffn_w2_2"][l], row0=k * D, kts=8, c0=512 * c, n=512, form="tok",
                                   use="residual", first=k == 0, last=k == 3, act0=8 * k, name=f"down{l}"))

    add_blocks("dsw", dram["a_w_qkv_2"][0], 0, D, [(512 * i, 512) for i in range(6)], "tok", "qk")
    add_blocks("dsw", dram["a_w_qkv_2"][0], 0, D, [(512 * i, 512) for i in range(6, 9)], "tok", "proj")
    add_blocks("dswo", dram["a_w_o_2"][0], 0, 512, [(0, 512), (512, 512)], "tok", "residual")
    add_ffn(0)
    add_blocks("moba", dram["b_w_qkv_2"][0], 0, D, [(512 * i, 512) for i in range(4)], "tok", "qk")
    add_blocks("moba", dram["b_w_qkv_2"][0], 0, D, [(512 * i, 512) for i in range(4, 6)], "tok", "proj")
    add_blocks("mobao", dram["b_w_o_2"][0], 0, D, [(0, 512), (512, 512)], "tok", "residual")
    add_ffn(1)
    NB = len(BLOCKS)
    CHUNKS = [(b, j) for b in range(NB) for j in range(BLOCKS[b]["kts"] // 4)]
    CHUNK0 = [sum(x["kts"] // 4 for x in BLOCKS[:b]) for b in range(NB + 1)]
    RAW = 3
    AHEAD = 2

    ACTS = [8, 8, 8, 8, 8, 4, 8, 8, 8, 8]
    X0, Y0, X1, Y1, DSW_U, DSW_Y, FFN0_U, MOBA_U, MOBA_Y, FFN1_U = range(10)
    LRU_CHUNK = [0, 1, 0, 1, 0, 0, 0, 0, 0, 0]
    ACT0 = [sum(ACTS[:i]) // 2 for i in range(11)]

    TRANS0 = [sum(n // 2 - c for n, c in zip(ACTS[:i], LRU_CHUNK)) for i in range(10)]

    UNIT0 = [0, 16, 32, 40]
    PCH0 = [0, 16, 32, 56]
    STG0 = [0, 8, 16, 32]

    def empties(ph, u, g):
        if ph < 2:
            return "d" if u in (7, 9, 11) else "a"
        return "ad"[g % 2 if ph == 2 else u % 2]

    ORDER = [(ph, u, g) for ph, n, parts in ((0, 16, 1), (1, 16, 1), (2, 8, 3), (3, 16, 1))
             for u in range(n) for g in range(parts)]
    EMPTIED = {c: (empties(*c), 1 + sum(empties(*o) == empties(*c) for o in ORDER[:i])) for i, c in enumerate(ORDER)}

    def emptied_by(ph, u, g):
        return EMPTIED[ph, u, g]

    ctx = ExitStack()
    with ctx:
        def sb(name, shape, dt=F):
            return ctx.enter_context(nc.sbuf_tensor(name, shape, dt))

        def sem(name):
            return ctx.enter_context(nc.semaphore(name))

        x = sb("x_res", [128, TT, D])
        y = sb("y_tok", [128, TT, D])
        act_hi = sb("act_hi", [128, KD, S], FR)
        act_lo = sb("act_lo", [128, KD, S], FR)
        w_raw = sb("w_raw", [128, RAW, 4, 512])
        w_hi = sb("w_hi", [128, AHEAD, 8, 512], FR)
        w_lo = sb("w_lo", [128, AHEAD, 8, 512], FR)
        ident = sb("ident", [128, 128])
        rope = sb("rope", [128, 2, TT, HD // 2])
        decay = sb("decay", [128, RET_HEADS, S])
        causal = sb("causal", [128, S])
        cmp_mask = sb("cmp_mask", [128, TT, 16])
        cmp_any = sb("cmp_any", [128, TT])
        head_of = sb("head_of", [128, 8])
        half_of = sb("half_of", [128, 2])
        rep = sb("rep", [32, 128])
        norm_g = sb("norm_g", [128, 4, KD])
        qk_g = sb("qk_g", [128, 4])
        qk_gain = sb("qk_gain", [128, 2])
        conv_w = sb("conv_w", [128, LAYERS, 2, 4])
        lru_v = sb("lru_v", [128, LAYERS, 4, 2])
        lru_hb = sb("lru_hb", [128, LAYERS, 2, 2])
        lru_sp = sb("lru_sp", [128, LAYERS * 2])
        lam_exp = sb("lam_exp", [128, LAYERS * 2])
        lam_p = sb("lam_p", [128, 4, LAYERS * 2])
        rstd = sb("rstd", [128, 2, TT])
        bn = sb("bn", [128, TT, 12])
        mv = sb("mv", [128, TT, 2])
        gate_w = sb("gate_w", [128, LAYERS, 2, 2, 128])
        relb = sb("relb", [33, 24])
        st = sb("st", [128, 8, 16])
        cmp_w = sb("cmp_weights", [128, 16])
        ttr = sb("ttr_min", [128, 2, TT])
        den = sb("den", [128, 16, TT])
        rms_sum = sb("rms_sum", [128, TT])
        rden = sb("rden", [128, 4, TT])
        gate_c = sb("gate_c", [128, TT, 24])
        AREA = 19008
        with nc.sbuf_tensor("area", [128, AREA], F) as area:
            pass
        hid = ctx.enter_context(nc.sbuf_tensor("hid", [128, 2, 32, S], FR))
        early_acts = sb("early_acts", [128, 2, 4, S], FR)
        sb("area_rest", [128, AREA - 16384 - 2048])
        h_hi, h_lo = hid[:, 0], hid[:, 1]

        def cut(at, n, pattern=None, **sizes):
            v = area[:, at:at + n]
            return v.rearrange(pattern, **sizes) if pattern else v

        proj = cut(0, TT * 2840, "p (t n) -> p t n", t=TT)
        R = TT * 2840
        rot = cut(R, 1024, "p (t n) -> p t n", t=TT)
        rot_b = cut(R + 1024, 1024, "p (t n) -> p t n", t=TT)
        ret_T = cut(R + 2048, 1024, "p (c n) -> p c n", c=4)
        ret_P = cut(R + 3072, 1536, "p (h n) -> p h n", h=4)
        lru_w = cut(R, 3584, "p (k c n) -> p k c n", k=7, c=2)
        R += 4608
        nT = cut(R, 3072, "p (c n) -> p c n", c=12)
        R += 3072
        blk = cut(R, 1024, "p (v m n) -> p v m n", v=2, m=16)
        R += 1024
        cw = cut(R, 2048, "p (v m n) -> p v m n", v=2, m=16)
        R += 2048
        lru_T = cut(R, 1024, "p (c n) -> p c n", c=4)
        R += 1024
        nsa_P = cut(R, 768, "p (s n) -> p s n", s=2)
        R += 768
        k_dup = cut(R - 768, 1024, "p (v t g n) -> p v t g n", v=2, t=2, g=2)
        nsa_PT = cut(R, 768, "p (s n) -> p s n", s=2)
        assert R + 768 <= AREA
        BLK, CW, LRU_T = R - 4864, R - 3840, R - 1792
        v_bd = cut(BLK, 512, "p (h n) -> p h n", h=8)
        k_bd = cut(BLK + 512, 32, "p (g n) -> p g n", g=2)
        k_c2 = cut(BLK + 544, 128, "p (c n) -> p c n", c=2)
        v_c = cut(BLK + 672, 64)
        cmp_L = cut(BLK + 736, 256)
        tmp_tok = cut(CW, 1024)
        o_part = cut(CW + 1024, 512)
        cmp_PT = cut(CW + 1536, 256)
        cmp_pos = cut(LRU_T, 32, "p (v m) -> p v m", v=2)
        ln_v = cut(10240, 2048, "p (v n) -> p v n", v=2)
        ln_f = cut(12288, 16, "p (v k) -> p v k", v=2)
        ln_fs = cut(12304, 16, "p (v k) -> p v k", v=2)
        qkv = cut(0, 9216, "p (t n) -> p t n", t=TT)
        sq = [cut(at, 1024, "p (t n) -> p t n", t=TT) for at in (9216, 13312)]
        stage = cut(10240, 3072, "p (s c n) -> p s c n", s=2, c=6)
        big_P = cut(13312, 2304, "p (s n) -> p s n", s=2)
        big_PT = cut(15616, 1536, "p (s n) -> p s n", s=4)
        bias_T = cut(17152, 1536, "p (s n) -> p s n", s=2)
        hot = cut(TT * 2840 + 4608, 1536, "p (k n) -> p k n", k=4)
        vec = cut(TT * 2840 + 6144, 1536, "p (k n) -> p k n", k=4)

        ps = [ctx.enter_context(nc.psum_tensor(f"ps{i}", [128, 512], F)) for i in (0, 1)]
        ps23 = ctx.enter_context(nc.psum_tensor("ps23", [128, 1024], F))
        ps4, ps5, ps6, ps7 = [ctx.enter_context(nc.psum_tensor(f"ps{i}", [128, 512], F)) for i in (4, 5, 6, 7)]
        tr_bank = [ps4, ps5]
        nsa_bank = [ps4, ps5, ps23[:, 0:512], ps23[:, 512:1024], ps6, ps5]
        act_bank = [ps4, ps5, ps23[:, 0:512], ps23[:, 512:1024]]
        bias_vec = nc.dram_tensor("bias_vec", [4, 16, 384], F, kind="Internal").ap()

        w_arrived = [sem(f"w_arrived{i}") for i in range(RAW)]
        w_hi_done = sem("w_hi_done")
        w_lo_done = sem("w_lo_done")
        acc_ready = sem("acc_ready")
        acc_free = [sem("acc_free0"), sem("acc_free1")]
        consts_in = sem("consts_in")
        ident_in = sem("ident_in")
        x_in = [sem("x_in0"), sem("x_in1")]
        hot_in = sem("hot_in")
        gatew_zero = sem("gatew_zero")
        relb_in = sem("relb_in")
        relb_one = sem("relb_one")
        cw_in = sem("cw_in")
        ln_in = sem("ln_in")
        y_ready = sem("y_ready")
        ln_norm = sem("ln_norm")
        ln_fs_done = sem("ln_fs_done")
        at_ps = sem("at_ps")
        at_hi = sem("at_hi")
        at_lo = sem("at_lo")
        vec_ps = sem("vec_ps")
        vec_sb = sem("vec_sb")
        vec_out = sem("vec_out")
        bias_in = [sem("bias_in0"), sem("bias_in1")]
        stg_ps = sem("stg_ps")
        stg_a = sem("stg_a")
        stg_d = sem("stg_d")
        rot_done = sem("rot_done")
        rs_ps = sem("rs_ps")
        rs_sb = sem("rs_sb")
        ro_ps = sem("ro_ps")
        ro_used = sem("ro_used")
        tanh_done = sem("tanh_done")
        cmp_blk = sem("cmp_blk")
        k_dup_done = sem("k_dup_done")
        cmp_raw = sem("cmp_raw")
        cmp_tok = sem("cmp_tok")
        cmp_kv = sem("cmp_kv")
        cmp_kv_used = sem("cmp_kv_used")
        cmp_s = sem("cmp_s")
        cmp_l = sem("cmp_l")
        cmp_p = sem("cmp_p")
        cmp_t = sem("cmp_t")
        cmp_pt = sem("cmp_pt")
        cmp_o = sem("cmp_o")
        cmp_o_used = sem("cmp_o_used")
        s_ready = sem("s_ready")
        ttr_done = sem("ttr_done")
        p_ready = sem("p_ready")
        t_ready = sem("t_ready")
        pt_a = sem("pt_a")
        pt_d = sem("pt_d")
        o_ready = sem("o_ready")
        o_free = sem("o_free")
        lru_x = sem("lru_x")
        lru_xc = sem("lru_xc")
        lru_z = sem("lru_z")
        lru_th = sem("lru_th")
        lru_nla = sem("lru_nla")
        lru_at = sem("lru_at")
        lru_v2 = sem("lru_v2")
        lru_m = sem("lru_m")
        lru_y = sem("lru_y")
        h_done = sem("h_done")
        hh_done = sem("hh_done")
        hl_done = sem("hl_done")
        qk_norm = sem("qk_norm")
        ssq_done = sem("ssq_done")
        rstd_done = sem("rstd_done")
        x_new = sem("x_new")
        out_done = sem("out_done")
        lam_abs = sem("lam_abs")
        lam_e = sem("lam_e")
        dve_step = sem("dve_step")
        small_in = sem("small_in")

        Y_OF = [Y0, Y1, DSW_Y, MOBA_Y]

        NEEDS = {"in0": X0, "out0": Y0, "in1": X1, "out1": Y1, "dsw": DSW_U, "dswo": DSW_Y,
                 "up0": FFN0_U, "moba": MOBA_U, "mobao": MOBA_Y, "up1": FFN1_U}

        def y_bank(i):
            return (ps23[:, 0:512], ps23[:, 512:1024], ps4, ps5)[i]

        def bank_of(a, i):
            return y_bank(i) if a in (Y0, Y1, DSW_Y, MOBA_Y) else act_bank[i]

        def t_bank(ph, u, g):
            return (ps4, ps5, ps[0])[g] if ph == 2 else tr_bank[u % 2]

        def stage_plan(ph, p):
            first = p < 2
            b23 = (ps4, ps5) if first else (ps[0], ps[1])
            if ph == 3:
                return [(b23[c], [0], c) for c in range(2)]
            return [(tr_bank[c], [0, 1], c) for c in range(2)] + [(b23[c], [2], c) for c in range(2)]

        AFTER = {"dswo": FFN0_U, "down0": MOBA_U, "mobao": FFN1_U}
        USED_BY = ["in0", "out0", "in1", "out1", "dsw", "dswo", "up0", "moba", "mobao", "up1"]
        last_block = {}
        for b, d in enumerate(BLOCKS):
            last_block[d["name"]] = b

        def blocks(name):
            return range(FIRST[name], last_block[name] + 1)

        def free_count(b):
            return sum(d["last"] for d in BLOCKS[:b])

        BIAS_BLOCK = 1
        def split_after(b, half):
            nxt = b + (AHEAD if half else AHEAD - 1)
            j = 1 - half
            return [CHUNK0[nxt] + j] if nxt < NB and j < BLOCKS[nxt]["kts"] // 4 else []

        HIDDEN0 = {0: 0, 1: 16}

        block = ctx.enter_context(nc.Block())

        @block.sync
        def _(sp):
            for c, (b, j) in enumerate(CHUNKS):
                d = BLOCKS[b]
                if c >= RAW:
                    sp.wait_ge(w_lo_done, c - RAW + 1)
                r0 = d["row0"] + 512 * j
                src = d["w"][r0:r0 + 512, d["c0"]:d["c0"] + d["n"]].rearrange("(k p) n -> p k n", p=128)
                sp.dma_start(w_raw[:, c % RAW, :, 0:d["n"]], src).then_inc(w_arrived[c % RAW], 16)
            for half in range(2):
                sp.wait_ge(acc_free[half], free_count(NB))
            sp.dma_start(out[0].rearrange("(t p) d -> p t d", p=128), x[:, :, :]).then_inc(out_done, 16)
            sp.wait_ge(out_done, 16)

        @block.gpsimd
        def _(pool):
            def compression_operands(l):
                if l:
                    pool.wait_ge(y_ready, 2 * l)
                    pool.wait_ge(lru_y, l)
                for v in range(2):
                    pool.dma_start(cw[:, v], dram["nsa_cmp_w"][l, v].rearrange("(m q) e -> q m e", q=128)).then_inc(cw_in, 16)
                for v in range(2):
                    for e in range(2):
                        pool.dma_start(cmp_pos[64 * e:64 * e + 64, v, :],
                                       dram["nsa_cmp_pos"][l, v].rearrange("(m e) d -> e d m", e=2)[e]).then_inc(cw_in, 16)
                b = FIRST[f"in{l}"] + 1
                for half in range(2):
                    pool.wait_ge(acc_free[half], free_count(b) + 1)
                pool.wait_ge(relb_one, 1)
                for v in range(2):
                    c0 = COL[("nkc", "nvc")[v]]
                    for e in range(2):
                        ins = pool.tensor_copy(k_dup[:, v, :, :, 64 * e:64 * e + 64],
                                               proj[:, :, c0:c0 + 128].rearrange("p t (g d) -> p t g d", g=2))
                ins.then_inc(k_dup_done, 1)

            pool.dma_start(ident[:, :], dram["c_ident"]).then_inc(ident_in, 16)
            pool.memset(gate_w[:, :, :, :, :], 0.0).then_inc(gatew_zero, 1)
            pool.wait_ge(gatew_zero, 1)
            pool.memset(relb[32:33, :], 1.0).then_inc(relb_one, 1)
            with nc.allow_non_contiguous_dma(reason="vectors of one element per partition"):
                pool.dma_start(hot[0:33], dram["c_hot"]).then_inc(hot_in, 16)
                pool.dma_start(relb[0:32, :], dram["rel_bias_2"]).then_inc(relb_in, 16)
                for dst, src in ((rope, "c_rope"), (decay, "c_decay"),
                                 (causal, "c_causal"), (cmp_mask, "c_cmp_mask"), (cmp_any, "c_cmp_any"),
                                 (head_of, "c_head_of"), (half_of, "c_half_of"), (rep, "c_rep")):
                    n = len(dst.shape)
                    pool.dma_start(dst[tuple([slice(None)] * n)], dram[src]).then_inc(consts_in, 16)
                compression_operands(0)
                pool.wait_ge(vec_sb, 1)
                pool.dma_start(bias_vec[0:3, 0:8].rearrange("k h m -> h k m"), vec[0:8, 0:3, :]).then_inc(vec_out, 16)
                pool.dma_start(bias_vec[3, 0:16], vec[0:16, 3, :]).then_inc(vec_out, 16)
                for l in range(LAYERS):
                    for c in range(2):
                        pool.dma_start(conv_w[:, l, c], dram["lru_conv_w"][l, :, 128 * c:128 * c + 128].rearrange("k p -> p k")).then_inc(small_in, 16)
                    for i, nm in enumerate(("lru_conv_b", "lru_b_a", "lru_b_x", "lru_lambda")):
                        pool.dma_start(lru_v[:, l, i], dram[nm][l].rearrange("(c p) -> p c", p=128)).then_inc(small_in, 16)
                    pool.dma_start(norm_g[:, l], dram["norm_mix_2"][l].rearrange("(c p) -> p c", p=128)).then_inc(small_in, 16)
                    pool.dma_start(norm_g[:, 2 + l], dram["norm_ffn_2"][l].rearrange("(c p) -> p c", p=128)).then_inc(small_in, 16)
                for i, nm in enumerate(("a_q_gain_2", "a_k_gain_2", "b_q_gain_2", "b_k_gain_2")):
                    for e in range(2):
                        pool.dma_start(qk_g[64 * e:64 * e + 64, i:i + 1], dram[nm][0].rearrange("(p o) -> p o", o=1)).then_inc(small_in, 16)
                pool.wait_ge(gatew_zero, 1)
                for l in range(LAYERS):
                    for i, nm in enumerate(("lru_w_a", "lru_w_x")):
                        for n in range(4):
                            e = n % 2
                            pool.dma_start(gate_w[64 * e:64 * e + 64, l, i, n // 2, 64 * e:64 * e + 64],
                                           dram[nm][l, n]).then_inc(small_in, 16)
                for l in range(LAYERS):
                    if l:
                        compression_operands(l)
                    pool.wait_ge(y_ready, 2 * l + 2)
                    for i, nm in enumerate(("ln_g", "ln_b")):
                        pool.dma_start(ln_v[:, i, :], dram[nm][l].partition_broadcast(128)).then_inc(ln_in, 16)
                        pool.dma_start(ln_f[:, i, :], dram[nm][l].rearrange("(c p) -> p c", p=128)).then_inc(ln_in, 16)
                for u in range(DSW_HEADS + MOBA_HEADS):
                    g = UNIT0[2] + u
                    if u < 2:
                        pool.wait_ge(x_new, TT * LAYERS)
                        pool.wait_ge(vec_out, 32)
                    elif u == DSW_HEADS or u == DSW_HEADS + 1:
                        for half in range(2):
                            pool.wait_ge(acc_free[half], free_count(FIRST["moba"]))
                    else:
                        pool.wait_ge(ttr_done, g - 2 + 1)
                    if u < DSW_HEADS:
                        src = bass.AP(bias_vec.tensor, u * 384, [[1, 128], [16 * 384, 3], [1, S]])
                        dst = bias_T[:, u % 2, :].rearrange("p (g n) -> p g n", g=3)
                    else:
                        src = bass.AP(bias_vec.tensor, (3 * 16 + u - DSW_HEADS) * 384, [[1, 128], [1, S]])
                        dst = bias_T[:, u % 2, 0:S]
                    pool.dma_start(dst, src).then_inc(bias_in[u % 2], 16)

        SMALL = 16 * (LAYERS * 8 + 8 + LAYERS * 8)

        @block.tensor
        def _(pe):
            def operand(b, half, k):
                name = BLOCKS[b]["name"]
                if name.startswith("down") and half == 0:
                    pe.wait_ge(hl_done, HIDDEN0[int(name[-1])] + (BLOCKS[b]["act0"] + k) // 2 + 1)
                elif name in ("in1", "dsw") and b == FIRST[name]:
                    pe.wait_ge(at_lo, ACT0[NEEDS[name]] + 2 * half + k // 4 + 1)
                elif b == FIRST[name] and half == 0:
                    a = NEEDS[name]
                    pe.wait_ge(at_lo, min(ACT0[a] + LRU_CHUNK[a] + k // 2 + 1, ACT0[a + 1]))

            def gemm(b, halves=(0, 1), midway=None, at=4):
                d = BLOCKS[b]
                slot, n = b % AHEAD, d["n"]
                hidden = d["name"].startswith("down")
                for half in halves:
                    bank = ps[half]
                    if d["first"] and free_count(b):
                        pe.wait_ge(acc_free[half], free_count(b))
                    if d["form"] == "tok":
                        for k in range(d["kts"]):
                            if half == 0 and k == at and midway:
                                midway()
                            if half == 0 and k % 4 == 0:
                                pe.wait_ge(w_lo_done, CHUNK0[b] + k // 4 + 1)
                            if k % 2 == 0:
                                operand(b, half, k)
                            if hidden:
                                ah = h_hi[:, d["act0"] + k, 128 * half:128 * half + 128]
                                al = h_lo[:, d["act0"] + k, 128 * half:128 * half + 128]
                            else:
                                ah = act_hi[:, k, 128 * half:128 * half + 128]
                                al = act_lo[:, k, 128 * half:128 * half + 128]
                            wh, wl = w_hi[:, slot, k, 0:n], w_lo[:, slot, k, 0:n]
                            first = d["first"] and k == 0
                            last = d["last"] and k == d["kts"] - 1
                            pe.matmul(bank[:, 0:n], ah, wh, start=first, stop=False)
                            pe.matmul(bank[:, 0:n], ah, wl, start=False, stop=False)
                            mm = pe.matmul(bank[:, 0:n], al, wh, start=False, stop=last)
                    else:
                        for f in (2 * half, 2 * half + 1):
                            o = bank[:, (f % 2) * S:(f % 2) * S + S]
                            cols = slice(128 * f, 128 * f + 128)
                            if f == 3 and midway and at > 4:
                                midway()
                            for k in range(d["kts"]):
                                if f == 0 and k == at and midway:
                                    midway()
                                if f == 0 and k % 4 == 0:
                                    pe.wait_ge(w_lo_done, CHUNK0[b] + k // 4 + 1)
                                if f == 0 and k % 2 == 0:
                                    operand(b, 0, k)
                                wh, wl = w_hi[:, slot, k, cols], w_lo[:, slot, k, cols]
                                early = k < 4 and d["use"] == "relu2"
                                ah = early_acts[:, 0, k, :] if early else act_hi[:, k, :]
                                al = early_acts[:, 1, k, :] if early else act_lo[:, k, :]
                                pe.matmul(o, wh, ah, start=k == 0, stop=False)
                                pe.matmul(o, wh, al, start=False, stop=False)
                                mm = pe.matmul(o, wl, ah, start=False, stop=k == d["kts"] - 1)
                    mm.then_inc(acc_ready, 1)

            def gemms(name, count=None, midway=None, at=4, between=None):
                for b in blocks(name)[:count]:
                    if name in ("in1", "dsw") and b == FIRST[name]:
                        gemm(b, midway=lambda: normalized_acts((name == "dsw") * 1, 1), at=4)
                    elif between and b == last_block[name]:
                        gemm(b, [0])
                        between()
                        gemm(b, [1])
                    elif name in AFTER and b == last_block[name]:
                        gemm(b, [0])
                        residual_acts(name, 0)
                        gemm(b, [1])
                    else:
                        gemm(b, midway=midway if b == FIRST[name] else None, at=at)
                    if b == BIAS_BLOCK:
                        bias_vectors()

            def bias_vectors():
                pe.wait_ge(hot_in, 16)
                pe.wait_ge(relb_in, 16)
                pe.wait_ge(relb_one, 1)
                for k in range(4):
                    cols = slice(8 * k, 8 * k + 8) if k < 3 else slice(0, 16)
                    o = (ps23[:, 0:512], ps23[:, 512:1024], ps6, ps7)[k]
                    mm = pe.matmul(o[0:8 if k < 3 else 16, 0:384], relb[:, cols], hot[0:33, k, :], start=True, stop=True)
                mm.then_inc(vec_ps, 1)

            def residual_acts(name, part):
                for t in range(TT):
                    pe.wait_ge(acc_free[t], free_count(last_block[name]) + part)
                    for i in (2 * part, 2 * part + 1):
                        for k in (0, 1):
                            mm = pe.transpose(act_bank[i][:, 128 * (2 * k + t):128 * (2 * k + t) + 128],
                                              x[:, t, 128 * (2 * i + k):128 * (2 * i + k) + 128], ident[:, :])
                        if t == TT - 1:
                            mm.then_inc(at_ps, 1)

            def normalized_acts(l, t):
                pe.wait_ge(ln_norm, TT * l + t + 1)
                for k in range(KD):
                    mm = pe.transpose(act_bank[2 * t + k // 4][:, 128 * (k % 4):128 * (k % 4) + 128],
                                      x[:, t, 128 * k:128 * k + 128], ident[:, :])
                    if k % 4 == 3:
                        mm.then_inc(at_ps, 1)

            def transpose_acts(a, src, kts, chunks=None):
                for i in range(kts // 2) if chunks is None else chunks:
                    if a == X0 and i % 2 == 0:
                        pe.wait_ge(x_in[i // 2], 16)
                    if a in (Y0, Y1):
                        pe.wait_ge(y_ready, 2 * (a == Y1) + (2 if i == 2 else 1))
                    if a in (DSW_Y, MOBA_Y):
                        pe.wait_ge(o_free, UNIT0[2 if a == DSW_Y else 3] // 4 + i + 1)
                    for q in range(4):
                        k, t = 2 * i + q // 2, q % 2
                        mm = pe.transpose(bank_of(a, i)[:, 128 * q:128 * q + 128],
                                          src[:, t, 128 * k:128 * k + 128], ident[:, :])
                    mm.then_inc(at_ps, 1)

            def retention_transposes(l):
                pe.wait_ge(rot_done, l + 1)
                for c in range(2):
                    for q in range(4):
                        p, t = q // 2, q % 2
                        mm = pe.transpose(tr_bank[c][:, 128 * q:128 * q + 128],
                                          rot[:, t, 256 * c + 128 * p:256 * c + 128 * p + 128], ident[:, :])
                    mm.then_inc(stg_ps, 1)

            def retention_scores(l, heads):
                pe.wait_ge(stg_a, STG0[l] // 2 + 4)
                pe.wait_ge(stg_d, STG0[l] // 2 + 4)
                for h in heads:
                    p, e = h // 2, 64 * (h % 2)
                    q = ret_T[e:e + 64, p, :]
                    k = ret_T[e:e + 64, 2 + p, :]
                    o = ps23[:, 512 * (h % 2):512 * (h % 2) + 384]
                    if h >= 2:
                        pe.wait_ge(rs_sb, RET_HEADS * l + h - 1)
                    pe.matmul(o[:, 0:S], k[:, 0:128], q[:, :], start=True, stop=True)
                    pe.matmul(o[:, S:384], k[:, 128:256], q[:, 128:256], start=True, stop=True).then_inc(rs_ps, 1)

            def retention_output(l):
                pe.wait_ge(cmp_o_used, l + 1)
                for h in range(RET_HEADS):
                    pe.wait_ge(rs_sb, RET_HEADS * l + h + 1)
                    v = lambda t: proj[:, t, COL["rv"] + 64 * h:COL["rv"] + 64 * h + 64]
                    o1 = ps6[:, 128 * h + 64:128 * h + 128]
                    pe.matmul(o1, ret_P[:, h, 128:256], v(0), start=True, stop=False)
                    pe.matmul(o1, ret_P[:, h, 256:384], v(1), start=False, stop=True)
                    mm = pe.matmul(ps6[:, 128 * h:128 * h + 64], ret_P[:, h, 0:128], v(0), start=True, stop=True)
                mm.then_inc(ro_ps, 1)

            def unit(ph, u, what):
                kind = ("nsa", "nsa", "dsw", "moba")[ph]
                gu = UNIT0[ph] + u
                parts = 3 if kind == "dsw" else 1
                if kind == "nsa":
                    br, h = u // 8, u % 8
                    e = 64 * (h // 4)
                    q = [nT[e:e + 64, h % 4, :]]
                    k = [nT[e:e + 64, 8 + br, :]]
                    c0 = COL[("nvs", "nvw")[br]] + e
                    v = [lambda t: proj[:, t, c0:c0 + 64]]
                    P, PT, slots = nsa_P, nsa_PT, 2
                else:
                    p, e = u // 2, 64 * (u % 2)
                    q = [stage[e:e + 64, p % 2, 2 * g, :] for g in range(parts)]
                    k = [stage[e:e + 64, p % 2, 2 * g + 1, :] for g in range(parts)]
                    if kind == "dsw":
                        v = [lambda t, g=g: qkv[:, t, 512 * (6 + g) + 64 * u:512 * (6 + g) + 64 * u + 64] for g in range(3)]
                    else:
                        v = [lambda t: qkv[:, t, 2048 + 64 * u:2048 + 64 * u + 64]]
                    P, PT, slots = big_P, big_PT, 4
                if what == "scores":
                    if kind == "dsw":
                        if u >= 1:
                            pe.wait_ge(ttr_done, gu)
                        for g in range(3):
                            pe.matmul(ps23[:, S * g:S * g + S], q[g][:, 128:256], k[g][:, :], start=True, stop=True)
                        for g in range(3):
                            mm = pe.matmul(ps7[:, 128 * g:128 * g + 128], q[g][:, 0:128], k[g][:, 0:128], start=True, stop=True)
                    else:
                        if u >= 2:
                            pe.wait_ge(ttr_done, gu - 1)
                        elif kind == "nsa":
                            pe.wait_ge(rs_sb, RET_HEADS * ph + 3 + u)
                        o = ps23[:, 512 * (u % 2):512 * (u % 2) + 384]
                        pe.matmul(o[:, 0:S], q[0][:, 128:256], k[0][:, :], start=True, stop=True)
                        mm = pe.matmul(o[:, S:384], q[0][:, 0:128], k[0][:, 0:128], start=True, stop=True)
                    mm.then_inc(s_ready, 1)
                if what == "transposes":
                    pe.wait_ge(p_ready, gu + 1)
                    for g in range(parts):
                        at = (S * g, S * g + 128, S * parts + 128 * g)
                        for i in range(3):
                            mm = pe.transpose(t_bank(ph, u, g)[:, 128 * i:128 * i + 128],
                                              P[:, u % 2, at[i]:at[i] + 128], ident[:, :])
                        mm.then_inc(t_ready, 1)
                if what == "output":
                    quad = gu // 4
                    o = ps6 if kind == "dsw" else (ps7, ps6)[quad % 2]
                    if u % 4 == 0 and kind == "dsw":
                        pe.wait_ge(o_free, quad)
                    elif u % 4 == 0 and quad >= 2:
                        pe.wait_ge(o_free, quad - 1)
                    if kind == "nsa" and u == 4:
                        pe.wait_ge(ro_used, ph + 1)
                    c = PCH0[ph] + parts * u
                    for g in range(parts):
                        engine, n = emptied_by(ph, u, g)
                        pe.wait_ge({"a": pt_a, "d": pt_d}[engine], n)
                    sl = lambda g: PT[:, (c - PCH0[ph] + g) % slots, :]
                    at = 128 * (u % 4)
                    for g in range(parts):
                        pe.matmul(o[:, at + 64:at + 128], sl(g)[:, 0:128], v[g](0), start=g == 0, stop=False)
                        pe.matmul(o[:, at + 64:at + 128], sl(g)[:, 128:256], v[g](1), start=False, stop=g == parts - 1)
                    for g in range(parts):
                        mm = pe.matmul(o[:, at:at + 64], sl(g)[:, 256:384], v[g](0), start=g == 0, stop=g == parts - 1)
                    if u % 4 == 3:
                        mm.then_inc(o_ready, 1)

            def stage_pair(ph, p):
                plan = stage_plan(ph, p)
                for i, (bank, gs, c) in enumerate(plan):
                    if p < 2 and i >= 2:
                        s = STG0[ph] + len(plan) * p + i - 2
                        pe.wait_ge((stg_a, stg_d)[c], s // 2 + 1)
                    for j, g in enumerate(gs):
                        c0 = 512 * (3 * c + g) + 128 * p if ph == 2 else 1024 * c + 128 * p
                        for t in range(2):
                            at = S * j + 128 * t
                            mm = pe.transpose(bank[:, at:at + 128], qkv[:, t, c0:c0 + 128], ident[:, :])
                    mm.then_inc(stg_ps, 1)

            def staged(ph, p):
                s = STG0[ph] + len(stage_plan(ph, p)) * (p + 1)
                pe.wait_ge(stg_a, s // 2)
                pe.wait_ge(stg_d, s // 2)

            def attention_start(ph):
                if ph >= 2:
                    stage_pair(ph, 0)
                    staged(ph, 0)
                unit(ph, 0, "scores")
                unit(ph, 1, "scores")
                if ph >= 2:
                    stage_pair(ph, 1)

            def attention(ph, units, hooks={}):
                pairs = units // 2 if ph >= 2 else 0
                if ph >= 2:
                    for half in range(2):
                        pe.wait_ge(acc_free[half], free_count(FIRST[("dswo", "mobao")[ph - 2]]))
                for u in range(units):
                    if pairs and u % 2 == 0 and u // 2 + 1 < pairs:
                        staged(ph, u // 2 + 1)
                    unit(ph, u, "transposes")
                    if u + 2 < units:
                        unit(ph, u + 2, "scores")
                    if pairs and u % 2 and (u + 3) // 2 < pairs:
                        if ph == 2:
                            for g in range(3):
                                engine, n = emptied_by(ph, u, g)
                                pe.wait_ge({"a": pt_a, "d": pt_d}[engine], n)
                        stage_pair(ph, (u + 3) // 2)
                    if u == units - 2 and ph != 2:
                        transpose_acts(Y_OF[ph], y, 0, (0,))
                    if u == units - 1:
                        transpose_acts(Y_OF[ph], y, 0, (1,) if ph != 2 else (0,))
                    unit(ph, u, "output")
                    if u in hooks:
                        hooks[u]()

            def nsa_transposes(l, chunks):
                s0 = STG0[l]
                before = FIRST[f"in{l}"] + (3 if chunks[-1] < 5 else 4)
                for half in range(2):
                    pe.wait_ge(acc_free[half], free_count(before))
                if l == 0:
                    pe.wait_ge(vec_sb, 1)
                for c in chunks:
                    if c == 2:
                        pe.wait_ge(k_dup_done, l + 1)
                    if c == 5:
                        pe.wait_ge(stg_d, s0 // 2 + 2)
                    for q in range(4 if c < 4 else 2):
                        i, t = q // 2, q % 2
                        if c < 2:
                            src = proj[:, t, COL["nq"] + 128 * (2 * c + i):COL["nq"] + 128 * (2 * c + i) + 128]
                        elif c < 4:
                            src = k_dup[:, c - 2, t, i, :]
                        else:
                            src = proj[:, t, COL[("nks", "nkw")[c - 4]]:COL[("nks", "nkw")[c - 4]] + 128]
                        mm = pe.transpose(nsa_bank[c][:, 128 * q:128 * q + 128], src, ident[:, :])
                    mm.then_inc(stg_ps, 1)

            def compress(l):
                pe.wait_ge(consts_in, 16 * 8)
                pe.wait_ge(cmp_blk, 2 * l + 2)
                for v in range(2):
                    for m in range(16):
                        mm = pe.matmul(ps23[0:32, 512 * v:512 * v + 64], blk[:, v, m, :], cw[:, v, m, :], start=m == 0, stop=m == 15)
                mm.then_inc(cmp_raw, 1)

            def compressed_operands(l):
                pe.wait_ge(cmp_tok, l + 1)
                pe.transpose(ps23[:, 0:32], k_c2[0:32].rearrange("p c n -> p (c n)"), ident[0:32, 0:32])
                pe.matmul(ps23[:, 512:576], rep[:, :], v_c[0:32], start=True, stop=True).then_inc(cmp_kv, 1)

            def compressed_scores(l):
                pe.wait_ge(cmp_kv_used, l + 1)
                for t in range(TT):
                    for p in range(4):
                        mm = pe.matmul(ps7[:, 128 * t + 32 * p:128 * t + 32 * p + 32],
                                       nT[:, p, 128 * t:128 * t + 128],
                                       k_bd.rearrange("p g n -> p (g n)"), start=True, stop=True)
                mm.then_inc(cmp_s, 1)

            def compressed_transposes(l):
                pe.wait_ge(cmp_p, l + 1)
                for t in range(TT):
                    mm = pe.transpose(ps4[:, 128 * t:128 * t + 128], cmp_L[:, 128 * t:128 * t + 128], ident[:, :])
                mm.then_inc(cmp_t, 1)

            def compressed_output(l):
                pe.wait_ge(cmp_pt, l + 1)
                for t in range(TT):
                    mm = pe.matmul((ps6, ps7)[t][:, :], cmp_PT[:, 128 * t:128 * t + 128],
                                   v_bd.rearrange("p h n -> p (h n)"), start=True, stop=True)
                mm.then_inc(cmp_o, 1)

            def hybrid(l):
                gemms(f"in{l}", 3)
                b = FIRST[f"in{l}"] + 4
                gemm(b - 1, [0])
                nsa_transposes(l, (0, 1, 2, 3, 4))
                gemm(b - 1, [1])
                gemm(b, [0])
                nsa_transposes(l, (5,))
                compress(l)
                gemm(b, [1])
                compressed_operands(l)
                gemm(b + 1, [0])
                compressed_scores(l)
                retention_transposes(l)
                gemm(b + 1, [1])
                retention_scores(l, (0, 1))
                compressed_transposes(l)
                gemm(b + 2, [0])
                compressed_output(l)
                retention_scores(l, (2, 3))
                gemm(b + 2, [1], midway=lambda: attention_start(l), at=KD)
                retention_output(l)
                attention(l, 16, {5: lambda: lru(l)})

            def lru(l):
                pe.wait_ge(small_in, SMALL)
                pe.wait_ge(lru_xc, 2 * l + 2)
                for half in range(2):
                    pe.wait_ge(acc_free[half], free_count(FIRST[f"out{l}"]))
                for i in range(2):
                    for c in range(2):
                        mm = pe.matmul(ps[i][:, S * c:S * c + S], gate_w[:, l, i, c, :],
                                       lru_w[:, 0, c, :], start=True, stop=True)
                mm.then_inc(lru_z, 1)

            pe.wait_ge(ident_in, 16)
            transpose_acts(X0, x, KD)
            for l in range(LAYERS):
                hybrid(l)
                gemms(f"out{l}", midway=lambda: transpose_acts((Y0, Y1)[l], y, 6, (2,)))
                normalized_acts(l, 0)

            def start(ph):
                pe.wait_ge(qk_norm, (6, 10)[ph - 2])
                attention_start(ph)

            gemms("dsw", between=lambda: start(2))
            attention(2, DSW_HEADS)
            gemms("dswo", midway=lambda: transpose_acts(DSW_Y, y, 4, (1,)), at=2)
            gemms("up0", midway=lambda: residual_acts("dswo", 1))
            gemms("down0")
            gemms("moba", midway=lambda: residual_acts("down0", 1), between=lambda: start(3))
            attention(3, MOBA_HEADS)
            transpose_acts(MOBA_Y, y, KD, (2,))
            gemms("mobao", midway=lambda: transpose_acts(MOBA_Y, y, KD, (3,)))
            gemms("up1", midway=lambda: residual_acts("mobao", 1))
            gemms("down1")

        @block.scalar
        def _(act):
            def split_hi(c):
                b, j = CHUNKS[c]
                n = BLOCKS[b]["n"]
                act.wait_ge(w_arrived[c % RAW], 16 * (c // RAW + 1))
                if b >= AHEAD:
                    act.wait_ge(acc_ready, 2 * (b - AHEAD) + 2)
                act.activation(w_hi[:, b % AHEAD, 4 * j:4 * j + 4, 0:n], w_raw[:, c % RAW, :, 0:n], ACT.Copy).then_inc(w_hi_done, 1)

            def hidden_hi(g):
                act.wait_ge(h_done, g + 1)
                k = (2 * (g % 16))
                act.activation(h_hi[:, k:k + 2, :].rearrange("p k n -> p (k n)"), y[:, 1, 512 * (g % 2):512 * (g % 2) + 512], ACT.Copy).then_inc(hh_done, 1)

            def take(b, half):
                d = BLOCKS[b]
                n = d["n"]
                if not d["last"] or d["use"] in ("deepnorm", "residual"):
                    return
                act.wait_ge(acc_ready, 2 * b + half + 1)
                if d["name"] in ("dsw", "moba") and d["use"] == "proj":
                    act.wait_ge(rstd_done, 1 if d["name"] == "dsw" else 3)
                if d["use"] == "proj":
                    dst = proj if d["name"].startswith("in") else qkv
                    if dst is proj and d["c0"] == COL["nq"]:
                        act.activation(dst[:, half, d["c0"]:d["c0"] + n].rearrange("p (j g d) -> p g j d", j=4, g=2),
                                       ps[half].rearrange("p (g j d) -> p g j d", j=4, g=2), ACT.Copy).then_inc(acc_free[half], 1)
                    else:
                        act.activation(dst[:, half, d["c0"]:d["c0"] + n], ps[half][:, 0:n], ACT.Copy,
                                       scale=1.0 if dst is proj else rstd[:, 0, half:half + 1]).then_inc(acc_free[half], 1)
                if d["use"] == "qk":
                    i = b - FIRST["dsw"] if d["name"] == "dsw" else 6 + b - FIRST["moba"]
                    if i >= 2:
                        act.wait_ge(qk_norm, i - 1)
                    act.activation(qkv[:, half, d["c0"]:d["c0"] + n], ps[half][:, :], ACT.Copy)
                    act.activation(sq[i % 2][:, half, :], ps[half][:, :], ACT.Square).then_inc(acc_free[half], 1)
                if d["use"] == "lru":
                    act.activation(lru_T[:, 2 * half:2 * half + 2, :].rearrange("p c n -> p (c n)"), ps[half][:, :], ACT.Copy).then_inc(acc_free[half], 1)
                if d["use"] == "relu2":
                    l = int(d["name"][-1])
                    g = HIDDEN0[l] + 2 * (b - FIRST[d["name"]]) + half
                    if g >= 2:
                        act.wait_ge(h_done, g - 1)
                    act.activation(y[:, 0, 512 * (g % 2):512 * (g % 2) + 512], ps[half][:, :], ACT.Relu).then_inc(acc_free[half], 1)

            def after_half(b, half, early=None, split=True):
                take(b, half)
                if early:
                    early()
                if split:
                    splits(b, half)
                if BLOCKS[b]["use"] == "relu2":
                    l = int(BLOCKS[b]["name"][-1])
                    hidden_hi(HIDDEN0[l] + 2 * (b - FIRST[BLOCKS[b]["name"]]) + half)

            def splits(b, half):
                for c in split_after(b, half):
                    split_hi(c)

            def gemms(name, count=None, early=None, begin=None, late=None, split=True):
                for b in blocks(name)[:count]:
                    for half in range(2):
                        last = b == last_block[name]
                        after_half(b, half, (early, late)[half] if last else None, split or not (last and half))
                        if begin and b == FIRST[name] and half == 0:
                            begin()
                    if b == BIAS_BLOCK:
                        bias_vectors()

            def bias_vectors():
                act.wait_ge(vec_ps, 1)
                for k in range(4):
                    n = 8 if k < 3 else 16
                    o = (ps23[:, 0:512], ps23[:, 512:1024], ps6, ps7)[k]
                    ins = act.activation(vec[0:n, k, :], o[0:n, 0:384], ACT.Copy)
                ins.then_inc(vec_sb, 1)

            def acts_hi(a, kts, gain=None, chunks=None, free=True):
                if a and free:
                    act.wait_ge(acc_ready, 2 * last_block[USED_BY[a - 1]] + 2)
                for i in range(kts // 2) if chunks is None else chunks:
                    act.wait_ge(at_ps, TRANS0[a] + i + 1)
                    if gain is None:
                        act.activation(act_hi[:, 2 * i:2 * i + 2, :].rearrange("p k n -> p (k n)"), bank_of(a, i)[:, :], ACT.Copy).then_inc(at_hi, 1)
                    else:
                        to = early_acts[:, 0] if a in (FFN0_U, FFN1_U) and i < 2 else act_hi
                        for k in range(2):
                            ins = act.activation(to[:, 2 * i + k, :], act_bank[i][:, S * k:S * k + S], ACT.Copy,
                                                 scale=norm_g[:, gain, 2 * i + k:2 * i + k + 1])
                        ins.then_inc(at_hi, 1)

            def normalized_scaled(l):
                a = (X1, DSW_U)[l]
                act.wait_ge(ln_in, 64 * (l + 1))
                if l:
                    act.wait_ge(ln_fs_done, 1)
                gs = (ln_f, ln_fs)[l]
                for i in range(4):
                    act.wait_ge(at_ps, TRANS0[a] + i + 1)
                    if i >= 2:
                        act.wait_ge(at_lo, ACT0[a] + i - 1)
                    for k in range(4):
                        kt = 4 * (i % 2) + k
                        ins = act.activation(y[:, i % 2, 128 * k:128 * k + 128], act_bank[i][:, 128 * k:128 * k + 128],
                                             ACT.Identity, bias=gs[:, 1, kt:kt + 1], scale=gs[:, 0, kt:kt + 1])
                    ins.then_inc(at_hi, 1)

            def units(ph, n, hooks={}, start=False):
                kind = ("nsa", "nsa", "dsw", "moba")[ph]
                parts = 3 if kind == "dsw" else 1
                P, PT, slots = (nsa_P, nsa_PT, 2) if kind == "nsa" else (big_P, big_PT, 4)

                def staged(p):
                    plan = stage_plan(ph, p)
                    for i, (bank, gs, c) in enumerate(plan):
                        if c == 0:
                            act.wait_ge(stg_ps, STG0[ph] + len(plan) * p + i + 1)
                            g = gs[0]
                            act.activation(stage[:, p % 2, 2 * g:2 * g + 2 * len(gs):2, :],
                                           bank[:, 0:S * len(gs)].rearrange("p (g n) -> p g n", n=S), ACT.Copy,
                                           scale=qk_gain[:, ph - 2:ph - 1]).then_inc(stg_a, 1)

                def softmax(u):
                    gu = UNIT0[ph] + u
                    act.wait_ge(ttr_done, gu + 1)
                    if gu >= 16 and gu % 4 == 0:
                        act.wait_ge(o_free, gu // 4 - 3)
                    w1, w0 = S * parts, 128 * parts
                    dn = den[:, gu % 16, :]
                    act.activation(P[:, u % 2, 0:w1], P[:, u % 2, 0:w1], ACT.Exp, bias=ttr[:, u % 2, 1:2], scale=-1.0,
                                   accum_out=dn[:, 1:2])
                    act.activation(P[:, u % 2, w1:w1 + w0], P[:, u % 2, w1:w1 + w0], ACT.Exp, bias=ttr[:, u % 2, 0:1],
                                   scale=-1.0, accum_out=dn[:, 0:1]).then_inc(p_ready, 1)

                def transposed(u):
                    for g in range(parts):
                        if emptied_by(ph, u, g)[0] == "a":
                            act.wait_ge(t_ready, PCH0[ph] + parts * u + g + 1)
                            act.activation(PT[:, (parts * u + g) % slots, :], t_bank(ph, u, g)[:, 0:384], ACT.Copy).then_inc(pt_a, 1)

                if start:
                    if ph >= 2:
                        staged(0)
                    softmax(0)
                    if ph >= 2:
                        staged(1)
                    softmax(1)
                    return
                for u in range(n):
                    transposed(u)
                    if ph >= 2 and u % 2 and u + 3 < n:
                        staged((u + 3) // 2)
                    if u + 2 < n:
                        softmax(u + 2)
                    if u in hooks:
                        hooks[u]()
                    if u == n - 2 and ph != 2:
                        acts_hi(Y_OF[ph], 0, chunks=(0,))
                    if u == n - 1:
                        acts_hi(Y_OF[ph], 0, chunks=(1,) if ph != 2 else (0,))

            def nsa_transposed(l):
                for c in (0, 2, 4):
                    act.wait_ge(stg_ps, STG0[l] + c + 1)
                    at, k = ((0, 2), None, (4, 2), None, (8, 1))[c]
                    act.activation(nT[:, at:at + k, :].rearrange("p c n -> p (c n)"), nsa_bank[c][:, 0:S * k], ACT.Copy,
                                   scale=HD ** -0.5 if c == 0 else 1.0).then_inc(stg_a, 1)

            def hybrid(l):
                gemms(f"in{l}", 3)
                b = FIRST[f"in{l}"] + 4
                take(b - 1, 0)
                act.wait_ge(vec_out, 32)
                nsa_transposed(l)
                for c in split_after(b - 1, 0):
                    split_hi(c)
                after_half(b - 1, 1)
                for half in range(2):
                    act.wait_ge(acc_free[half], free_count(b))
                act.activation(y[:, :, 256:768], proj[:, :, COL["ng"]:COL["ng"] + 512], ACT.Tanh, scale=0.5)
                act.activation(gate_c[:, :, :], proj[:, :, COL["ngl"]:COL["ngl"] + 24], ACT.Tanh, scale=0.5).then_inc(tanh_done, 1)
                after_half(b, 0)
                after_half(b, 1)
                after_half(b + 1, 0)
                act.wait_ge(stg_ps, STG0[l] + 7)
                act.activation(ret_T[:, 0:2, :].rearrange("p c n -> p (c n)"), ps4[:, :], ACT.Copy).then_inc(stg_a, 1)
                act.wait_ge(cmp_l, l + 1)
                act.activation(cmp_L, cmp_L, ACT.Exp).then_inc(cmp_p, 1)
                after_half(b + 1, 1)
                for half in range(2):
                    act.wait_ge(acc_free[half], free_count(b + 1) + 1)
                act.activation(y[:, :, 0:256], proj[:, :, COL["rg"]:COL["rg"] + 256], ACT.Tanh, scale=0.5).then_inc(tanh_done, 1)
                act.wait_ge(cmp_t, l + 1)
                act.activation(cmp_PT, ps4[:, 0:256], ACT.Copy).then_inc(cmp_pt, 1)
                act.wait_ge(cmp_blk, 2 * l + 2)
                take(b + 2, 0)
                units(l, 16, start=True)
                if l == 0:
                    act.wait_ge(lam_abs, 1)
                    act.activation(lam_exp[:, :], lam_exp[:, :], ACT.Exp, scale=-1.0).then_inc(lam_e, 1)
                splits(b + 2, 0)
                after_half(b + 2, 1, split=False)
                units(l, 16, {6: lambda: [lru_gates(l, i) for i in range(3)], 8: lambda: lru_decay(l),
                              10: lambda: lru_root(l), 13: lambda: lru_operand(l)})

            def lru_gates(l, step):
                if step < 2:
                    act.wait_ge(lru_z, l + 1)
                    for c in range(2):
                        act.activation(lru_w[:, 1 + step, c, :], ps[step][:, S * c:S * c + S], ACT.Tanh,
                                       bias=lru_hb[:, l, step, c:c + 1], scale=0.5)
                else:
                    act.activation(lru_w[:, 6, :, :].rearrange("p c n -> p (c n)"), lru_T[:, 2:4, :].rearrange("p c n -> p (c n)"), ACT.Tanh, scale=0.5).then_inc(lru_th, 1)

            def lru_decay(l):
                act.wait_ge(lru_nla, l + 1)
                nla = lru_w[:, 1, :, :].rearrange("p c n -> p (c n)")
                act.activation(lru_w[:, 3, :, :].rearrange("p c n -> p (c n)"), nla, ACT.Exp, scale=-1.0)
                act.activation(lru_w[:, 4, :, :].rearrange("p c n -> p (c n)"), nla, ACT.Tanh).then_inc(lru_at, 1)

            def lru_root(l):
                act.wait_ge(lru_v2, l + 1)
                v2 = lru_w[:, 4, :, :].rearrange("p c n -> p (c n)")
                act.activation(v2, v2, ACT.Sqrt).then_inc(lru_m, 1)

            def lru_operand(l):
                act.wait_ge(lru_y, l + 1)
                act.wait_ge(acc_ready, 2 * last_block[f"in{l}"] + 2)
                act.activation(act_hi[:, 6:8, :].rearrange("p c n -> p (c n)"), lru_w[:, 5, :, :].rearrange("p c n -> p (c n)"), ACT.Copy).then_inc(at_hi, 1)

            def square_sums(i):
                if i:
                    for half in range(2):
                        act.wait_ge(acc_free[half], free_count(FIRST[("", "up0", "moba", "up1")[i]]))
                for t in range(TT):
                    if i == 0:
                        act.wait_ge(x_new, TT * (LAYERS - 1) + t + 1)
                    ins = act.activation(y[:, t, :], x[:, t, :], ACT.Square, accum_out=rms_sum[:, t:t + 1])
                ins.then_inc(ssq_done, 1)
                if i % 2:
                    act.wait_ge(ssq_done, i + 1)

            for c in range(2):
                act.dma_start(x[:, :, 512 * c:512 * c + 512],
                              dram["x"][0, :, 512 * c:512 * c + 512].rearrange("(t p) d -> p t d", p=128)).then_inc(x_in[c], 16)
            acts_hi(X0, KD, chunks=(0, 1))
            split_hi(0)
            acts_hi(X0, KD, chunks=(2, 3))
            for c in range(1, CHUNK0[AHEAD - 1] + 1):
                split_hi(c)
            for l in range(LAYERS):
                hybrid(l)
                acts_hi((Y0, Y1)[l], 6, chunks=(2,))
                splits(last_block[f"in{l}"], 1)
                gemms(f"out{l}")
                normalized_scaled(l)
            gemms("dsw", begin=lambda: square_sums(0), early=lambda: units(2, DSW_HEADS, start=True), split=False)
            units(2, DSW_HEADS)
            acts_hi(DSW_Y, 4, chunks=(1,))
            splits(last_block["dsw"], 1)
            gemms("dswo", early=lambda: acts_hi(FFN0_U, KD, 2, (0, 1), False), late=lambda: acts_hi(FFN0_U, KD, 2, (2, 3)))
            square_sums(1)
            gemms("up0")
            gemms("down0", early=lambda: acts_hi(MOBA_U, KD, 1, (0, 1), False), late=lambda: acts_hi(MOBA_U, KD, 1, (2, 3), False))
            square_sums(2)
            gemms("moba", early=lambda: units(3, MOBA_HEADS, start=True), split=False)
            units(3, MOBA_HEADS)
            acts_hi(MOBA_Y, KD, chunks=(2, 3))
            splits(last_block["moba"], 1)
            gemms("mobao", early=lambda: acts_hi(FFN1_U, KD, 3, (0, 1), False), late=lambda: acts_hi(FFN1_U, KD, 3, (2, 3)))
            square_sums(3)
            gemms("up1")
            gemms("down1")

        @block.vector
        def _(dve):
            steps = [0]

            def done(ins):
                steps[0] += 1
                ins.then_inc(dve_step, 1)
                dve.wait_ge(dve_step, steps[0])

            def spread(ap, dims):
                return bass.AP(ap.tensor, ap.offset, [ap.ap[0], *[list(d) for d in dims]])

            def split_lo(c):
                b, j = CHUNKS[c]
                n = BLOCKS[b]["n"]
                dve.wait_ge(w_hi_done, c + 1)
                hi = w_hi[:, b % AHEAD, 4 * j:4 * j + 4, 0:n]
                lo = w_lo[:, b % AHEAD, 4 * j:4 * j + 4, 0:n]
                dve.tensor_tensor(lo, w_raw[:, c % RAW, :, 0:n], hi.bitcast(F), ALU.subtract).then_inc(w_lo_done, 1)

            def rsqrt(v, scale, eps, o, finish=None):
                n = v.shape[-1]
                m, a, c = st[:, 2, 0:n], st[:, 3, 0:n], st[:, 4, 0:n]
                done(dve.tensor_scalar(m, v, scale, eps, ALU.mult, ALU.add))
                done(dve.tensor_scalar(a.bitcast(I32), m.bitcast(I32), 1, None, ALU.logical_shift_right))
                done(dve.tensor_scalar(o.bitcast(I32), a.bitcast(I32), -1.0, float(0x5F3759DF), ALU.mult, ALU.add))
                for i in range(3):
                    done(dve.tensor_tensor(a, o, o, ALU.mult))
                    done(dve.scalar_tensor_tensor(out=c, in0=a, scalar=-0.5, in1=m, op0=ALU.mult, op1=ALU.mult))
                    (finish if finish and i == 2 else done)(dve.scalar_tensor_tensor(out=o, in0=c, scalar=1.5, in1=o, op0=ALU.add, op1=ALU.mult))

            def take(b, half):
                d = BLOCKS[b]
                n = d["n"]
                if not d["last"]:
                    return
                ready = free_count(b) + 1
                if d["use"] in ("deepnorm", "residual"):
                    dve.wait_ge(acc_ready, 2 * b + half + 1)
                    r = x[:, half, d["c0"]:d["c0"] + n]
                    if d["use"] == "deepnorm":
                        dve.scalar_tensor_tensor(out=r, in0=r, scalar=ALPHA, in1=ps[half][:, 0:n],
                                                 op0=ALU.mult, op1=ALU.add).then_inc(acc_free[half], 1)
                    else:
                        w = rstd[:, 1, half:half + 1] if d["name"].startswith("down") else 1.0
                        dve.scalar_tensor_tensor(out=r, in0=ps[half][:, 0:n], scalar=w, in1=r,
                                                 op0=ALU.mult, op1=ALU.add).then_inc(acc_free[half], 1)
                if d["use"] == "qk" and half == 1:
                    dve.wait_ge(acc_free[0], ready)
                    dve.wait_ge(acc_free[1], ready)
                    i = b - FIRST[d["name"]]
                    done(dve.tensor_reduce(out=st[:, 5, 0:16], in_=sq[i % 2].rearrange("p t (h d) -> p (t h) d", d=HD), axis=AX, op=ALU.add))
                    heads = [spread(rstd[:, i, 0:1], [(1, 2), (0, 8)]) for i in range(2)]
                    done(dve.tensor_tensor(st[:, 5, 0:16], st[:, 5, 0:16], heads[1], ALU.mult))
                    rsqrt(st[:, 5, 0:16], 1.0 / HD, 1e-6, st[:, 6, 0:16])
                    done(dve.tensor_tensor(st[:, 6, 0:16], st[:, 6, 0:16], heads[0], ALU.mult))
                    v = qkv[:, :, d["c0"]:d["c0"] + 512].rearrange("p t (h d) -> p t h d", d=HD)
                    dve.tensor_tensor(v, v, spread(st[:, 6, 0:1], [(8, 2), (1, 8), (0, HD)]), ALU.mult).then_inc(qk_norm, 1)
                if d["use"] == "relu2":
                    l = int(d["name"][-1])
                    g = HIDDEN0[l] + 2 * (b - FIRST[d["name"]]) + half
                    dve.wait_ge(acc_free[half], ready)
                    r = y[:, 0, 512 * (g % 2):512 * (g % 2) + 512]
                    dve.tensor_tensor(y[:, 1, 512 * (g % 2):512 * (g % 2) + 512], r, r, ALU.mult).then_inc(h_done, 1)

            def hidden_lo(g):
                k = 2 * (g % 16)
                dve.wait_ge(hh_done, g + 1)
                flat = "p k n -> p (k n)"
                dve.tensor_tensor(h_lo[:, k:k + 2, :].rearrange(flat), y[:, 1, 512 * (g % 2):512 * (g % 2) + 512],
                                  h_hi[:, k:k + 2, :].rearrange(flat).bitcast(F), ALU.subtract).then_inc(hl_done, 1)

            def after_half(b, half, early=None, split=True):
                take(b, half)
                if early:
                    early()
                if split:
                    splits(b, half)
                if BLOCKS[b]["use"] == "relu2":
                    l = int(BLOCKS[b]["name"][-1])
                    hidden_lo(HIDDEN0[l] + 2 * (b - FIRST[BLOCKS[b]["name"]]) + half)

            def splits(b, half):
                for c in split_after(b, half):
                    split_lo(c)

            def gemms(name, count=None, early=None, begin=None, late=None, split=True):
                for b in blocks(name)[:count]:
                    for half in range(2):
                        last = b == last_block[name]
                        after_half(b, half, (early, late)[half] if last else None, split or not (last and half))
                        if begin and b == FIRST[name] and half == 0:
                            begin()

            def small_params():
                dve.wait_ge(small_in, SMALL)
                done(dve.tensor_tensor(qk_gain[:, :], qk_g[:, 0:4:2], qk_g[:, 1:4:2], ALU.mult))
                done(dve.tensor_scalar(qk_gain[:, :], qk_gain[:, :], HD ** -0.5, None, ALU.mult))
                done(dve.tensor_scalar(lru_hb[:, :, :, :], lru_v[:, :, 1:3, :], 0.5, None, ALU.mult))
                lam = lru_v[:, :, 3, :]
                le = lam_exp[:, :].rearrange("p (l c) -> p l c", l=LAYERS)
                dve.scalar_tensor_tensor(out=le, in0=lam, scalar=-1.0, in1=lam, op0=ALU.mult, op1=ALU.max).then_inc(lam_abs, 1)
                dve.wait_ge(lam_e, 1)
                e, s1, s2, pl = lam_exp[:, :], lam_p[:, 0], lam_p[:, 1], lam_p[:, 2]
                done(dve.tensor_scalar(s2, e, 2.0, None, ALU.add))
                done(dve.reciprocal(s1, s2))
                done(dve.tensor_tensor(s1, s1, e, ALU.mult))
                done(dve.tensor_tensor(s2, s1, s1, ALU.mult))
                done(dve.tensor_scalar(pl, s2, 1.0 / 15, None, ALU.mult))
                for k in (13, 11, 9, 7, 5, 3):
                    done(dve.scalar_tensor_tensor(out=pl, in0=pl, scalar=1.0 / k, in1=s2, op0=ALU.add, op1=ALU.mult))
                done(dve.scalar_tensor_tensor(out=pl, in0=pl, scalar=1.0, in1=s1, op0=ALU.add, op1=ALU.mult))
                done(dve.tensor_scalar(lam_p[:, 3].rearrange("p (l c) -> p l c", l=LAYERS), lam, -1.0, 0.0, ALU.mult, ALU.max))
                done(dve.tensor_scalar(lam_p[:, 3], lam_p[:, 3], 4.0, None, ALU.mult))
                done(dve.scalar_tensor_tensor(out=lru_sp[:, :], in0=pl, scalar=8.0, in1=lam_p[:, 3], op0=ALU.mult, op1=ALU.add))

            def acts_lo(a, kts, gain=None, chunks=None):
                for i in range(kts // 2) if chunks is None else chunks:
                    dve.wait_ge(at_hi, ACT0[a] + LRU_CHUNK[a] + i + 1)
                    if gain is None:
                        hi = act_hi[:, 2 * i:2 * i + 2, :].rearrange("p k n -> p (k n)").bitcast(F)
                        lo = act_lo[:, 2 * i:2 * i + 2, :].rearrange("p k n -> p (k n)")
                        dve.tensor_tensor(lo, bank_of(a, i)[:, :], hi, ALU.subtract).then_inc(at_lo, 1)
                    else:
                        early = a in (FFN0_U, FFN1_U) and i < 2
                        hi, lo = (early_acts[:, 0], early_acts[:, 1]) if early else (act_hi, act_lo)
                        for k in (2 * i, 2 * i + 1):
                            ins = dve.scalar_tensor_tensor(
                                out=lo[:, k, :], in0=act_bank[i][:, S * (k % 2):S * (k % 2) + S],
                                scalar=norm_g[:, gain, k:k + 1], in1=hi[:, k, :].bitcast(F),
                                op0=ALU.mult, op1=ALU.subtract)
                        ins.then_inc(at_lo, 1)

            def rotate():
                half = HD // 2

                def part(v, c0, e):
                    base = v[:, :, c0 + half * e:c0 + half * e + 1]
                    return spread(base, [(v.ap[1][0], 2), (HD, 8), (1, half)])

                for e in range(2):
                    cos, sin = [spread(rope[:, i, 0, 0:1], [(half, 2), (0, 8), (1, half)]) for i in range(2)]
                    dve.tensor_tensor(part(rot, 0, e), part(proj, COL["rq"], e), cos, ALU.mult)
                    done(dve.tensor_tensor(part(rot_b, 0, e), part(proj, COL["rq"], 1 - e), sin, ALU.mult))
                for e in range(2):
                    ins = dve.tensor_tensor(part(rot, 0, e), part(rot, 0, e), part(rot_b, 0, e), (ALU.subtract, ALU.add)[e])
                ins.then_inc(rot_done, 1)

            def units(ph, n, hooks={}, start=False):
                kind = ("nsa", "nsa", "dsw", "moba")[ph]
                parts = 3 if kind == "dsw" else 1
                P, PT, slots = (nsa_P, nsa_PT, 2) if kind == "nsa" else (big_P, big_PT, 4)
                w1 = S * parts

                def staged(p):
                    plan = stage_plan(ph, p)
                    for i, (bank, gs, c) in enumerate(plan):
                        if c == 1:
                            dve.wait_ge(stg_ps, STG0[ph] + len(plan) * p + i + 1)
                            g = gs[0]
                            dve.tensor_copy(stage[:, p % 2, 2 * g + 1:2 * g + 2 * len(gs):2, :],
                                            bank[:, 0:S * len(gs)].rearrange("p (g n) -> p g n", n=S)).then_inc(stg_d, 1)

                def logits(u):
                    gu = UNIT0[ph] + u
                    dve.wait_ge(s_ready, gu + 1)
                    if u >= 2:
                        dve.wait_ge(t_ready, PCH0[ph] + parts * (u - 1))
                    if kind == "nsa":
                        m1, m0 = causal[:, :], causal[:, 128:256]
                    else:
                        bu = u + (DSW_HEADS if kind == "moba" else 0)
                        dve.wait_ge(bias_in[bu % 2], 16 * (bu // 2 + 1))
                        m1 = spread(bias_T[:, bu % 2, 255:256], [(S, parts), (-1, S)])
                        m0 = spread(bias_T[:, bu % 2, 127:128], [(S, parts), (-1, 128)])
                    if kind == "dsw":
                        s1, s0 = ps23[:, 0:w1].rearrange("p (g n) -> p g n", g=3), ps7[:, 0:384].rearrange("p (g n) -> p g n", g=3)
                        o0 = P[:, u % 2, w1:w1 + 384].rearrange("p (g n) -> p g n", g=3)
                    else:
                        s1, s0 = [ps23[:, 512 * (u % 2) + a:512 * (u % 2) + b] for a, b in ((0, S), (S, 384))]
                        o0 = P[:, u % 2, S:384]
                        if kind == "moba":
                            m1, m0 = spread(bias_T[:, bu % 2, 255:256], [(-1, S)]), spread(bias_T[:, bu % 2, 127:128], [(-1, 128)])
                    o1 = P[:, u % 2, 0:w1]
                    if kind == "dsw":
                        o1 = o1.rearrange("p (g n) -> p g n", g=3)
                    dve.tensor_tensor_reduce(out=o1, in0=s1, in1=m1, scale=-1.0, scalar=3.0e38,
                                             op0=ALU.add, op1=ALU.min, accum_out=ttr[:, u % 2, 1:2])
                    dve.tensor_tensor_reduce(out=o0, in0=s0, in1=m0, scale=-1.0, scalar=3.0e38,
                                             op0=ALU.add, op1=ALU.min, accum_out=ttr[:, u % 2, 0:1]).then_inc(ttr_done, 1)

                def transposed(u):
                    for g in range(parts):
                        if emptied_by(ph, u, g)[0] == "d":
                            dve.wait_ge(t_ready, PCH0[ph] + parts * u + g + 1)
                            dve.tensor_copy(PT[:, (parts * u + g) % slots, :], t_bank(ph, u, g)[:, 0:384]).then_inc(pt_d, 1)

                def quad_output(u0):
                    quad = (UNIT0[ph] + u0) // 4
                    dve.wait_ge(o_ready, quad + 1)
                    sums = den[:, 4 * quad % 16:4 * quad % 16 + 4, :]
                    done(dve.reciprocal(rden[:, :, :], sums))
                    o = (ps6 if kind == "dsw" else (ps7, ps6)[quad % 2]).rearrange("p (h d) -> p h d", d=HD)
                    if kind == "nsa":
                        br, h = u0 // 8, u0 % 8
                        gc = spread(gate_c[:, 0, 3 * h + 1 + br:3 * h + 2 + br], [(3, 4), (24, 2)])
                        done(dve.tensor_tensor(rden[:, :, :], rden[:, :, :], gc, ALU.mult))
                        part = o_part.rearrange("p (h d) -> p h d", d=HD)
                        dve.tensor_tensor(part, o, spread(rden[:, 0, 0:1], [(1, 8), (0, HD)]), ALU.mult).then_inc(o_free, 1)
                        dve.wait_ge(o_free, quad + 1)
                        yv = spread(y[:, 0, 256 + HD * h:257 + HD * h], [(HD, 4), (D, 2), (1, HD)])
                        done(dve.tensor_tensor(yv, yv, part.rearrange("p (h t) d -> p h t d", t=2), ALU.add))
                        if br:
                            gated = spread(proj[:, 0, COL["ng"] + HD * h:COL["ng"] + HD * h + 1], [(HD, 4), (2840, 2), (1, HD)])
                            dve.tensor_tensor(yv, yv, gated, ALU.mult).then_inc(y_ready, 1)
                    else:
                        yv = spread(y[:, 0, HD * u0:HD * u0 + 1], [(HD, 4), (D, 2), (1, HD)])
                        dve.tensor_tensor(yv, o.rearrange("p (h t) d -> p h t d", t=2),
                                          spread(rden[:, 0, 0:1], [(2, 4), (1, 2), (0, HD)]), ALU.mult).then_inc(o_free, 1)

                if start:
                    if ph >= 2:
                        staged(0)
                    logits(0)
                    logits(1)
                    if ph >= 2:
                        staged(1)
                    return
                for u in range(n):
                    transposed(u)
                    if ph == 2 and u == 4:
                        quad_output(0)
                    if u + 2 < n:
                        logits(u + 2)
                    if ph >= 2 and u % 2 and u + 3 < n:
                        staged((u + 3) // 2)
                    if u % 4 == 0 and u and ph != 2:
                        quad_output(u - 4)
                    if u in hooks:
                        hooks[u]()
                    if u == n - 2 and ph != 2:
                        acts_lo(Y_OF[ph], 0, chunks=(0,))
                    if u == n - 1:
                        acts_lo(Y_OF[ph], 0, chunks=(1,) if ph != 2 else (0,))
                quad_output(n - 4)

            def decay_scores(l, heads):
                for h in heads:
                    dve.wait_ge(rs_ps, RET_HEADS * l + h + 1)
                    o = ps23[:, 512 * (h % 2):512 * (h % 2) + 384]
                    dve.tensor_tensor(ret_P[:, h, 0:S], o[:, 0:S], decay[:, h, :], ALU.mult)
                    dve.tensor_tensor(ret_P[:, h, S:384], o[:, S:384], decay[:, h, 0:128], ALU.mult).then_inc(rs_sb, 1)

            def gate_silu(l, c0, n, g0):
                g = proj[:, :, g0:g0 + n]
                return dve.scalar_tensor_tensor(out=g, in0=y[:, :, c0:c0 + n], scalar=1.0, in1=g, op0=ALU.add, op1=ALU.mult)

            ret_o = ps6.rearrange("p (h d) -> p h d", d=HD)
            cen = tmp_tok[:, 0:512].rearrange("p (h d) -> p h d", d=HD)
            squ = tmp_tok[:, 512:1024].rearrange("p (h d) -> p h d", d=HD)

            def retention_norm(l, step):
                if step == 0:
                    dve.wait_ge(ro_ps, l + 1)
                    done(dve.tensor_reduce(out=st[:, 0, 0:8], in_=ret_o, axis=AX, op=ALU.add))
                    done(dve.tensor_scalar(st[:, 1, 0:8], st[:, 0, 0:8], 1.0 / HD, None, ALU.mult))
                    dve.tensor_tensor(cen, ret_o, spread(st[:, 1, 0:1], [(1, 8), (0, HD)]), ALU.subtract).then_inc(ro_used, 1)
                    dve.wait_ge(ro_used, l + 1)
                if step == 1:
                    done(dve.tensor_tensor(squ, cen, cen, ALU.mult))
                    done(dve.tensor_reduce(out=st[:, 5, 0:8], in_=squ, axis=AX, op=ALU.add))
                if step == 2:
                    rsqrt(st[:, 5, 0:8], 1.0 / HD, 1e-5, st[:, 6, 0:8])
                    done(dve.tensor_scalar(st[:, 7, 0:8], st[:, 6, 0:8], 0.5, None, ALU.mult))
                if step == 3:
                    done(dve.tensor_tensor(cen, cen, spread(st[:, 7, 0:1], [(1, 8), (0, HD)]), ALU.mult))
                    done(dve.tensor_tensor(spread(y[:, 0, 0:1], [(HD, 4), (D, 2), (1, HD)]), cen.rearrange("p (h t) d -> p h t d", t=2),
                                           spread(proj[:, 0, COL["rg"]:COL["rg"] + 1], [(HD, 4), (2840, 2), (1, HD)]), ALU.mult))

            def nsa_transposed(l, chunks):
                for c in chunks:
                    dve.wait_ge(stg_ps, STG0[l] + c + 1)
                    at, k = (None, (2, 2), None, (6, 2), None, (9, 1))[c]
                    dve.tensor_scalar(nT[:, at:at + k, :].rearrange("p c n -> p (c n)"), nsa_bank[c][:, 0:S * k],
                                      HD ** -0.5 if c == 1 else 1.0, None, ALU.mult).then_inc(stg_d, 1)

            def nsa_operands(l):
                dve.wait_ge(vec_out, 32)
                for v in range(2):
                    dve.memset(spread(blk[:, v, 0, 15:16], [(32, 16), (16, 2), (1, 1)]), 0.0)
                nsa_transposed(l, (1, 3))
                dve.wait_ge(stg_a, STG0[l] // 2 + 2)
                dve.wait_ge(stg_d, STG0[l] // 2 + 2)
                dve.wait_ge(cw_in, 16 * 6 * (l + 1))
                for v in range(2):
                    for e in range(2):
                        r = slice(64 * e, 64 * e + 64)
                        ins = dve.tensor_tensor(
                            spread(blk[r, v, 0, 0:1], [(32, 16), (16, 2), (1, N_CMP)]),
                            spread(nT[r, 4 + 2 * v, e:e + 1], [(2, 16), (S, 2), (16, N_CMP)]),
                            spread(cmp_pos[r, v, 0:1], [(1, 16), (0, 2), (0, N_CMP)]), ALU.add)
                    ins.then_inc(cmp_blk, 1)

            def compressed_rows(l):
                dve.wait_ge(cmp_raw, l + 1)
                dve.tensor_copy(k_c2[0:32], spread(ps23[0:32, 0:1], [(0, 2), (1, HD)]))
                dve.tensor_copy(v_c[0:32], ps23[0:32, 512:576]).then_inc(cmp_tok, 1)

            def compressed_operands(l):
                dve.wait_ge(cmp_kv, l + 1)
                dve.tensor_tensor(k_bd, spread(ps23[:, 0:1], [(16, 2), (1, 16)]),
                                  spread(half_of[:, 0:1], [(1, 2), (0, 16)]), ALU.mult)
                dve.tensor_tensor(v_bd, spread(ps23[:, 512:513], [(0, 8), (1, HD)]),
                                  spread(head_of[:, 0:1], [(1, 8), (0, HD)]), ALU.mult).then_inc(cmp_kv_used, 1)

            def compressed_logits(l):
                dve.wait_ge(cmp_s, l + 1)
                lv = cmp_L.rearrange("p (t h n) -> p t h n", t=2, h=8)
                rows = cmp_L.rearrange("p (r n) -> p r n", n=16)
                done(dve.tensor_tensor(lv, ps7[:, 0:256].rearrange("p (t h n) -> p t h n", t=2, h=8),
                                       spread(cmp_mask[:, 0, 0:1], [(16, 2), (0, 8), (1, 16)]), ALU.add))
                done(dve.tensor_reduce(out=st[:, 0, 0:16], in_=rows, axis=AX, op=ALU.max))
                dve.tensor_tensor(rows, rows, spread(st[:, 0, 0:1], [(1, 16), (0, 16)]), ALU.subtract).then_inc(cmp_l, 1)

            def compressed_weights(l):
                rows = cmp_L.rearrange("p (r n) -> p r n", n=16)
                dve.wait_ge(cmp_p, l + 1)
                done(dve.tensor_reduce(out=st[:, 1, 0:16], in_=rows, axis=AX, op=ALU.add))
                done(dve.reciprocal(st[:, 2, 0:16], st[:, 1, 0:16]))
                co = cmp_w[:, 0:16].rearrange("p (t h) -> p t h", t=2)
                done(dve.tensor_tensor(spread(cmp_w[:, 0:1], [(8, 2), (1, 4), (4, 2)]),
                                       spread(st[:, 2, 0:1], [(8, 2), (2, 4), (1, 2)]),
                                       spread(gate_c[:, 0, 0:1], [(24, 2), (3, 4), (12, 2)]), ALU.mult))
                done(dve.tensor_tensor(co, co, spread(cmp_any[:, 0:1], [(1, 2), (0, 8)]), ALU.mult))

            def compressed_output(l):
                dve.wait_ge(cmp_o, l + 1)
                for t in range(TT):
                    ins = dve.tensor_tensor(y[:, t, 256:768].rearrange("p (h d) -> p h d", d=HD),
                                            (ps6, ps7)[t].rearrange("p (h d) -> p h d", d=HD),
                                            spread(cmp_w[:, 8 * t:8 * t + 1], [(1, 8), (0, HD)]), ALU.mult)
                ins.then_inc(cmp_o_used, 1)
                dve.wait_ge(cmp_o_used, l + 1)

            def hybrid(l):
                gemms(f"in{l}", 3, begin=(lambda: scale_residual(0)) if l else None)
                b = FIRST[f"in{l}"] + 4
                nsa_operands(l)
                after_half(b - 1, 0)
                after_half(b - 1, 1)
                dve.wait_ge(tanh_done, 2 * l + 1)
                gate_silu(l, 256, 512, COL["ng"])
                done(dve.tensor_scalar(gate_c[:, :, :], gate_c[:, :, :], 1.0, 0.25, ALU.add, ALU.mult))
                after_half(b, 0)
                nsa_transposed(l, (5,))
                compressed_rows(l)
                compressed_operands(l)
                for half in range(2):
                    dve.wait_ge(acc_free[half], free_count(b) + 1)
                dve.wait_ge(consts_in, 16 * 8)
                rotate()
                splits(b, 1)
                compressed_logits(l)
                dve.wait_ge(stg_ps, STG0[l] + 8)
                dve.tensor_copy(ret_T[:, 2:4, :].rearrange("p c n -> p (c n)"), ps5[:, :]).then_inc(stg_d, 1)
                splits(b + 1, 0)
                after_half(b + 1, 1)
                compressed_weights(l)
                decay_scores(l, (0, 1))
                dve.wait_ge(tanh_done, 2 * l + 2)
                done(gate_silu(l, 0, 256, COL["rg"]))
                compressed_output(l)
                decay_scores(l, (2, 3))
                units(l, 16, start=True)
                if l == 0:
                    small_params()
                splits(b + 2, 0)
                after_half(b + 2, 1, split=False)
                norm = [lambda i=i: retention_norm(l, i) for i in range(4)]
                units(l, 16, {0: norm[0], 1: norm[1], 2: lambda: lru_conv(l, 0), 3: lambda: lru_conv(l, 1), 4: norm[2],
                              5: norm[3], 7: lambda: lru_gate(l), 9: lambda: lru_square(l), 11: lambda: lru_scan(l, 0),
                              12: lambda: lru_scan(l, 1), 13: lambda: lru_operand(l)})

            def lru_views():
                return [lru_w[:, i] for i in range(7)], [lru_w[:, i].rearrange("p c n -> p (c n)") for i in range(7)]

            def lru_conv(l, c):
                xc = lru_w[:, 0]
                w = conv_w[:, l, c]
                xv = lru_T[:, c, :]
                done(dve.tensor_scalar(xc[:, c, :], xv, w[:, 3:4], lru_v[:, l, 0, c:c + 1], ALU.mult, ALU.add))
                for s in (1, 2, 3):
                    ins = dve.scalar_tensor_tensor(out=xc[:, c, s:S], in0=xv[:, 0:S - s], scalar=w[:, 3 - s:4 - s],
                                                   in1=xc[:, c, s:S], op0=ALU.mult, op1=ALU.add)
                    if s < 3:
                        done(ins)
                ins.then_inc(lru_xc, 1)

            def lru_gate(l):
                (xc, th_r, *_), (xf, _, ti, _, _, _, tg) = lru_views()
                dve.wait_ge(lru_th, l + 1)
                for c in range(2):
                    ins = dve.tensor_scalar(th_r[:, c, :], th_r[:, c, :], 1.0, lru_sp[:, 2 * l + c:2 * l + c + 1], ALU.add, ALU.mult)
                ins.then_inc(lru_nla, 1)
                dve.scalar_tensor_tensor(out=ti, in0=ti, scalar=1.0, in1=xf, op0=ALU.add, op1=ALU.mult)
                done(dve.scalar_tensor_tensor(out=tg, in0=tg, scalar=1.0, in1=lru_T[:, 2:4, :].rearrange("p c n -> p (c n)"), op0=ALU.add, op1=ALU.mult))

            def lru_square(l):
                _, (_, _, _, af, tf, rf, _) = lru_views()
                dve.wait_ge(lru_at, l + 1)
                done(dve.tensor_tensor(rf, af, af, ALU.mult))
                dve.scalar_tensor_tensor(out=tf, in0=rf, scalar=1.0, in1=tf, op0=ALU.add, op1=ALU.mult).then_inc(lru_v2, 1)

            def lru_scan(l, c):
                (_, _, _, a, t, res, _), (_, _, ti, _, tf, rf, tg) = lru_views()
                if c == 0:
                    dve.wait_ge(lru_m, l + 1)
                    done(dve.scalar_tensor_tensor(out=tf, in0=tf, scalar=0.5, in1=ti, op0=ALU.mult, op1=ALU.mult))
                done(dve.tensor_tensor_scan(res[:, c, :], a[:, c, :], t[:, c, :], 0.0, ALU.mult, ALU.add))
                if c == 1:
                    dve.scalar_tensor_tensor(out=rf, in0=rf, scalar=0.5, in1=tg, op0=ALU.mult, op1=ALU.mult).then_inc(lru_y, 1)

            def lru_operand(l):
                _, (_, _, _, _, _, rf, _) = lru_views()
                dve.wait_ge(at_hi, ACT0[2 * l + 1] + 1)
                dve.wait_ge(lru_y, l + 1)
                dve.tensor_tensor(act_lo[:, 6:8, :].rearrange("p c n -> p (c n)"), rf,
                                  act_hi[:, 6:8, :].rearrange("p c n -> p (c n)").bitcast(F), ALU.subtract).then_inc(at_lo, 1)

            def layer_norm(l):
                first, last = FIRST[f"out{l}"], last_block[f"out{l}"]
                dve.wait_ge(ln_in, 64 * (l + 1))
                if l:
                    dve.tensor_tensor(ln_fs, ln_f, spread(norm_g[:, 0, 0:1], [(0, 2), (1, KD)]), ALU.mult).then_inc(ln_fs_done, 1)
                for half in range(2):
                    after_half(first, half)
                for c in split_after(last, 0):
                    split_lo(c)
                for half in range(2):
                    dve.wait_ge(acc_free[half], free_count(last))
                for tt in range(TT):
                    dve.bn_stats(bn[:, tt, 0:6], x[:, tt, 0:512])
                take(last, 0)
                dve.wait_ge(acc_free[0], free_count(last) + 1)
                statistics(0, ((0, 1),))
                normalize(l, 0)

            def statistics(t, pieces):
                for tt, c in pieces:
                    done(dve.bn_stats(bn[:, tt, 6 * c:6 * c + 6], x[:, tt, 512 * c:512 * c + 512]))
                done(dve.bn_aggr(mv[:, t, :], bn[:, t, :]))

            def normalize(l, t):
                rsqrt(mv[:, t, 1:2], 1.0, 1e-5, st[:, 1, t:t + 1])
                dve.tensor_scalar(x[:, t, :], x[:, t, :], mv[:, t, 0:1], st[:, 1, t:t + 1],
                                  ALU.subtract, ALU.mult).then_inc(ln_norm, 1)

            def normalized_lo(l):
                a = (X1, DSW_U)[l]
                last = last_block[f"out{l}"]
                take(last, 1)
                dve.wait_ge(acc_free[1], free_count(last) + 1)
                statistics(1, ((1, 1),))
                for i in range(4):
                    if i == 2:
                        normalize(l, 1)
                    t = i // 2
                    scaled = y[:, i % 2, 0:512].rearrange("p (k n) -> p k n", n=128)
                    hi = act_hi[:, 4 * (i % 2):4 * (i % 2) + 4, 128 * t:128 * t + 128]
                    lo = act_lo[:, 4 * (i % 2):4 * (i % 2) + 4, 128 * t:128 * t + 128]
                    dve.wait_ge(at_hi, ACT0[a] + i + 1)
                    done(dve.tensor_copy(hi, scaled))
                    dve.tensor_tensor(lo, scaled, hi.bitcast(F), ALU.subtract).then_inc(at_lo, 1)
                if l:
                    scale_residual(l)
                for c in split_after(last_block[f"out{l}"], 1):
                    split_lo(c)

            def scale_residual(l):
                dve.wait_ge(at_ps, TRANS0[(X1, DSW_U)[l]] + 4)
                for t in range(TT):
                    done(dve.tensor_tensor(x[:, t, :], x[:, t, :], ln_v[:, 0, :], ALU.mult))
                    dve.tensor_tensor(x[:, t, :], x[:, t, :], ln_v[:, 1, :], ALU.add).then_inc(x_new, 1)

            def rms(i):
                dve.wait_ge(ssq_done, i + 1)
                rsqrt(rms_sum[:, 0:2], 1.0 / D, 1e-6, rstd[:, 0, :])
                dve.tensor_tensor(rstd[:, 1, :], rstd[:, 0, :], rstd[:, 0, :], ALU.mult).then_inc(rstd_done, 1)

            dve.memset(st[:, :, :], 0.0)
            acts_lo(X0, KD, chunks=(0, 1))
            split_lo(0)
            acts_lo(X0, KD, chunks=(2, 3))
            for c in range(1, CHUNK0[AHEAD - 1] + 1):
                split_lo(c)
            for l in range(LAYERS):
                hybrid(l)
                acts_lo((Y0, Y1)[l], 6, chunks=(2,))
                splits(last_block[f"in{l}"], 1)
                layer_norm(l)
                normalized_lo(l)
            gemms("dsw", begin=lambda: rms(0), early=lambda: units(2, DSW_HEADS, start=True), split=False)
            units(2, DSW_HEADS)
            acts_lo(DSW_Y, 4, chunks=(1,))
            splits(last_block["dsw"], 1)
            gemms("dswo", early=lambda: acts_lo(FFN0_U, KD, 2, (0, 1)), late=lambda: acts_lo(FFN0_U, KD, 2, (2, 3)))
            rms(1)
            gemms("up0")
            gemms("down0", early=lambda: acts_lo(MOBA_U, KD, 1, (0, 1)), late=lambda: acts_lo(MOBA_U, KD, 1, (2, 3)))
            rms(2)
            gemms("moba", early=lambda: units(3, MOBA_HEADS, start=True), split=False)
            units(3, MOBA_HEADS)
            acts_lo(MOBA_Y, KD, chunks=(2, 3))
            splits(last_block["moba"], 1)
            gemms("mobao", early=lambda: acts_lo(FFN1_U, KD, 3, (0, 1)), late=lambda: acts_lo(FFN1_U, KD, 3, (2, 3)))
            rms(3)
            gemms("up1")
            gemms("down1")


def kernel(**inputs):
    import concourse.bacc as bacc
    from concourse.bass_utils import run_bass_kernel_spmd

    nc = bacc.Bacc("TRN2", target_bir_lowering=False, num_devices=1)
    arrays, dram = {}, {}
    for name, a in [(n, inputs[n]) for n in PARAMS] + list(shape_constants().items()):
        a = np.ascontiguousarray(a)
        arrays[f"in_{name}"] = a
        dram[name] = nc.dram_tensor(f"in_{name}", a.shape, mybir.dt.from_np(a.dtype), kind="ExternalInput").ap()
    out = nc.dram_tensor("out_0", (1, S, D), mybir.dt.float32, kind="ExternalOutput").ap()
    build(nc, dram, out)
    r = run_bass_kernel_spmd(nc, [arrays], core_ids=[0])
    return r.results[0]["out_0"]
```
